# Optimizing a Trainium2 kernel written in Bass

```python
import math
import jax, jax.numpy as jnp
from jax import lax
import numpy as np

D_MODEL = 1024
BATCH = 1
SEQ = 128
DEPTH = 2
DEC_BATCH = 1
DEC_SEQ = 256
PAST_LEN = 128

GRID_W = 64
N_BRANCH = 4
BRANCH_W = D_MODEL // 4
POOL_GROUPS = 4
POOL_GC = BRANCH_W // POOL_GROUPS
POOL_WINDOWS = (2, 4, 8, 16)
DA_HEADS = 4
DA_HD = BRANCH_W // DA_HEADS
DA_D = DA_HD // 2
FT_GROUPS = 4
FT_GC = BRANCH_W // FT_GROUPS
MLA_HEADS = 4
MLA_NOPE = 64
MLA_ROPE = 32
MLA_V = 64
MLA_QK = MLA_NOPE + MLA_ROPE
Q_LORA = 192
KV_LORA = 128
FFN_HIDDEN = 2816
CONV_W = 3
ROPE_BASE = 10000.0
EPS = 1e-6
Q_BLOCK = 128
GATE_COLS = N_BRANCH * D_MODEL
POOL_COLS = BRANCH_W
DA_COLS = 3 * DA_HEADS * DA_HD
FT_COLS = BRANCH_W
MLA_COLS = Q_LORA + KV_LORA + MLA_ROPE
IN_COLS = GATE_COLS + POOL_COLS + DA_COLS + FT_COLS + MLA_COLS
IN_SPLITS = [GATE_COLS, GATE_COLS + POOL_COLS, GATE_COLS + POOL_COLS + DA_COLS,
             GATE_COLS + POOL_COLS + DA_COLS + FT_COLS]

kernel_name = 'hybrid_diffusion_prefix_trunk_step'

def _rms(x, g):
    xf = x.astype(jnp.float32)
    y = xf * lax.rsqrt(jnp.mean(xf * xf, axis=-1, keepdims=True) + EPS)
    return (y * g.astype(jnp.float32)).astype(x.dtype)

def _rope_half(x, pos):
    half = x.shape[-1] // 2
    inv = ROPE_BASE ** (-jnp.arange(half, dtype=jnp.float32) / half)
    ang = pos.astype(jnp.float32)[:, None] * inv[None, :]
    cos = jnp.cos(ang)[:, None, :].astype(x.dtype)
    sin = jnp.sin(ang)[:, None, :].astype(x.dtype)
    x1, x2 = x[..., :half], x[..., half:]
    return jnp.concatenate([x1 * cos - x2 * sin, x1 * sin + x2 * cos], axis=-1)

def _rope_2d(x, pos):
    rows, cols = pos
    half = x.shape[-1] // 2
    return jnp.concatenate([_rope_half(x[..., :half], rows), _rope_half(x[..., half:], cols)], axis=-1)

def _map_query_blocks(fn, *qs):
    B, Q = qs[0].shape[:2]
    nb = Q // Q_BLOCK
    blocks = tuple(jnp.swapaxes(q.reshape((B, nb, Q_BLOCK) + q.shape[2:]), 0, 1) for q in qs)
    out = lax.map(lambda args: fn(*args), blocks)
    return jnp.swapaxes(out, 0, 1).reshape((B, Q) + out.shape[3:])

def _pool_mixer(xa, pool_w, pool_scale):
    B, T, _ = xa.shape
    xf = xa.reshape(B, T, POOL_GROUPS, POOL_GC).astype(jnp.float32)
    csum = jnp.concatenate([jnp.zeros_like(xf[:, :1]), jnp.cumsum(xf, axis=1)], axis=1)
    t = jnp.arange(T)[:, None]
    half = jnp.array(POOL_WINDOWS, dtype=jnp.int32)[None, :] // 2
    lo = jnp.clip(t - half, 0, T)
    hi = jnp.clip(t + half, 0, T)
    g = jnp.arange(POOL_GROUPS)[None, :]
    win = csum[:, hi, g, :] - csum[:, lo, g, :]
    mean = win / (hi - lo).astype(jnp.float32)[None, :, :, None]
    pooled = (mean - xf).astype(xa.dtype)
    y = jnp.einsum('btgc,gce->btge', pooled, pool_w)
    return y.reshape(B, T, BRANCH_W) * pool_scale

def _fourier(xc):
    B, T, _ = xc.shape
    xf = xc.reshape(B, T, FT_GROUPS, FT_GC).astype(jnp.float32)
    y = jnp.fft.fft2(xf, axes=(1, 3), norm='ortho').real
    return y.reshape(B, T, BRANCH_W).astype(xc.dtype)

def _diff_attention(q1, q2, k, v, lam):
    k1, k2 = k[..., :DA_D], k[..., DA_D:]
    scale = DA_D ** -0.5

    def blk(q1b, q2b):
        a1 = jax.nn.softmax((jnp.einsum('bqhd,bkhd->bhqk', q1b, k1) * scale).astype(jnp.float32), axis=-1)
        a2 = jax.nn.softmax((jnp.einsum('bqhd,bkhd->bhqk', q2b, k2) * scale).astype(jnp.float32), axis=-1)
        a = (a1 - lam * a2).astype(v.dtype)
        return jnp.einsum('bhqk,bkhd->bqhd', a, v)

    return _map_query_blocks(blk, q1, q2)

def _softmax_attention(q, k, v):
    scale = q.shape[-1] ** -0.5

    def blk(qb):
        s = jnp.einsum('bqhd,bkhd->bhqk', qb, k) * scale
        a = jax.nn.softmax(s.astype(jnp.float32), axis=-1).astype(v.dtype)
        return jnp.einsum('bhqk,bkhd->bqhd', a, v)

    return _map_query_blocks(blk, q)

def _mla_keys(ckv_n, krope, w_ukv, knorm, pos):
    B, T, _ = ckv_n.shape
    kv = (ckv_n @ w_ukv).reshape(B, T, MLA_HEADS, MLA_NOPE + MLA_V)
    k_nope, v = kv[..., :MLA_NOPE], kv[..., MLA_NOPE:]
    k_r = jnp.broadcast_to(krope[:, :, None, :], (B, T, MLA_HEADS, MLA_ROPE))
    k = _rms(jnp.concatenate([k_nope, k_r], axis=-1), knorm)
    if pos is not None:
        k = jnp.concatenate([k[..., :MLA_NOPE], _rope_2d(k[..., MLA_NOPE:], pos)], axis=-1)
    return k, v

def _conv_ffn(h, w_up, conv_w, conv_b, w_down):
    u = h @ w_up
    up = jnp.pad(u, ((0, 0), (1, 1), (0, 0)))
    u = up[:, :-2] * conv_w[0] + up[:, 1:-1] * conv_w[1] + up[:, 2:] * conv_w[2] + conv_b
    gate, val = jnp.split(u, 2, axis=-1)
    return (jax.nn.silu(gate) * val) @ w_down

def _layer(x, cond, p, lam_init, pos, ctx):
    B, T, _ = x.shape
    mod = jnp.einsum('bd,de->be', jax.nn.silu(cond), p['w_ada']) + p['b_ada']
    sh1, sc1, g1, sh2, sc2, g2 = jnp.split(mod[:, None, :], 6, axis=-1)
    h = _rms(x, p['g_norm1']) * (1 + sc1) + sh1
    u = h @ p['w_in']
    gates, xa, qkv_da, xc, mla_in = jnp.split(u, IN_SPLITS, axis=-1)

    out_a = _pool_mixer(xa, p['pool_w'], p['pool_scale'])

    qkv = qkv_da.reshape(B, T, 3, DA_HEADS, DA_HD)
    q_da, k_da, v_da = qkv[:, :, 0], qkv[:, :, 1], qkv[:, :, 2]
    q1 = _rms(q_da[..., :DA_D], p['diff_qnorm'])
    q2 = _rms(q_da[..., DA_D:], p['diff_qnorm'])
    k1 = _rms(k_da[..., :DA_D], p['diff_knorm'])
    k2 = _rms(k_da[..., DA_D:], p['diff_knorm'])
    k_cache_form = jnp.concatenate([k1, k2], axis=-1)
    if pos is not None:
        q1, q2 = _rope_2d(q1, pos), _rope_2d(q2, pos)
        k_self = jnp.concatenate([_rope_2d(k1, pos), _rope_2d(k2, pos)], axis=-1)
    else:
        k_self = k_cache_form
    if ctx is None:
        k_all, v_all = k_self, v_da
    else:
        k_all = jnp.concatenate([ctx['diff_k'], k_self], axis=1)
        v_all = jnp.concatenate([ctx['diff_v'], v_da], axis=1)
    lq = p['diff_lambda'].astype(jnp.float32)
    lam = jnp.exp(jnp.sum(lq[0] * lq[1])) - jnp.exp(jnp.sum(lq[2] * lq[3])) + lam_init
    out_b = _diff_attention(q1, q2, k_all, v_all, lam)
    out_b = (_rms(out_b, p['diff_subln']) * (1.0 - lam_init)).reshape(B, T, BRANCH_W)

    out_c = _fourier(xc)

    c_q = mla_in[..., :Q_LORA]
    c_kv = mla_in[..., Q_LORA:Q_LORA + KV_LORA]
    k_rope = mla_in[..., Q_LORA + KV_LORA:]
    q = (_rms(c_q, p['mla_qa_norm']) @ p['w_uq']).reshape(B, T, MLA_HEADS, MLA_QK)
    q = _rms(q, p['mla_qnorm'])
    if pos is not None:
        q = jnp.concatenate([q[..., :MLA_NOPE], _rope_2d(q[..., MLA_NOPE:], pos)], axis=-1)
    ckv_n = _rms(c_kv, p['mla_kv_norm'])
    k_m, v_m = _mla_keys(ckv_n, k_rope, p['w_ukv'], p['mla_knorm'], pos)
    if ctx is not None:
        k_c, v_c = _mla_keys(ctx['ckv'], ctx['krope'], p['w_ukv'], p['mla_knorm'], None)
        k_m = jnp.concatenate([k_c, k_m], axis=1)
        v_m = jnp.concatenate([v_c, v_m], axis=1)
    out_d = _softmax_attention(q, k_m, v_m).reshape(B, T, MLA_HEADS * MLA_V)

    branches = jnp.stack([out_a, out_b, out_c, out_d], axis=2)
    proj = jnp.einsum('btnw,nwd->btnd', branches, p['w_branch'])
    gsig = jax.nn.sigmoid(gates.reshape(B, T, N_BRANCH, D_MODEL).astype(jnp.float32)).astype(x.dtype)
    merged = jnp.sum(gsig * proj, axis=2)
    x = x + g1 * (merged @ p['w_out'])

    h2 = _rms(x, p['g_norm2']) * (1 + sc2) + sh2
    x = x + g2 * _conv_ffn(h2, p['w_up'], p['conv_w'], p['conv_b'], p['w_down'])
    return x, (k_cache_form, v_da, ckv_n, k_rope)

def _lambda_init(l):
    return 0.8 - 0.6 * math.exp(-0.3 * l)

def setup_inputs(seed: int = 0) -> dict:
    key = jax.random.key(seed)
    ks = jax.random.split(key, 32)
    f32 = jnp.float32

    def nrm(k, shape, scale=1.0):
        return jax.random.normal(k, shape, f32) * scale

    def gain(k, shape):
        return 1.0 + 0.05 * jax.random.normal(k, shape, f32)

    F2 = 2 * FFN_HIDDEN
    return {
        'x_prompt': nrm(ks[0], (BATCH, SEQ, D_MODEL)),
        'x_sample': nrm(ks[1], (DEC_BATCH, DEC_SEQ, D_MODEL)),
        'c': nrm(ks[2], (DEC_BATCH, D_MODEL)),
        'c_ctx': nrm(ks[3], (D_MODEL,)),
        'cache_diff_k': nrm(ks[4], (DEC_BATCH, DEPTH, PAST_LEN, DA_HEADS, DA_HD)),
        'cache_diff_v': nrm(ks[5], (DEC_BATCH, DEPTH, PAST_LEN, DA_HEADS, DA_HD)),
        'cache_mla_ckv': nrm(ks[6], (DEC_BATCH, DEPTH, PAST_LEN, KV_LORA)),
        'cache_mla_krope': nrm(ks[7], (DEC_BATCH, DEPTH, PAST_LEN, MLA_ROPE)),
        'w_ada': nrm(ks[8], (DEPTH, D_MODEL, 6 * D_MODEL), 0.5 * D_MODEL ** -0.5),
        'b_ada': nrm(ks[9], (DEPTH, 6 * D_MODEL), 0.01),
        'g_norm1': gain(ks[10], (DEPTH, D_MODEL)),
        'g_norm2': gain(ks[11], (DEPTH, D_MODEL)),
        'w_in': nrm(ks[12], (DEPTH, D_MODEL, IN_COLS), D_MODEL ** -0.5),
        'pool_w': nrm(ks[13], (DEPTH, POOL_GROUPS, POOL_GC, POOL_GC), POOL_GC ** -0.5),
        'pool_scale': gain(ks[14], (DEPTH, BRANCH_W)),
        'diff_qnorm': gain(ks[15], (DEPTH, DA_D)),
        'diff_knorm': gain(ks[16], (DEPTH, DA_D)),
        'diff_lambda': nrm(ks[17], (DEPTH, 4, DA_D), 0.1),
        'diff_subln': gain(ks[18], (DEPTH, DA_HD)),
        'mla_qa_norm': gain(ks[19], (DEPTH, Q_LORA)),
        'w_uq': nrm(ks[20], (DEPTH, Q_LORA, MLA_HEADS * MLA_QK), Q_LORA ** -0.5),
        'mla_kv_norm': gain(ks[21], (DEPTH, KV_LORA)),
        'w_ukv': nrm(ks[22], (DEPTH, KV_LORA, MLA_HEADS * (MLA_NOPE + MLA_V)), KV_LORA ** -0.5),
        'mla_qnorm': gain(ks[23], (DEPTH, MLA_QK)),
        'mla_knorm': gain(ks[24], (DEPTH, MLA_QK)),
        'w_branch': nrm(ks[25], (DEPTH, N_BRANCH, BRANCH_W, D_MODEL), BRANCH_W ** -0.5),
        'w_out': nrm(ks[26], (DEPTH, D_MODEL, D_MODEL), D_MODEL ** -0.5),
        'w_up': nrm(ks[27], (DEPTH, D_MODEL, F2), D_MODEL ** -0.5),
        'conv_w': nrm(ks[28], (DEPTH, CONV_W, F2), CONV_W ** -0.5),
        'conv_b': nrm(ks[29], (DEPTH, F2), 0.01),
        'w_down': nrm(ks[30], (DEPTH, FFN_HIDDEN, D_MODEL), FFN_HIDDEN ** -0.5),
    }

def reference(x_prompt, x_sample, c, c_ctx, cache_diff_k, cache_diff_v, cache_mla_ckv, cache_mla_krope,
              w_ada, b_ada, g_norm1, g_norm2, w_in, pool_w, pool_scale, diff_qnorm, diff_knorm,
              diff_lambda, diff_subln, mla_qa_norm, w_uq, mla_kv_norm, w_ukv, mla_qnorm, mla_knorm,
              w_branch, w_out, w_up, conv_w, conv_b, w_down):
    def params(l):
        return {
            'w_ada': w_ada[l], 'b_ada': b_ada[l], 'g_norm1': g_norm1[l], 'g_norm2': g_norm2[l],
            'w_in': w_in[l], 'pool_w': pool_w[l], 'pool_scale': pool_scale[l],
            'diff_qnorm': diff_qnorm[l], 'diff_knorm': diff_knorm[l], 'diff_lambda': diff_lambda[l],
            'diff_subln': diff_subln[l], 'mla_qa_norm': mla_qa_norm[l], 'w_uq': w_uq[l],
            'mla_kv_norm': mla_kv_norm[l], 'w_ukv': w_ukv[l], 'mla_qnorm': mla_qnorm[l],
            'mla_knorm': mla_knorm[l], 'w_branch': w_branch[l], 'w_out': w_out[l],
            'w_up': w_up[l], 'conv_w': conv_w[l], 'conv_b': conv_b[l], 'w_down': w_down[l],
        }

    y = x_prompt
    ks_, vs_, cs_, rs_ = [], [], [], []
    for l in range(DEPTH):
        y, (kc, vc, ckv, kr) = _layer(y, c_ctx[None, :], params(l), _lambda_init(l), None, None)
        ks_.append(kc)
        vs_.append(vc)
        cs_.append(ckv)
        rs_.append(kr)
    y_prompt = y
    new_diff_k = jnp.stack(ks_, axis=1)
    new_diff_v = jnp.stack(vs_, axis=1)
    new_mla_ckv = jnp.stack(cs_, axis=1)
    new_mla_krope = jnp.stack(rs_, axis=1)

    n_tok = x_sample.shape[1]
    n_rows = n_tok // GRID_W
    rows = jnp.repeat(jnp.arange(n_rows), GRID_W)
    cols = jnp.tile(jnp.arange(GRID_W), n_rows)
    pos = (rows, cols)
    z = x_sample
    for l in range(DEPTH):
        ctx = {'diff_k': cache_diff_k[:, l], 'diff_v': cache_diff_v[:, l],
               'ckv': cache_mla_ckv[:, l], 'krope': cache_mla_krope[:, l]}
        z, _ = _layer(z, c, params(l), _lambda_init(l), pos, ctx)
    y_sample = z

    return (y_prompt, y_sample, new_diff_k, new_diff_v, new_mla_ckv, new_mla_krope)


_drawn_inputs = setup_inputs


def setup_inputs(seed=0):
    import zlib

    import numpy as np

    out = dict(_drawn_inputs(seed))
    spreads = {}
    factors = {'cache_mla_ckv': 4.675,
     'cache_mla_krope': 8.0,
     'b_ada': 3.306,
     'g_norm2': 2.689,
     'pool_scale': 5.529,
     'diff_qnorm': 8.0,
     'diff_lambda': 8.0,
     'diff_subln': 6.597,
     'mla_qa_norm': 8.0,
     'mla_qnorm': 8.0,
     'mla_knorm': 8.0,
     'conv_b': 8.0}
    for name, (base, spread) in spreads.items():
        noise = np.random.default_rng([zlib.crc32(name.encode()), seed]).standard_normal(out[name].shape)
        drawn = base * np.exp(spread * noise) if base else spread * noise
        out[name] = __import__('jax').numpy.asarray(drawn.astype(out[name].dtype))
    for name, factor in factors.items():
        out[name] = (out[name] * factor).astype(out[name].dtype)
    return out
```

```python
import math
from contextlib import ExitStack

import concourse.bass as bass
from concourse import mybir

F32 = mybir.dt.float32
F32R = mybir.dt.float32r
ACT = mybir.ActivationFunctionType
ALU = mybir.AluOpType
AX = mybir.AxisListType.X

P = 128
D = 1024
KD = D // P
DEPTH = 2
CTX, LAT, PAST = 128, 256, 128
GAP = 2
L0 = CTX + GAP
TOK = CTX + GAP + LAT
GRID_W = 64
HEADS = 4
HD = 64
DAD = 32
QKW = 96
NOPE, ROPE, VW = 64, 32, 64
QL, KVL = 192, 128
FFN = 2816
FB = FFN // P
EPS = 1e-6
WINDOWS = (2, 4, 8, 16)

UNIT = KD * P
SLOTS = 4
U_MIX, U_GATE, U_BR, U_OUT, U_UP, U_DN = 13, 32, 8, 8, 2 * FB, 3 * KD
G0 = U_MIX
B0 = G0 + U_GATE
O0 = B0 + U_BR
P0 = O0 + U_OUT
D0 = P0 + U_UP
UNITS = D0 + U_DN
SLOT_USES = [len(range(s, UNITS, SLOTS)) for s in range(SLOTS)]
ADA_HEAD, ADA = 16, 48
PREP_GATES = 8
STEPS = 24

MIX = ["xa0", "xa1", "q0", "q1", "k0", "k1", "v0", "v1", "xc0", "xc1", "cq", "ckv", "cqr"]
PJ = {n: i for i, n in enumerate(n for n in MIX if n not in ("v0", "v1"))}

PCOL, _n = {}, 0
for _name, _w in (("g1", 8), ("g2", 8), ("b_ada", ADA), ("conv_w", 3 * 2 * FB), ("conv_b", 2 * FB),
                  ("pool_scale", 2), ("qn", 1), ("kn", 1), ("subln", 1), ("one_minus_init", 1),
                  ("lam_init", 1), ("lam", 4 * DAD), ("qa_a", 1), ("qa_b", 1), ("kvn", 1),
                  ("mqn", 1), ("mkn", 1), ("w_uq_a", HEADS * QKW), ("w_uq_b", HEADS * QKW),
                  ("w_ukv", HEADS * (NOPE + VW)), ("pool_w", 2 * P)):
    PCOL[_name] = (_n, _n + _w)
    _n += _w
PW = _n
CCOL = {n: (i * P, (i + 1) * P) for i, n in enumerate(("ident", "ones", "ones32", "ones64", "rot"))}
CCOL["dft"] = (5 * P, 7 * P)
CCOL["cos"] = (7 * P, 9 * P)
CCOL["sin"] = (9 * P, 11 * P)
CW = 11 * P
TP_C, TP_L = 0, 4 * CTX
TF_C = TP_L + 4 * 2 * LAT
TF_L = TF_C + 2 * CTX
TW = TF_L + 2 * 2 * LAT
HC = 2 * PAST + HEADS * HD + PAST + PAST


ACT_OWN, DVE_OWN = 19, 294


class Links:

    def __init__(self, eng, sem, per_layer):
        self.eng, self.sem, self.per, self.n = eng, sem, per_layer, 0
        self.layer, self.loop, self.step = 0, 0, 0

    def __call__(self, ins):
        self.n += 1
        return ins.then_inc(self.sem, 1)

    def wait(self):
        self.eng.wait_ge(self.sem, self.layer * self.per + self.loop * self.step + self.n)

    def begin(self, index, step):
        self.loop, self.step, self.start = index, step, self.n

    def end(self, times):
        assert self.n - self.start == self.step, (self.n - self.start)
        self.n += self.step * (times - 1)
        self.loop = self.step = 0


def program(nc, stream, ada_w, params, caches, consts, time_consts, x_in, cond,
            y_out, k_out, v_out, ckv_out, krope_out):
    ctx = ExitStack()
    with ctx:
        def tile(name, width, offset, dt=F32, parts=P):
            offset = -(-offset // 32) * 32
            return nc.alloc_sbuf_tensor_at(name, [parts, width], dt, offset=offset), offset + 4 * width

        def sem(name):
            return ctx.enter_context(nc.semaphore(name))

        def blocks(t, width=TOK):
            return t[:, :].rearrange("p (k t) -> p k t", t=width)

        o = nc.sbuf_base
        x_t, o = tile("x", KD * TOK, o)
        ahi_t, o = tile("act_hi", KD * TOK, o, F32R)
        alo_t, o = tile("act_lo", KD * TOK, o, F32R)
        raw, whi, wlo = [], [], []
        for s in range(SLOTS):
            wlo.append(tile(f"w_lo{s}", UNIT, o, F32R)[0])
            t, o = tile(f"w_raw{s}", UNIT, o)
            raw.append(t)
            t, o = tile(f"w_hi{s}", UNIT, o, F32R)
            whi.append(t)
        ada = []
        for s in range(2):
            t, o = tile(f"ada{s}", UNIT, o)
            ada.append(t)
        par, o = tile("params", PW, o)
        cn, o = tile("consts", CW, o)
        ca, o = tile("cached", HC, o)
        wide_t, o = tile("wide", KD * TOK, o)
        mod_t, o = tile("mod", ADA * 2, o)
        sc1_t, o = tile("scale1", 2 * KD, o)
        sc2_t, o = tile("scale2", 2 * KD, o)
        cond_t, o = tile("cond", 2 * KD, o)
        conds_t, o = tile("cond_silu", 2 * KD, o)
        lamp_t, o = tile("lam_prod", 2 * DAD, o)
        sm, o = tile("small", 24, o)
        top = o
        gate_a, o = tile("gates_a", PREP_GATES * TOK, top)
        tail = o
        tc, o = tile("time_consts", TW, tail)
        rs_t, o = tile("rstd", 4 * (TOK + PAST), o)
        z_t, o = tile("pool_z", 3 * 2 * P, o)
        fa_t, o = tile("fourier_a", 3 * 4 * P, o)
        prep_end = o
        gate_b, o = tile("gates_b", (U_GATE - PREP_GATES) * TOK, tail)
        o = max(o, prep_end)
        br_t, o = tile("branch", 8 * TOK, o)
        val_t, o = tile("val", 3 * HEADS * HD, o)
        vm_t, o = tile("mla_val", 4 * HEADS * VW, o)
        att = o
        pj_t, o = tile("proj", len(PJ) * TOK, att)
        qm_t, o = tile("mla_q", HEADS * TOK, o)
        km_t, o = tile("mla_k", HEADS * TOK, o)
        kmp_t, o = tile("mla_k_past", HEADS * PAST, o)
        pt_t, o = tile("probs_t", 384, o)
        rt_t, o = tile("rope_tmp", 2 * LAT, o)
        assert o <= nc.sbuf_usable_end, (o, nc.sbuf_usable_end)
        mhi_t, o = tile("merged_hi", KD * TOK, att, F32R)
        mlo_t, o = tile("merged_lo", KD * TOK, o, F32R)
        ms_t, o = tile("merge_sum", 2 * TOK, o)
        assert o <= nc.sbuf_usable_end, (o, nc.sbuf_usable_end)
        ghi_t, o = tile("mlp_hi", FB * TOK, top, F32R)
        glo_t, o = tile("mlp_lo", FB * TOK, o, F32R)
        ft_t, o = tile("mlp_tmp", 2 * 4 * TOK, o)
        assert o <= nc.sbuf_usable_end, (o, nc.sbuf_usable_end)

        x, ahi, alo, wide = blocks(x_t), blocks(ahi_t), blocks(alo_t), blocks(wide_t)
        mhi, mlo, br, pj = blocks(mhi_t), blocks(mlo_t), blocks(br_t), blocks(pj_t)
        ghi, glo = blocks(ghi_t), blocks(glo_t)
        qm, km, kmp = blocks(qm_t), blocks(km_t), blocks(kmp_t, PAST)
        val, vm = blocks(val_t, HEADS * HD), blocks(vm_t, HEADS * VW)
        mod, sc1, sc2 = blocks(mod_t, 2), blocks(sc1_t, 2), blocks(sc2_t, 2)
        gated = wide_t[:, :].rearrange("p (a n t) -> p a n t", a=2, n=4)
        msum = blocks(ms_t)
        ftmp = ft_t[:, :].rearrange("p (a n t) -> p a n t", a=2, n=4)
        gates = [blocks(gate_a)[:, g] if g < PREP_GATES else blocks(gate_b)[:, g - PREP_GATES]
                 for g in range(U_GATE)]
        rs = blocks(rs_t, TOK + PAST)
        exps = wide_t[:, 4 * TOK:4 * TOK + 4 * 384].rearrange("p (a m k) -> p a m k", a=2, m=2)
        pt = pt_t[:, :].rearrange("p (k q) -> p k q", q=P)
        rsn = rs_t[:, 0:TOK]
        zz, fa = blocks(z_t, 2 * P), blocks(fa_t, 4 * P)
        wb = [(whi[s][:, :].rearrange("p (k m) -> p k m", m=P), wlo[s][:, :].rearrange("p (k m) -> p k m", m=P))
              for s in range(SLOTS)]
        small = sm[:, :]
        EPSC, NEGLAM, GSUB = small[:, 0:1], small[:, 1:2], small[:, 2:3]

        def pc(name, a=0, b=None, p0=0, p1=P):
            lo, hi = PCOL[name]
            return par[p0:p1, lo + a:(hi if b is None else lo + b)]

        def cc(name, p0=0, p1=P, a=0, b=None):
            lo, hi = CCOL[name]
            return cn[p0:p1, lo + a:(hi if b is None else lo + b)]

        bank = [ctx.enter_context(nc.psum_tensor(f"bank{i}", [P, 512], F32)) for i in range(8)]
        RANGES = ((0, CTX, 0), (L0, TOK, 1))
        TILES = (0, L0, L0 + P)

        raw_loaded = [sem(f"raw_loaded{s}") for s in range(SLOTS)]
        ada_loaded = [sem(f"ada_loaded{s}") for s in range(2)]
        fixed_loaded, par_loaded = sem("fixed_loaded"), sem("par_loaded")
        tc_loaded, stored, y_stored = sem("tc_loaded"), sem("stored"), sem("y_stored")
        hi_ready, lo_ready, unit_done, ada_done = sem("hi_ready"), sem("lo_ready"), sem("unit_done"), sem("ada_done")
        act_own, dve_own, pool_own = sem("act_own"), sem("dve_own"), sem("pool_own")
        cond_exp, cond_ready, eps_ready, br_gap = sem("cond_exp"), sem("cond_ready"), sem("eps_ready"), sem("branch_gap")
        sq_ready, ss_done, rstd_ready, norm_full, norm_hi, norm_lo = (
            sem(n) for n in ("sq_ready", "ss_done", "rstd_ready", "norm_full", "norm_hi", "norm_lo"))
        mod_read = sem("mod_read")
        mix_out, gate_exp, gate_ready = sem("mix_out"), sem("gate_exp"), sem("gate_ready")
        lam_prod, lam_exp = sem("lam_prod_ready"), sem("lam_exp")
        psq, pss, prs = sem("prep_sq"), sem("prep_ss"), sem("prep_rstd")
        da_normed, ckv_normed, rot_done, da_roped = sem("da_normed"), sem("ckv_normed"), sem("rot_done"), sem("da_roped")
        uq_done, uq_out, uqsq, uqss, uqrs, uq_normed = (
            sem(n) for n in ("uq_done", "uq_out", "uq_sq", "uq_ss", "uq_rstd", "uq_normed"))
        uk_done, uk_out, kr_copied, uksq, ukss, ukrs, uk_normed = (
            sem(n) for n in ("uk_done", "uk_out", "kr_copied", "uk_sq", "uk_ss", "uk_rstd", "uk_normed"))
        vm_done, vm_out, mrot_done, mla_roped = sem("vm_done"), sem("vm_out"), sem("mrot_done"), sem("mla_roped")
        tm1_done, tm1_out, tm2_done, tm2_out = sem("tm1_done"), sem("tm1_out"), sem("tm2_done"), sem("tm2_out")
        scores_done, nm_ready, exp_done, probs_ready, turned, turned_out, av_done, av_out = (
            sem(n) for n in ("scores_done", "negmax_ready", "exp_done", "probs_ready", "turned", "turned_out",
                             "av_done", "av_out"))
        subsq, subss, subrs, sub_out = sem("sub_sq"), sem("sub_ss"), sem("sub_rstd"), sem("sub_out")
        br_hi, br_lo = sem("branch_hi"), sem("branch_lo")
        br_done, gated_ready, merged_ready, mrg_hi, mrg_lo = (
            sem(n) for n in ("branch_done", "gated_ready", "merged_ready", "merged_hi", "merged_lo"))
        x1_ready, x2_ready = sem("x1_ready"), sem("x2_ready")
        tap1, conv_g, conv_v, mlp_exp, mlp_full, mlp_hi, mlp_lo = (
            sem(n) for n in ("tap1", "conv_gate", "conv_val", "mlp_exp", "mlp_full", "mlp_hi", "mlp_lo"))
        block = ctx.enter_context(nc.Block())

        @block.sync
        def _(sp):
            sp.dma_start(x_t[:, :], x_in).then_inc(fixed_loaded, 16)
            sp.dma_start(cond_t[:, :], cond).then_inc(fixed_loaded, 16)
            sp.dma_start(cn[:, :], consts).then_inc(fixed_loaded, 16)
            with sp.Fori(0, DEPTH) as l:
                def load_ada(a):
                    sp.wait_ge(ada_done, l * ADA + max(a - 1, 0))
                    sp.dma_start(ada[a % 2][:, :], ada_w[bass.ds(l * ADA + a, 1), :, :].rearrange("a p n -> (a p) n")
                                 ).then_inc(ada_loaded[a % 2], 16)

                def load_unit(u, i=0):
                    sp.wait_ge(unit_done, l * UNITS + i * SLOTS + max(u - SLOTS + 1, 0))
                    sp.dma_start(raw[u % SLOTS][:, :],
                                 stream[bass.ds(l * UNITS + i * SLOTS + u, 1), :, :].rearrange("a p n -> (a p) n")
                                 ).then_inc(raw_loaded[u % SLOTS], 16)

                load_ada(0)
                load_ada(1)
                sp.wait_ge(x2_ready, l * KD)
                sp.dma_start(par[:, :], params[bass.ds(l, 1), :, :].rearrange("a p n -> (a p) n")).then_inc(par_loaded, 16)
                sp.dma_start(ca[:, :], caches[bass.ds(l, 1), :, :].rearrange("a p n -> (a p) n")).then_inc(par_loaded, 16)
                sp.wait_ge(unit_done, l * UNITS)
                sp.dma_start(tc[:, :], time_consts).then_inc(tc_loaded, 16)
                for a in range(2, ADA_HEAD + 2):
                    load_ada(a)
                    if a in (3, 5, 7, 9):
                        load_unit((a - 3) // 2)
                for u in range(SLOTS, G0 + PREP_GATES + SLOTS):
                    load_unit(u)
                for i in range(16):
                    for a in range(ADA_HEAD + 2 * i + 2, min(ADA_HEAD + 2 * i + 4, ADA)):
                        load_ada(a)
                    load_unit(G0 + PREP_GATES + SLOTS + i)
                first = G0 + PREP_GATES + SLOTS + 16
                rounds = (UNITS - first) // SLOTS
                with sp.Fori(0, rounds) as i:
                    for j in range(SLOTS):
                        load_unit(first + j, i)
                for u in range(first + rounds * SLOTS, UNITS):
                    load_unit(u)
            sp.wait_ge(x2_ready, DEPTH * KD)
            sp.dma_start(y_out, x_t[:, :]).then_inc(y_stored, 16)
            sp.wait_ge(y_stored, 16)
            sp.wait_ge(stored, 16 * 4 * DEPTH)

        @block.gpsimd
        def _(pool):
            nc.gpsimd.memset(small[:, 0:1], EPS).then_inc(eps_ready, 1)
            own = Links(pool, pool_own, KD * 2)
            with pool.Fori(0, DEPTH) as l:
                own.layer = l
                own.n = 0
                pool.wait_ge(da_normed, l * 4 + 4)
                pool.dma_start(k_out[bass.ds(l, 1), :, :].rearrange("a p n -> (a p) n").rearrange("p (b t) -> p b t", t=CTX),
                               pj[:, PJ["k0"]:PJ["k1"] + 1, 0:CTX]).then_inc(stored, 16)
                pool.dma_start(v_out[bass.ds(l, 1), :, :].rearrange("a p n -> (a p) n"), val[:, 0, :]).then_inc(stored, 16)
                pool.dma_start(krope_out[bass.ds(l, 1), :, :].rearrange("a p n -> (a p) n"),
                               pj[NOPE:QKW, PJ["cqr"], 0:CTX]).then_inc(stored, 16)
                pool.wait_ge(ckv_normed, l + 1)
                pool.dma_start(ckv_out[bass.ds(l, 1), :, :].rearrange("a p n -> (a p) n"),
                               pj[:, PJ["ckv"], 0:CTX]).then_inc(stored, 16)
                pool.wait_ge(stored, l * 64 + 64)
                for d in range(KD):
                    s = d % 2
                    pool.wait_ge(gated_ready, (l * KD + d + 1) * 4)
                    if d >= 2:
                        pool.wait_ge(mrg_lo, l * KD + d - 1)
                    own(nc.gpsimd.tensor_tensor(gated[:, s, 0, :], gated[:, s, 0, :], gated[:, s, 1, :], ALU.add))
                    own(nc.gpsimd.tensor_tensor(gated[:, s, 2, :], gated[:, s, 2, :], gated[:, s, 3, :], ALU.add))
                    own.wait()
                    nc.gpsimd.tensor_tensor(msum[:, s, :], gated[:, s, 0, :], gated[:, s, 2, :], ALU.add).then_inc(merged_ready, 1)

        @block.scalar
        def _(act):
            def A(out, in_, func, **kw):
                return nc.scalar.activation(out, in_, func, **kw)

            nc.scalar.preload_act_table_set("natural_log_exp_and_others")
            act.wait_ge(fixed_loaded, 48)
            act.wait_ge(eps_ready, 1)
            A(conds_t[:, :], cond_t[:, :], ACT.Exp, scale=-1.0).then_inc(cond_exp, 1)
            own = Links(act, act_own, ACT_OWN)
            with act.Fori(0, DEPTH) as l:
                own.layer = l
                own.n = 0

                def split(u, i=0):
                    s = u % SLOTS
                    act.wait_ge(raw_loaded[s], 16 * (l * SLOT_USES[s] + i + u // SLOTS + 1))
                    act.wait_ge(unit_done, l * UNITS + i * SLOTS + max(u - SLOTS + 1, 0))
                    A(whi[s][:, :], raw[s][:, :], ACT.Copy).then_inc(hi_ready, 1)

                def rstd(out, ss, width, exs, p1=P):
                    own(A(out, ss, ACT.Ln, scale=1.0 / width, bias=EPSC[0:p1]))
                    own.wait()
                    A(out, out, ACT.Exp, scale=-0.5).then_inc(exs, 1)

                def norm(n):
                    if n == 0:
                        act.wait_ge(x2_ready, l * KD)
                    else:
                        act.wait_ge(x1_ready, l * KD + KD)
                    for k in range(0, KD, 2):
                        A(wide[:, k:k + 2, :], x[:, k:k + 2, :], ACT.Square).then_inc(sq_ready, 1)
                    if n == 1:
                        for u in range(P0, P0 + 3):
                            split(u)
                    act.wait_ge(ss_done, l * 2 + n + 1)
                    own(A(rsn, bank[2][:, 0:TOK], ACT.Ln, scale=1.0 / D, bias=EPSC))
                    own.wait()
                    A(rsn, rsn, ACT.Exp, scale=-0.5).then_inc(rstd_ready, 1)
                    if n == 0:
                        split(0)
                        split(1)
                    for k in range(KD):
                        act.wait_ge(norm_full, (l * 2 + n) * KD + k + 1)
                        A(ahi[:, k, :], wide[:, k, :], ACT.Copy).then_inc(norm_hi, 1)

                norm(0)
                act.wait_ge(lam_prod, l + 1)
                A(small[:, 6:8], small[:, 4:6], ACT.Exp).then_inc(lam_exp, 1)
                for u in range(U_MIX):
                    split(u + 2)
                    act.wait_ge(unit_done, l * UNITS + u + 1)
                    name = MIX[u]
                    if name in PJ:
                        rows = QKW if name == "cqr" else P
                        A(pj[0:rows, PJ[name], :], bank[u % 2][0:rows, 0:TOK], ACT.Copy).then_inc(mix_out, 1)
                    else:
                        c = P * (u - MIX.index("v0"))
                        A(val[:, :, c:c + P], bank[u % 2][:, 0:3 * P].rearrange("p (t c) -> p t c", c=P),
                          ACT.Copy).then_inc(mix_out, 1)
                act.wait_ge(mix_out, (l + 1) * U_MIX)
                for i, (name, rows) in enumerate((("q0", P), ("q1", P), ("k0", P), ("k1", P), ("cq", P), ("cqr", NOPE), ("ckv", P))):
                    A(wide[0:rows, i, :], pj[0:rows, PJ[name], :], ACT.Square).then_inc(psq, 1)

                def gate(g):
                    u = G0 + g
                    act.wait_ge(unit_done, l * UNITS + u + 1)
                    A(gates[g], bank[u % 2][:, 0:TOK], ACT.Exp, scale=-1.0).then_inc(gate_exp, 1)

                for i in range(6):
                    act.wait_ge(pss, l * 6 + i + 1)
                    out = rs_t[:, i * TOK:(i + 1) * TOK] if i < 5 else z_t[:, 0:TOK]
                    rstd(out, bank[2 + i][:, 0:TOK], (DAD, DAD, DAD, DAD, QL, KVL)[i], prs)
                    if i == 2:
                        split(G0 + 2)
                gate(0)
                split(G0 + 3)
                for h in range(HEADS):
                    act.wait_ge(uq_done, l * HEADS + h + 1)
                    A(qm[0:QKW, h, :], bank[4 + h][0:QKW, 0:TOK], ACT.Copy).then_inc(uq_out, 1)
                act.wait_ge(uq_out, (l + 1) * HEADS)
                A(wide[0:QKW, 0:4, :], qm[0:QKW, :, :], ACT.Square).then_inc(uqsq, 1)
                gate(1)
                split(G0 + 4)
                for h in range(HEADS):
                    act.wait_ge(uqss, l * HEADS + h + 1)
                    rstd(rs[0:QKW, h, 0:TOK], bank[4 + h][0:QKW, 0:TOK], QKW, uqrs, QKW)
                gate(2)
                split(G0 + 5)
                act.wait_ge(uk_done, l * 5 + 1)
                A(kmp[0:NOPE, :, :], bank[2][0:NOPE, :].rearrange("p (h t) -> p h t", h=HEADS), ACT.Copy).then_inc(uk_out, 1)
                for h in range(HEADS):
                    act.wait_ge(uk_done, l * 5 + h + 2)
                    A(km[0:NOPE, h, :], bank[4 + h][0:NOPE, 0:TOK], ACT.Copy).then_inc(uk_out, 1)
                act.wait_ge(vm_done, l * 2 + 1)
                A(vm[:, 0:2, :], bank[3][:, :].rearrange("p (t c) -> p t c", t=2), ACT.Copy).then_inc(vm_out, 1)
                act.wait_ge(uk_out, (l + 1) * 5)
                act.wait_ge(kr_copied, (l + 1) * 2)
                A(wide[0:QKW, 0:4, :], km[0:QKW, :, :], ACT.Square).then_inc(uksq, 1)
                A(wide_t[0:QKW, 4 * TOK:4 * TOK + 512], kmp_t[0:QKW, :], ACT.Square).then_inc(uksq, 1)
                gate(3)
                split(G0 + 6)
                act.wait_ge(uq_normed, (l + 1) * HEADS)
                for h in range(HEADS):
                    act.wait_ge(ukss, l * 5 + h + 1)
                    rstd(rs_t[0:QKW, h * TOK:(h + 1) * TOK], bank[4 + h][0:QKW, 0:TOK], QKW, ukrs, QKW)
                act.wait_ge(ukss, l * 5 + 5)
                rstd(rs_t[0:QKW, 4 * TOK:4 * TOK + 512], bank[2][0:QKW, :], QKW, ukrs, QKW)
                act.wait_ge(vm_done, l * 2 + 2)
                A(vm[:, 2:4, :], bank[3][:, :].rearrange("p (t c) -> p t c", t=2), ACT.Copy).then_inc(vm_out, 1)
                gate(4)
                split(G0 + 7)
                gate(5)
                split(G0 + 8)
                act.wait_ge(prs, (l + 1) * 6)
                act.wait_ge(ckv_normed, l + 1)
                act.wait_ge(tm1_done, l * 5 + 1)
                A(zz[:, 0:2, :], bank[2][:, :].rearrange("p (t c) -> p t c", t=2), ACT.Copy).then_inc(tm1_out, 1)
                act.wait_ge(tm1_done, l * 5 + 2)
                A(zz[:, 2, :], bank[3][:, 0:2 * P], ACT.Copy).then_inc(tm1_out, 1)
                for t in range(3):
                    act.wait_ge(tm1_done, l * 5 + 3 + t)
                    A(fa[:, t, :], bank[4 + t][:, :], ACT.Copy).then_inc(tm1_out, 1)
                gate(6)
                split(G0 + 9)
                for b in range(2):
                    act.wait_ge(tm2_done, l * 4 + b + 1)
                    for a, e, _ in RANGES:
                        ins = A(br[:, b, a:e], bank[2 + b][:, a:e], ACT.Copy, scale=pc("pool_scale", b, b + 1))
                    ins.then_inc(tm2_out, 1)
                for b in range(2):
                    act.wait_ge(tm2_done, l * 4 + b + 3)
                    for a, e, _ in RANGES:
                        ins = A(br[:, 4 + b, a:e], bank[4 + b][:, a:e], ACT.Copy)
                    ins.then_inc(tm2_out, 1)
                gate(7)

                def turn_out(i):
                    act.wait_ge(turned, l * STEPS + i + 1)
                    act.wait_ge(av_done, l * STEPS + i)
                    n = P if (i // 4) % 3 == 0 else 3 * P
                    A(pt_t[:, 0:n], bank[4][:, 0:n], ACT.Copy).then_inc(turned_out, 1)

                for i in range(STEPS):
                    split(G0 + PREP_GATES + i + 2)
                    if i >= 1:
                        turn_out(i - 1)
                    maps = 2 if i < 12 else 1
                    n = P if (i // 4) % 3 == 0 else 3 * P
                    act.wait_ge(nm_ready, l * STEPS + i + 1)
                    c = 8 + 8 * (i % 2)
                    for m in range(maps):
                        ins = A(exps[:, i % 2, m, 0:n], bank[2 + m][:, 0:n], ACT.Exp,
                                scale=DAD ** -0.5 if i < 12 else QKW ** -0.5,
                                bias=small[:, c + 2 + m:c + 3 + m], accum_out=small[:, c + 4 + m:c + 5 + m])
                    ins.then_inc(exp_done, 1)
                    if i == 13:
                        act.wait_ge(av_out, l * 6 + 3)
                        act.wait_ge(br_gap, l + 1)
                        A(wide[:, 0:2, :], br[:, 2:4, :], ACT.Square).then_inc(subsq, 1)
                    if i in (14, 15):
                        act.wait_ge(subss, l * 2 + i - 13)
                        rstd(wide[:, 2 + i - 14, :], bank[6][:, 0:TOK], HD, subrs)
                    gate(PREP_GATES + i)
                turn_out(STEPS - 1)
                act.wait_ge(unit_done, l * UNITS + B0)
                act.wait_ge(tm2_out, (l + 1) * 4)
                act.wait_ge(sub_out, (l + 1) * 2)
                for b in (0, 1, 2, 3, 4, 5, 6, 7):
                    if b == 6:
                        act.wait_ge(av_out, (l + 1) * 6)
                    A(ahi[:, b, :], br[:, b, :], ACT.Copy).then_inc(br_hi, 1)
                for d in range(KD):
                    split(B0 + d + 2)
                    act.wait_ge(merged_ready, l * KD + d + 1)
                    A(mhi[:, d, :], msum[:, d % 2, :], ACT.Copy).then_inc(mrg_hi, 1)
                for d in range(KD - 2):
                    split(O0 + d + 2)
                norm(1)
                with act.Fori(0, FB // 2) as i:
                    own.begin(i, 0)
                    for j in range(2):
                        u = P0 + 2 * j
                        p = l * FB + i * 2 + j
                        f = ftmp[:, j]
                        split(u + 3, i)
                        act.wait_ge(unit_done, l * UNITS + i * SLOTS + u + 2)
                        act.wait_ge(mlp_lo, l * FB + i * 2 + j)
                        for m in range(2):
                            col = i * 4 + 2 * j + m
                            A(f[:, m, :], bank[2 * j + m][:, 0:TOK], ACT.Identity,
                              scale=par[:, bass.ds(PCOL["conv_w"][0] + 2 * FB + col, 1)],
                              bias=par[:, bass.ds(PCOL["conv_b"][0] + col, 1)]).then_inc(tap1, 1)
                        act.wait_ge(conv_g, p + 2)
                        A(f[:, 2, :], f[:, 0, :], ACT.Exp, scale=-1.0).then_inc(mlp_exp, 1)
                        split(u + 4, i)
                        act.wait_ge(mlp_full, p + 1)
                        A(ghi[:, bass.ds(i * 2 + j, 1), :].rearrange("p a t -> p (a t)"), f[:, 3, :],
                          ACT.Copy).then_inc(mlp_hi, 1)
                    own.end(FB // 2)
                for u in range(3, U_DN):
                    split(D0 + u)
                assert own.n == ACT_OWN, own.n

        @block.vector
        def _(dve):
            V = nc.vector
            dve.wait_ge(cond_exp, 1)
            setup = sem("setup")
            V.tensor_scalar(conds_t[:, :], conds_t[:, :], 1.0, None, ALU.add).then_inc(setup, 1)
            dve.wait_ge(setup, 1)
            V.reciprocal(conds_t[:, :], conds_t[:, :]).then_inc(setup, 1)
            dve.wait_ge(setup, 2)
            V.tensor_tensor(conds_t[:, :], conds_t[:, :], cond_t[:, :], ALU.mult).then_inc(cond_ready, 1)
            for s in (conv_g, conv_v, mlp_lo):
                V.sem_inc(s, 1)
            own = Links(dve, dve_own, DVE_OWN)
            with dve.Fori(0, DEPTH) as l:
                own.layer = l
                own.n = 0

                def split(u, i=0):
                    s = u % SLOTS
                    dve.wait_ge(hi_ready, l * UNITS + i * SLOTS + u + 1)
                    V.tensor_tensor(wlo[s][:, :], raw[s][:, :], whi[s][:, :].bitcast(F32), ALU.subtract).then_inc(lo_ready, 1)

                def low(out, full, high):
                    return V.tensor_tensor(out, full, high.bitcast(F32), ALU.subtract)

                def norm(n):
                    scale = sc1 if n == 0 else sc2
                    shift = 0 if n == 0 else 24
                    dve.wait_ge(rstd_ready, l * 2 + n + 1)
                    for k in range(KD):
                        own(V.tensor_tensor(wide[:, k, :], x[:, k, :], rsn, ALU.mult))
                    if n == 0:
                        split(0)
                        split(1)
                        dve.wait_ge(par_loaded, 32 * l + 32)
                        dve.wait_ge(ada_done, l * ADA + ADA_HEAD)
                        V.tensor_tensor(mod[:, 0:ADA_HEAD, :], bank[7][:, 0:2 * ADA_HEAD].rearrange("p (e c) -> p e c", c=2),
                                        pc("b_ada", 0, ADA_HEAD).unsqueeze(2).to_broadcast([P, ADA_HEAD, 2]), ALU.add).then_inc(mod_read, 1)
                        dve.wait_ge(mod_read, 2 * l + 1)
                        own(V.scalar_tensor_tensor(sc1, mod[:, 8:16, :], 1.0,
                                                   pc("g1").unsqueeze(2).to_broadcast([P, KD, 2]), ALU.add, ALU.mult))
                        own.wait()
                    else:
                        own.wait()
                    for k in range(KD + 1):
                        if k < KD:
                            for a, b, c in RANGES:
                                ins = V.tensor_scalar(wide[:, k, a:b], wide[:, k, a:b], scale[:, k, c:c + 1],
                                                      mod[:, shift + k, c:c + 1], ALU.mult, ALU.add)
                            ins.then_inc(norm_full, 1)
                        if k >= 1:
                            dve.wait_ge(norm_hi, (l * 2 + n) * KD + k)
                            low(alo[:, k - 1, :], wide[:, k - 1, :], ahi[:, k - 1, :]).then_inc(norm_lo, 1)

                dve.wait_ge(unit_done, l * UNITS)
                V.memset(br[:, :, CTX:L0], 0.0).then_inc(br_gap, 1)
                norm(0)
                lam = pc("lam").rearrange("p (a b d) -> p a b d", a=2, b=2)
                lp = lamp_t[:, :].rearrange("p (a d) -> p a d", a=2)
                own(V.tensor_tensor(lp, lam[:, :, 0, :], lam[:, :, 1, :], ALU.mult))
                own.wait()
                V.reduce_sum(small[:, 4:6], lp, AX).then_inc(lam_prod, 1)
                dve.wait_ge(lam_exp, l + 1)
                own(V.tensor_tensor(small[:, 1:2], small[:, 7:8], small[:, 6:7], ALU.subtract))
                own.wait()
                own(V.tensor_tensor(NEGLAM, NEGLAM, pc("lam_init"), ALU.subtract))
                own(V.tensor_tensor(GSUB, pc("subln"), pc("one_minus_init"), ALU.mult))
                for u in range(U_MIX):
                    split(u + 2)

                def gate(g):
                    dve.wait_ge(gate_exp, l * U_GATE + g + 1)
                    own(V.tensor_scalar(gates[g], gates[g], 1.0, None, ALU.add))
                    own.wait()
                    own(V.reciprocal(gates[g], gates[g]))

                for i, (name, gain) in enumerate((("q0", "qn"), ("q1", "qn"), ("k0", "kn"), ("k1", "kn"))):
                    dve.wait_ge(prs, l * 6 + i + 1)
                    r = pj[:, PJ[name], :]
                    V.scalar_tensor_tensor(r, r, pc(gain), rs_t[:, i * TOK:(i + 1) * TOK], ALU.mult, ALU.mult).then_inc(da_normed, 1)
                dve.wait_ge(prs, l * 6 + 5)
                r = pj[:, PJ["cq"], :]
                own(V.scalar_tensor_tensor(r, r, pc("qa_a"), rs_t[:, 4 * TOK:5 * TOK], ALU.mult, ALU.mult))
                r = pj[0:NOPE, PJ["cqr"], :]
                own(V.scalar_tensor_tensor(r, r, pc("qa_b", p1=NOPE), rs_t[0:NOPE, 4 * TOK:5 * TOK], ALU.mult, ALU.mult))
                dve.wait_ge(prs, l * 6 + 6)
                own.wait()
                r = pj[:, PJ["ckv"], :]
                V.scalar_tensor_tensor(r, r, pc("kvn"), z_t[:, 0:TOK], ALU.mult, ALU.mult).then_inc(ckv_normed, 1)
                split(G0 + 2)
                gate(0)
                split(G0 + 3)
                for i, (n0, n1) in enumerate((("q0", "q1"), ("k0", "k1"))):
                    dve.wait_ge(rot_done, l * 2 + i + 1)
                    dve.wait_ge(da_normed, l * 4 + 2 * i + 2)
                    dve.wait_ge(da_roped, l * 2 + i)
                    xs = pj[:, PJ[n0]:PJ[n1] + 1, L0:TOK]
                    tmp = rt_t[:, :].rearrange("p (b t) -> p b t", b=2)
                    own(V.tensor_tensor(tmp, bank[2 + i][:, :].rearrange("p (b t) -> p b t", b=2),
                                        cc("sin").unsqueeze(1).to_broadcast([P, 2, LAT]), ALU.mult))
                    own(V.tensor_tensor(xs, xs, cc("cos").unsqueeze(1).to_broadcast([P, 2, LAT]), ALU.mult))
                    own.wait()
                    V.tensor_tensor(xs, xs, tmp, ALU.add).then_inc(da_roped, 1)
                gate(1)
                split(G0 + 4)
                dve.wait_ge(mix_out, (l + 1) * U_MIX)
                src = pj[NOPE:QKW, PJ["cqr"], :].unsqueeze(1).to_broadcast([ROPE, HEADS, TOK])
                V.tensor_copy(km[NOPE:QKW, :, :], src).then_inc(kr_copied, 1)
                src = ca[NOPE:QKW, HC - PAST:HC].unsqueeze(1).to_broadcast([ROPE, HEADS, PAST])
                V.tensor_copy(kmp[NOPE:QKW, :, :], src).then_inc(kr_copied, 1)
                for h in range(HEADS):
                    dve.wait_ge(uqrs, l * HEADS + h + 1)
                    V.scalar_tensor_tensor(qm[0:QKW, h, :], qm[0:QKW, h, :], pc("mqn", p1=QKW), rs[0:QKW, h, 0:TOK],
                                           ALU.mult, ALU.mult).then_inc(uq_normed, 1)
                gate(2)
                split(G0 + 5)
                gate(3)
                split(G0 + 6)
                for h in range(HEADS):
                    dve.wait_ge(ukrs, l * 5 + h + 1)
                    V.scalar_tensor_tensor(km[0:QKW, h, :], km[0:QKW, h, :], pc("mkn", p1=QKW),
                                           rs_t[0:QKW, h * TOK:(h + 1) * TOK], ALU.mult, ALU.mult).then_inc(uk_normed, 1)
                dve.wait_ge(ukrs, l * 5 + 5)
                V.scalar_tensor_tensor(kmp_t[0:QKW, :], kmp_t[0:QKW, :], pc("mkn", p1=QKW),
                                       rs_t[0:QKW, 4 * TOK:4 * TOK + 512], ALU.mult, ALU.mult).then_inc(uk_normed, 1)
                gate(4)
                split(G0 + 7)
                for i in range(4):
                    t = qm if i < 2 else km
                    h = 2 * (i % 2)
                    dve.wait_ge(mrot_done, l * 4 + i + 1)
                    if i == 0:
                        dve.wait_ge(uq_normed, (l + 1) * HEADS)
                        dve.wait_ge(uk_normed, (l + 1) * 5)
                    xs = t[NOPE:QKW, h:h + 2, L0:TOK]
                    dve.wait_ge(mla_roped, l * 4 + i)
                    tmp = rt_t[NOPE:QKW, :].rearrange("p (b t) -> p b t", b=2)
                    own(V.tensor_tensor(tmp, bank[4 + i][NOPE:QKW, :].rearrange("p (b t) -> p b t", b=2),
                                        cc("sin", NOPE, QKW).unsqueeze(1).to_broadcast([ROPE, 2, LAT]), ALU.mult))
                    own(V.tensor_tensor(xs, xs, cc("cos", NOPE, QKW).unsqueeze(1).to_broadcast([ROPE, 2, LAT]), ALU.mult))
                    own.wait()
                    V.tensor_tensor(xs, xs, tmp, ALU.add).then_inc(mla_roped, 1)
                gate(5)
                split(G0 + 8)
                gate(6)
                split(G0 + 9)
                gate(7)

                def attention_out(i):
                    n, c0 = (2 if i < 12 else 6), TILES[(i // 4) % 3]
                    dve.wait_ge(av_done, l * STEPS + i + 1)
                    V.tensor_copy(br[:, n:n + 2, c0:c0 + P],
                                  bank[5][:, 0:2 * P].rearrange("p (b t) -> p b t", b=2)).then_inc(av_out, 1)

                for i in range(STEPS):
                    split(G0 + PREP_GATES + i + 2)
                    maps = 2 if i < 12 else 1
                    n = P if (i // 4) % 3 == 0 else 3 * P
                    scale = DAD ** -0.5 if i < 12 else QKW ** -0.5
                    c = 8 + 8 * (i % 2)
                    mx, nm, su, ri = (small[:, c + 2 * q:c + 2 * q + maps] for q in range(4))
                    dve.wait_ge(scores_done, l * STEPS + i + 1)
                    for m in range(maps):
                        own(V.reduce_max(small[:, c + m:c + m + 1], bank[2 + m][:, 0:n], AX))
                    own.wait()
                    V.tensor_scalar(nm, mx, -scale, None, ALU.mult).then_inc(nm_ready, 1)
                    dve.wait_ge(exp_done, l * STEPS + i + 1)
                    own(V.reciprocal(ri, su))
                    own.wait()
                    a0 = exps[:, i % 2, 0, 0:n]
                    if maps == 2:
                        own(V.tensor_tensor(ri[:, 1:2], ri[:, 1:2], NEGLAM, ALU.mult))
                        own(V.tensor_scalar(a0, a0, ri[:, 0:1], None, ALU.mult))
                        own.wait()
                        V.scalar_tensor_tensor(a0, exps[:, i % 2, 1, 0:n], ri[:, 1:2], a0, ALU.mult, ALU.add).then_inc(probs_ready, 1)
                    else:
                        V.tensor_scalar(a0, a0, ri[:, 0:1], None, ALU.mult).then_inc(probs_ready, 1)
                    gate(PREP_GATES + i)
                    if i == 15:
                        dve.wait_ge(av_out, l * 6 + 3)
                        for b in range(2):
                            dve.wait_ge(subrs, l * 2 + b + 1)
                            r = br[:, 2 + b, :]
                            V.scalar_tensor_tensor(r, r, GSUB, wide[:, 2 + b, :], ALU.mult, ALU.mult).then_inc(sub_out, 1)
                    if i >= 1 and (i - 1) % 4 == 3:
                        attention_out(i - 1)
                attention_out(STEPS - 1)
                dve.wait_ge(ada_done, (l + 1) * ADA)
                V.tensor_tensor(mod[:, ADA_HEAD:ADA, :], bank[7][:, 0:2 * (ADA - ADA_HEAD)].rearrange("p (e c) -> p e c", c=2),
                                pc("b_ada", ADA_HEAD, ADA).unsqueeze(2).to_broadcast([P, ADA - ADA_HEAD, 2]), ALU.add).then_inc(mod_read, 1)
                dve.wait_ge(mod_read, 2 * l + 2)
                own(V.scalar_tensor_tensor(sc2, mod[:, 32:40, :], 1.0,
                                           pc("g2").unsqueeze(2).to_broadcast([P, KD, 2]), ALU.add, ALU.mult))
                own.wait()
                for b in range(8):
                    dve.wait_ge(br_hi, l * 8 + b + 1)
                    low(alo[:, b, :], br[:, b, :], ahi[:, b, :]).then_inc(br_lo, 1)

                def merged_low(d):
                    dve.wait_ge(mrg_hi, l * KD + d + 1)
                    low(mlo[:, d, :], msum[:, d % 2, :], mhi[:, d, :]).then_inc(mrg_lo, 1)

                for d in range(KD):
                    split(B0 + d + 2)
                    for n in range(4):
                        if n < 3:
                            dve.wait_ge(br_done, (l * KD + d) * 3 + n + 1)
                        else:
                            dve.wait_ge(unit_done, l * UNITS + B0 + d + 1)
                        if d >= 2:
                            dve.wait_ge(merged_ready, l * KD + d - 1)
                        V.tensor_tensor(gated[:, d % 2, n, :], bank[n][:, 0:TOK], gates[n * KD + d], ALU.mult).then_inc(gated_ready, 1)
                    if d >= 1:
                        merged_low(d - 1)
                merged_low(KD - 1)

                def residual(d, b, gate0, done):
                    for a, e, c in RANGES:
                        ins = V.scalar_tensor_tensor(x[:, d, a:e], bank[b][:, a:e], mod[:, gate0 + d, c:c + 1], x[:, d, a:e],
                                                     ALU.mult, ALU.add)
                    ins.then_inc(done, 1)

                for d in range(KD):
                    if d < KD - 2:
                        split(O0 + d + 2)
                    dve.wait_ge(unit_done, l * UNITS + O0 + d + 1)
                    residual(d, 4 + d % 4, 16, x1_ready)
                for u in range(P0, P0 + 3):
                    split(u)
                norm(1)
                PAIR = 5
                with dve.Fori(0, FB // 2) as i:
                    own.begin(i, 2 * PAIR)
                    for j in range(2):
                        u = P0 + 2 * j
                        p = l * FB + i * 2 + j
                        f = ftmp[:, j]
                        split(u + 3, i)
                        for m in range(2):
                            dve.wait_ge(tap1, 2 * p + m + 1)
                            b = bank[2 * j + m]
                            col = i * 4 + 2 * j + m + PCOL["conv_w"][0]
                            own(V.scalar_tensor_tensor(f[:, m, 1:TOK], b[:, 0:TOK - 1], par[:, bass.ds(col, 1)],
                                                       f[:, m, 1:TOK], ALU.mult, ALU.add))
                            own.wait()
                            V.scalar_tensor_tensor(f[:, m, 0:TOK - 1], b[:, 1:TOK], par[:, bass.ds(col + 4 * FB, 1)],
                                                   f[:, m, 0:TOK - 1], ALU.mult, ALU.add).then_inc((conv_g, conv_v)[m], 1)
                        dve.wait_ge(mlp_exp, p + 1)
                        own(V.tensor_scalar(f[:, 2, :], f[:, 2, :], 1.0, None, ALU.add))
                        own.wait()
                        own(V.reciprocal(f[:, 2, :], f[:, 2, :]))
                        dve.wait_ge(conv_v, p + 2)
                        own(V.tensor_tensor(f[:, 1, :], f[:, 1, :], f[:, 0, :], ALU.mult))
                        own.wait()
                        V.tensor_tensor(f[:, 3, :], f[:, 1, :], f[:, 2, :], ALU.mult).then_inc(mlp_full, 1)
                        split(u + 4, i)
                        dve.wait_ge(mlp_hi, p + 1)
                        low(glo[:, bass.ds(i * 2 + j, 1), :].rearrange("p a t -> p (a t)"), f[:, 3, :],
                            ghi[:, bass.ds(i * 2 + j, 1), :].rearrange("p a t -> p (a t)")).then_inc(mlp_lo, 1)
                    own.end(FB // 2)
                for d in range(KD):
                    for u in range(3 * d, 3 * d + 3):
                        if u + 3 < U_DN:
                            split(D0 + u + 3)
                    dve.wait_ge(unit_done, l * UNITS + D0 + 3 * d + 3)
                    residual(d, 4 + d % 4, 40, x2_ready)
                assert own.n == DVE_OWN, own.n

        @block.tensor
        def _(pe):
            T = nc.tensor
            pe.wait_ge(fixed_loaded, 48)
            pe.wait_ge(cond_ready, 1)
            with pe.Fori(0, DEPTH) as l:
                def unit_ready(u, i=0):
                    pe.wait_ge(hi_ready, l * UNITS + i * SLOTS + u + 1)
                    pe.wait_ge(lo_ready, l * UNITS + i * SLOTS + u + 1)

                def dense(out, u, ws, hi, lo, first=True, last=True):
                    s = u % SLOTS
                    n = len(ws)
                    for k, w in enumerate(ws):
                        T.matmul(out, wb[s][0][:, w, :], hi[k], start=first and k == 0, stop=False)
                        T.matmul(out, wb[s][0][:, w, :], lo[k], start=False, stop=False)
                        ins = T.matmul(out, wb[s][1][:, w, :], hi[k], start=False, stop=last and k == n - 1)
                    return ins

                HI = [ahi[:, k, :] for k in range(KD)]
                LO = [alo[:, k, :] for k in range(KD)]

                def ada_units(a0, a1):
                    for a in range(a0, a1):
                        pe.wait_ge(ada_loaded[a % 2], 16 * (l * (ADA // 2) + a // 2 + 1))
                        w = ada[a % 2][:, :].rearrange("p (k m) -> p k m", m=P)
                        c = 2 * (a if a < ADA_HEAD else a - ADA_HEAD)
                        for k in range(KD):
                            ins = T.matmul(bank[7][:, c:c + 2], w[:, k, :], conds_t[:, 2 * k:2 * k + 2],
                                           start=k == 0, stop=k == KD - 1)
                        ins.then_inc(ada_done, 1)

                def square_sums(n):
                    for k in range(KD):
                        if k % 2 == 0:
                            pe.wait_ge(sq_ready, (l * 2 + n) * 4 + k // 2 + 1)
                        ins = T.matmul(bank[2][:, 0:TOK], cc("ones"), wide[:, k, :], start=k == 0, stop=k == KD - 1)
                    ins.then_inc(ss_done, 1)

                pe.wait_ge(x2_ready, l * KD)
                ada_units(0, 2)
                square_sums(0)
                ada_units(2, ADA_HEAD)
                for u in range(U_MIX):
                    unit_ready(u)
                    if u == 0:
                        pe.wait_ge(norm_lo, l * 2 * KD + KD)
                    if u >= 2:
                        pe.wait_ge(mix_out, l * U_MIX + u - 1)
                    name = MIX[u]
                    if name in PJ:
                        ins = dense(bank[u % 2][:, 0:TOK], u, range(KD), HI, LO)
                    else:
                        s = u % SLOTS
                        for t, c0 in enumerate(TILES):
                            out = bank[u % 2][:, t * P:(t + 1) * P]
                            for k in range(KD):
                                h, lw = ahi[:, k, c0:c0 + P], alo[:, k, c0:c0 + P]
                                T.matmul(out, h, wb[s][0][:, k, :], start=k == 0, stop=False)
                                T.matmul(out, h, wb[s][1][:, k, :], start=False, stop=False)
                                ins = T.matmul(out, lw, wb[s][0][:, k, :], start=False, stop=k == KD - 1)
                    ins.then_inc(unit_done, 1)

                def gate(g):
                    u = G0 + g
                    unit_ready(u)
                    if g < 2:
                        pe.wait_ge(mix_out, (l + 1) * U_MIX)
                    else:
                        pe.wait_ge(gate_exp, l * U_GATE + g - 1)
                    dense(bank[u % 2][:, 0:TOK], u, range(KD), HI, LO).then_inc(unit_done, 1)

                for i in range(4):
                    pe.wait_ge(psq, l * 7 + i + 1)
                    T.matmul(bank[2 + i][:, 0:TOK], cc("ones32"), wide[:, i, :], start=True, stop=True).then_inc(pss, 1)
                pe.wait_ge(psq, l * 7 + 6)
                T.matmul(bank[6][:, 0:TOK], cc("ones"), wide[:, 4, :], start=True, stop=False)
                T.matmul(bank[6][:, 0:TOK], cc("ones", 0, NOPE), wide[0:NOPE, 5, :], start=False, stop=True).then_inc(pss, 1)
                pe.wait_ge(psq, l * 7 + 7)
                pe.wait_ge(mod_read, 2 * l + 1)
                T.matmul(bank[7][:, 0:TOK], cc("ones"), wide[:, 6, :], start=True, stop=True).then_inc(pss, 1)
                gate(0)
                pe.wait_ge(prs, (l + 1) * 6)
                for i, (n0, n1) in enumerate((("q0", "q1"), ("k0", "k1"))):
                    pe.wait_ge(da_normed, l * 4 + 2 * i + 2)
                    T.matmul(bank[2 + i][:, :].rearrange("p (b t) -> p b t", b=2), cc("rot"),
                             pj[:, PJ[n0]:PJ[n1] + 1, L0:TOK], start=True, stop=True).then_inc(rot_done, 1)
                pe.wait_ge(ckv_normed, l + 1)
                for h in range(HEADS):
                    out = bank[4 + h][0:QKW, 0:TOK]
                    T.matmul(out, pc("w_uq_a", h * QKW, (h + 1) * QKW), pj[:, PJ["cq"], :], start=True, stop=False)
                    T.matmul(out, pc("w_uq_b", h * QKW, (h + 1) * QKW, 0, NOPE), pj[0:NOPE, PJ["cqr"], :],
                             start=False, stop=True).then_inc(uq_done, 1)
                gate(1)
                pe.wait_ge(uqsq, l + 1)
                for h in range(HEADS):
                    T.matmul(bank[4 + h][0:QKW, 0:TOK], cc("ones", 0, QKW, 0, QKW), wide[0:QKW, h, :],
                             start=True, stop=True).then_inc(uqss, 1)
                gate(2)
                wk = pc("w_ukv").rearrange("p (h c) -> p h c", h=HEADS)
                pe.wait_ge(da_roped, (l + 1) * 2)
                for h in range(HEADS):
                    ins = T.matmul(bank[2][0:NOPE, h * PAST:(h + 1) * PAST], wk[:, h, 0:NOPE], ca[:, 512:512 + PAST],
                                   start=True, stop=True)
                ins.then_inc(uk_done, 1)
                pe.wait_ge(uqrs, (l + 1) * HEADS)
                for h in range(HEADS):
                    T.matmul(bank[4 + h][0:NOPE, 0:TOK], wk[:, h, 0:NOPE], pj[:, PJ["ckv"], :],
                             start=True, stop=True).then_inc(uk_done, 1)

                def latent_values(t):
                    src = ca[:, 512:512 + PAST] if t == 3 else pj[:, PJ["ckv"], TILES[t]:TILES[t] + P]
                    return T.matmul(bank[3][:, (t % 2) * 256:(t % 2) * 256 + 256].rearrange("p (h c) -> p h c", h=HEADS),
                                    src, wk[:, :, NOPE:], start=True, stop=True)

                latent_values(0)
                latent_values(1).then_inc(vm_done, 1)
                gate(3)
                pe.wait_ge(uksq, (l + 1) * 2)
                pe.wait_ge(uk_out, (l + 1) * 5)
                for h in range(HEADS):
                    T.matmul(bank[4 + h][0:QKW, 0:TOK], cc("ones", 0, QKW, 0, QKW), wide[0:QKW, h, :],
                             start=True, stop=True).then_inc(ukss, 1)
                T.matmul(bank[2][0:QKW, :], cc("ones", 0, QKW, 0, QKW), wide_t[0:QKW, 4 * TOK:4 * TOK + 512],
                         start=True, stop=True).then_inc(ukss, 1)
                pe.wait_ge(vm_out, l * 2 + 1)
                latent_values(2)
                latent_values(3).then_inc(vm_done, 1)
                gate(4)
                pe.wait_ge(uk_normed, (l + 1) * 5)
                for i in range(4):
                    t, h = (qm, km)[i // 2], 2 * (i % 2)
                    T.matmul(bank[4 + i][NOPE:QKW, :].rearrange("p (b t) -> p b t", b=2), cc("rot", 0, QKW, NOPE, QKW),
                             t[0:QKW, h:h + 2, L0:TOK], start=True, stop=True).then_inc(mrot_done, 1)
                gate(5)
                pe.wait_ge(vm_out, (l + 1) * 2)
                pe.wait_ge(mla_roped, (l + 1) * 4)
                for t, c0 in enumerate(TILES):
                    for b in range(2):
                        c = (t % 2) * 2 * P + b * P
                        ins = T.matmul(bank[2 + t // 2][:, c:c + P], pj[:, PJ["xa0"] + b, c0:c0 + P],
                                       pc("pool_w", b * P, (b + 1) * P), start=True, stop=True)
                    if t >= 1:
                        ins.then_inc(tm1_done, 1)
                for t, c0 in enumerate(TILES):
                    for b in range(2):
                        ins = T.matmul(bank[4 + t][:, b * 2 * P:(b + 1) * 2 * P], pj[:, PJ["xc0"] + b, c0:c0 + P], cc("dft"),
                                       start=True, stop=True)
                    ins.then_inc(tm1_done, 1)
                gate(6)
                pe.wait_ge(tm1_out, (l + 1) * 5)
                pe.wait_ge(tc_loaded, (l + 1) * 16)
                for b in range(2):
                    for g in (2 * b, 2 * b + 1):
                        r = HD * (g % 2)
                        T.matmul(bank[2 + b][r:r + HD, 0:CTX], zz[:, 0, g * HD:(g + 1) * HD],
                                 tc[:, TP_C + g * CTX:TP_C + (g + 1) * CTX], start=True, stop=True)
                        for t in range(2):
                            c = TP_L + (g * 2 + t) * LAT
                            ins = T.matmul(bank[2 + b][r:r + HD, L0:TOK], zz[:, 1 + t, g * HD:(g + 1) * HD],
                                           tc[:, c:c + LAT], start=t == 0, stop=t == 1)
                    ins.then_inc(tm2_done, 1)
                for b in range(2):
                    for q in range(2):
                        T.matmul(bank[4 + b][:, 0:CTX], fa[:, 0, (2 * b + q) * P:(2 * b + q + 1) * P],
                                 tc[:, TF_C + q * CTX:TF_C + (q + 1) * CTX], start=q == 0, stop=q == 1)
                    for t in range(2):
                        for q in range(2):
                            c = TF_L + (q * 2 + t) * LAT
                            ins = T.matmul(bank[4 + b][:, L0:TOK], fa[:, 1 + t, (2 * b + q) * P:(2 * b + q + 1) * P],
                                           tc[:, c:c + LAT], start=t == 0 and q == 0, stop=t == 1 and q == 1)
                    ins.then_inc(tm2_done, 1)
                gate(7)

                pe.wait_ge(tm2_out, (l + 1) * 4)

                def scores(i):
                    qt, h = (i // 4) % 3, i % 4
                    q0 = TILES[qt]
                    if i >= 1:
                        pe.wait_ge(exp_done, l * STEPS + i)
                    maps = 2 if i < 12 else 1
                    for m in range(maps):
                        if i < 12:
                            p0, b = (h % 2) * HD + m * DAD, h // 2
                            q = pj[p0:p0 + DAD, PJ["q0"] + b, q0:q0 + P]
                            k_self, k_past = pj[p0:p0 + DAD, PJ["k0"] + b, :], ca[p0:p0 + DAD, b * PAST:(b + 1) * PAST]
                        else:
                            q = qm[0:QKW, h, q0:q0 + P]
                            k_self, k_past = km[0:QKW, h, :], kmp[0:QKW, h, :]
                        out = bank[2 + m]
                        if qt == 0:
                            ins = T.matmul(out[:, 0:P], q, k_self[:, 0:CTX], start=True, stop=True)
                        else:
                            T.matmul(out[:, 0:LAT], q, k_self[:, L0:TOK], start=True, stop=True)
                            ins = T.matmul(out[:, LAT:LAT + PAST], q, k_past, start=True, stop=True)
                    ins.then_inc(scores_done, 1)

                def turn(i):
                    pe.wait_ge(probs_ready, l * STEPS + i + 1)
                    pe.wait_ge(turned_out, l * STEPS + i)
                    n = 1 if (i // 4) % 3 == 0 else 3
                    for k in range(n):
                        ins = T.transpose(bank[4][:, k * P:(k + 1) * P], exps[:, i % 2, 0, k * P:(k + 1) * P], cc("ident"))
                    ins.then_inc(turned, 1)

                def weigh(i):
                    qt, h = (i // 4) % 3, i % 4
                    pe.wait_ge(turned_out, l * STEPS + i + 1)
                    if h == 0:
                        pe.wait_ge(av_out, l * 6 + i // 4)
                    out = bank[5][(h % 2) * HD:(h % 2) * HD + HD, (h // 2) * P:(h // 2) * P + P]
                    hs = slice(h * HD, (h + 1) * HD)
                    if i < 12:
                        vs = [val[:, 0, hs]] if qt == 0 else [val[:, 1, hs], val[:, 2, hs], ca[:, 256 + h * HD:256 + (h + 1) * HD]]
                    else:
                        vs = [vm[:, 0, hs]] if qt == 0 else [vm[:, 1, hs], vm[:, 2, hs], vm[:, 3, hs]]
                    for k, v in enumerate(vs):
                        ins = T.matmul(out, v, pt[:, k, :], start=k == 0, stop=k == len(vs) - 1)
                    ins.then_inc(av_done, 1)

                for i in range(STEPS):
                    if i >= 1:
                        turn(i - 1)
                    scores(i)
                    gate(PREP_GATES + i)
                    if i >= 1:
                        weigh(i - 1)
                    if i < 16:
                        if i == 0:
                            pe.wait_ge(mla_roped, (l + 1) * 4)
                        ada_units(ADA_HEAD + 2 * i, ADA_HEAD + 2 * i + 2)
                    if i in (13, 14):
                        b = i - 13
                        pe.wait_ge(subsq, l + 1)
                        if b == 1:
                            pe.wait_ge(subrs, l * 2 + 1)
                        T.matmul(bank[6][:, 0:TOK], cc("ones64"), wide[:, b, :], start=True, stop=True).then_inc(subss, 1)
                turn(STEPS - 1)
                weigh(STEPS - 1)

                with pe.Fori(0, U_BR // SLOTS) as i:
                    pe.wait_ge(gate_exp, (l + 1) * U_GATE)
                    pe.wait_ge(exp_done, (l + 1) * STEPS)
                    for j in range(SLOTS):
                        unit_ready(B0 + j, i)
                        for n in range(4):
                            pe.wait_ge(br_lo, l * 8 + 2 * n + 2)
                            if j == 0:
                                pe.wait_ge(gated_ready, l * KD * 4 + i * (13 + n))
                            else:
                                pe.wait_ge(gated_ready, (l * KD + i * SLOTS + j - 1) * 4 + n + 1)
                            ins = dense(bank[n][:, 0:TOK], B0 + j, (2 * n, 2 * n + 1), HI[2 * n:2 * n + 2], LO[2 * n:2 * n + 2])
                            ins.then_inc(br_done if n < 3 else unit_done, 1)
                MH = [mhi[:, k, :] for k in range(KD)]
                ML = [mlo[:, k, :] for k in range(KD)]
                with pe.Fori(0, U_OUT // SLOTS) as i:
                    pe.wait_ge(mrg_lo, (l + 1) * KD)
                    pe.wait_ge(av_out, (l + 1) * 6)
                    pe.wait_ge(turned_out, (l + 1) * STEPS)
                    pe.wait_ge(mod_read, 2 * l + 2)
                    for j in range(SLOTS):
                        unit_ready(O0 + j, i)
                        pe.wait_ge(x1_ready, l * KD + i * (j + 1))
                        dense(bank[4 + j][:, 0:TOK], O0 + j, range(KD), MH, ML).then_inc(unit_done, 1)
                square_sums(1)
                with pe.Fori(0, U_UP // SLOTS) as i:
                    pe.wait_ge(norm_lo, (l * 2 + 1) * KD + KD)
                    for j in range(SLOTS):
                        unit_ready(P0 + j, i)
                        pe.wait_ge((conv_g, conv_v)[j % 2], l * FB + i * 2 + j // 2)
                        dense(bank[j][:, 0:TOK], P0 + j, range(KD), HI, LO).then_inc(unit_done, 1)
                with pe.Fori(0, 2) as i:
                    pe.wait_ge(mlp_lo, (l + 1) * FB + 1)
                    pe.wait_ge(x1_ready, (l + 1) * KD)
                    for d in range(4):
                        pe.wait_ge(x2_ready, l * KD + i * (d + 1))
                        for q in range(3):
                            u = D0 + 3 * d + q
                            unit_ready(u, i * 3)
                            k0 = q * KD
                            n = min(KD, FB - k0)
                            dense(bank[4 + d][:, 0:TOK], u, range(n), [ghi[:, k0 + k, :] for k in range(n)],
                                  [glo[:, k0 + k, :] for k in range(n)], first=q == 0, last=q == 2).then_inc(unit_done, 1)


def _constants():
    import numpy as np
    f = np.float32
    cn = np.zeros((P, CW), f)

    def put(name, a):
        cn[:a.shape[0], CCOL[name][0]:CCOL[name][0] + a.shape[1]] = a

    put("ident", np.eye(P))
    put("ones", np.ones((P, P)))
    put("ones32", np.kron(np.eye(4), np.ones((32, 32))))
    put("ones64", np.kron(np.eye(2), np.ones((64, 64))))
    r = np.zeros((16, 16))
    for i in range(8):
        r[i, i + 8], r[i + 8, i] = -1, 1
    put("rot", np.kron(np.eye(8), r).T)
    j = np.arange(HD)
    ang = 2 * np.pi * np.outer(j, j) / HD
    put("dft", np.concatenate([np.kron(np.eye(2), np.cos(ang)), np.kron(np.eye(2), np.sin(ang))], 1))
    half = 8
    inv = (np.float32(10000.0) ** (-np.arange(half, dtype=f) / f(half))).astype(f)
    t = np.arange(LAT)
    for name, fn in (("cos", np.cos), ("sin", np.sin)):
        rows = fn((t // GRID_W).astype(f)[None, :] * inv[:, None])
        cols = fn((t % GRID_W).astype(f)[None, :] * inv[:, None])
        put(name, np.tile(np.concatenate([rows, rows, cols, cols]), (4, 1)))

    tc = np.zeros((P, TW), f)
    for n_tok, p0, f0 in ((CTX, TP_C, TF_C), (LAT, TP_L, TF_L)):
        tt = np.arange(n_tok)
        tiles = n_tok // P
        for g, w in enumerate(WINDOWS):
            lo, hi = np.clip(tt - w // 2, 0, n_tok), np.clip(tt + w // 2, 0, n_tok)
            m = ((tt[:, None] >= lo[None, :]) & (tt[:, None] < hi[None, :])) / (hi - lo)[None, :] - np.eye(n_tok)
            for k in range(tiles):
                c = p0 + (g * tiles + k) * n_tok
                tc[:, c:c + n_tok] = m[k * P:(k + 1) * P]
        ang = 2 * np.pi * (np.outer(tt, tt) % n_tok) / n_tok
        s = 1.0 / math.sqrt(n_tok * HD)
        for q, m in enumerate((np.cos(ang) * s, -np.sin(ang) * s)):
            for k in range(tiles):
                c = f0 + (q * tiles + k) * n_tok
                tc[:, c:c + n_tok] = m[k * P:(k + 1) * P]
    return cn, tc


def kernel(**inputs):
    import numpy as np
    import concourse.bacc as bacc
    from concourse.bass_utils import run_bass_kernel_spmd

    w = {k: np.asarray(v) for k, v in inputs.items()}
    f = np.float32

    def units(a, n):
        k = a.shape[0] // P
        return a.reshape(k, P, n, P).transpose(2, 1, 0, 3).reshape(n, P, k * P)

    stream = np.zeros((DEPTH * UNITS, P, UNIT), f)
    ada = np.zeros((DEPTH * ADA, P, UNIT), f)
    par = np.zeros((DEPTH, P, PW), f)
    cache = np.zeros((DEPTH, P, HC), f)
    for l in range(DEPTH):
        wi = w["w_in"][l]
        g, base = wi[:, :4 * D], 4 * D
        xa, qkv, xc, ml = np.split(wi[:, base:], [256, 256 + 768, 256 + 768 + 256], axis=1)
        last = np.zeros((D, P), f)
        last[:, 0:NOPE] = ml[:, P:QL]
        last[:, NOPE:QKW] = ml[:, QL + KVL:]
        mix = np.concatenate([xa, qkv, xc, ml[:, 0:P], ml[:, QL:QL + KVL], last], axis=1)
        s = stream[l * UNITS:(l + 1) * UNITS]
        s[0:G0] = units(mix, U_MIX)
        s[G0:B0] = units(g, U_GATE)
        s[B0:O0] = units(w["w_branch"][l].reshape(D, D), KD)
        s[O0:P0] = units(w["w_out"][l], KD)
        up = units(w["w_up"][l], 2 * FB)
        s[P0:D0:2], s[P0 + 1:D0:2] = up[:FB], up[FB:]
        dn = w["w_down"][l].reshape(FB, P, KD, P).transpose(2, 1, 0, 3)
        for q in range(3):
            part = dn[:, :, q * KD:(q + 1) * KD]
            s[D0 + q::3, :, 0:part.shape[2] * P] = part.reshape(KD, P, -1)
        ada[l * ADA:(l + 1) * ADA] = units(w["w_ada"][l], ADA)

        def put(name, a):
            a = np.asarray(a)
            par[l, :a.shape[0], PCOL[name][0]:PCOL[name][0] + a.shape[1]] = a

        put("g1", w["g_norm1"][l].reshape(KD, P).T)
        put("g2", w["g_norm2"][l].reshape(KD, P).T)
        put("b_ada", w["b_ada"][l].reshape(ADA, P).T)
        put("conv_w", w["conv_w"][l].reshape(3, 2, FB, P).transpose(3, 0, 2, 1).reshape(P, -1))
        put("conv_b", w["conv_b"][l].reshape(2, FB, P).transpose(2, 1, 0).reshape(P, -1))
        put("pool_scale", w["pool_scale"][l].reshape(2, P).T)
        put("qn", np.tile(w["diff_qnorm"][l], 4)[:, None])
        put("kn", np.tile(w["diff_knorm"][l], 4)[:, None])
        put("subln", np.tile(w["diff_subln"][l], 2)[:, None])
        init = 0.8 - 0.6 * math.exp(-0.3 * l)
        put("lam_init", np.full((P, 1), init, f))
        put("one_minus_init", np.full((P, 1), 1.0 - init, f))
        put("lam", np.broadcast_to(w["diff_lambda"][l].reshape(1, -1), (P, 4 * DAD)))
        put("qa_a", w["mla_qa_norm"][l][0:P, None])
        put("qa_b", w["mla_qa_norm"][l][P:, None])
        put("kvn", w["mla_kv_norm"][l][:, None])
        put("mqn", w["mla_qnorm"][l][:, None])
        put("mkn", w["mla_knorm"][l][:, None])
        put("w_uq_a", w["w_uq"][l][0:P])
        put("w_uq_b", w["w_uq"][l][P:])
        put("w_ukv", w["w_ukv"][l])
        for b in range(2):
            for q in range(2):
                c = PCOL["pool_w"][0] + b * P + q * HD
                par[l, q * HD:(q + 1) * HD, c:c + HD] = w["pool_w"][l][2 * b + q]
        cache[l, :, 0:256] = w["cache_diff_k"][0, l].reshape(PAST, 2, P).transpose(2, 1, 0).reshape(P, 256)
        cache[l, :, 256:512] = w["cache_diff_v"][0, l].reshape(PAST, 256)
        cache[l, :, 512:640] = w["cache_mla_ckv"][0, l].T
        cache[l, NOPE:QKW, 640:768] = w["cache_mla_krope"][0, l].T

    x_in = np.zeros((P, KD, TOK), f)
    x_in[:, :, 0:CTX] = w["x_prompt"][0].reshape(CTX, KD, P).transpose(2, 1, 0)
    x_in[:, :, L0:] = w["x_sample"][0].reshape(LAT, KD, P).transpose(2, 1, 0)
    cond = np.stack([w["c_ctx"].reshape(KD, P).T, w["c"][0].reshape(KD, P).T], axis=2).reshape(P, 2 * KD)
    cn, tc = _constants()
    arrays = {"stream": stream, "ada_w": ada, "params": par, "caches": cache, "consts": cn, "time_consts": tc,
              "x_in": x_in.reshape(P, KD * TOK), "cond": np.ascontiguousarray(cond)}
    outs = {"y_out": (P, KD * TOK), "k_out": (DEPTH, P, 2 * CTX), "v_out": (DEPTH, CTX, 256),
            "ckv_out": (DEPTH, KVL, CTX), "krope_out": (DEPTH, ROPE, CTX)}
    nc = bacc.Bacc("TRN2", target_bir_lowering=False, num_devices=1)
    args = {k: nc.dram_tensor(k, v.shape, F32, kind="ExternalInput").ap() for k, v in arrays.items()}
    args |= {k: nc.dram_tensor(k, v, F32, kind="ExternalOutput").ap() for k, v in outs.items()}
    program(nc, **args)
    got = run_bass_kernel_spmd(nc, [arrays], core_ids=[0]).results[0]
    y = np.asarray(got["y_out"]).reshape(P, KD, TOK)
    y_prompt = y[:, :, 0:CTX].transpose(2, 1, 0).reshape(1, CTX, D)
    y_sample = y[:, :, L0:].transpose(2, 1, 0).reshape(1, LAT, D)
    k = np.asarray(got["k_out"]).reshape(DEPTH, P, 2, CTX).transpose(0, 3, 2, 1).reshape(1, DEPTH, CTX, HEADS, HD)
    v = np.asarray(got["v_out"]).reshape(1, DEPTH, CTX, HEADS, HD)
    ckv = np.asarray(got["ckv_out"]).transpose(0, 2, 1).reshape(1, DEPTH, CTX, KVL)
    kr = np.asarray(got["krope_out"]).transpose(0, 2, 1).reshape(1, DEPTH, CTX, ROPE)
    return tuple(np.ascontiguousarray(a) for a in (y_prompt, y_sample, k, v, ckv, kr))
```

```python
import math
from contextlib import ExitStack

import concourse.bass as bass
from concourse import mybir

F32 = mybir.dt.float32
F32R = mybir.dt.float32r
ACT = mybir.ActivationFunctionType
ALU = mybir.AluOpType
AX = mybir.AxisListType.X

P = 128
D = 1024
KD = D // P
DEPTH = 2
CTX, LAT, PAST = 128, 256, 128
GAP = 2
L0 = CTX + GAP
TOK = CTX + GAP + LAT
GRID_W = 64
HEADS = 4
HD = 64
DAD = 32
QKW = 96
NOPE, ROPE, VW = 64, 32, 64
QL, KVL = 192, 128
FFN = 2816
FB = FFN // P
EPS = 1e-6
WINDOWS = (2, 4, 8, 16)

UNIT = KD * P
SLOTS = 4
U_MIX, U_GATE, U_BR, U_OUT, U_UP, U_DN = 13, 32, 8, 8, 2 * FB, 3 * KD
G0 = U_MIX
B0 = G0 + U_GATE
O0 = B0 + U_BR
P0 = O0 + U_OUT
D0 = P0 + U_UP
UNITS = D0 + U_DN
SLOT_USES = [len(range(s, UNITS, SLOTS)) for s in range(SLOTS)]
ADA_G = 16
ADA = 3 * ADA_G
ADA_OWN = 2 * ADA_G
ADA_STEP = [1, 1, 2] * 4 + [0] + [1] * 11
ADA_INIT = 12
STRIP = 32
PREP_GATES = 8
STEPS = 24

MIX = ["xa0", "xa1", "q0", "q1", "k0", "k1", "v0", "v1", "xc0", "xc1", "cq", "ckv", "cqr"]
PJ = {n: i for i, n in enumerate(n for n in MIX if n not in ("v0", "v1"))}

PCOL, _n = {}, 0
for _name, _w in (("g1", 8), ("g2", 8), ("b_ada", ADA), ("conv_w", 3 * 2 * FB), ("conv_b", 2 * FB),
                  ("pool_scale", 2), ("qn", 1), ("kn", 1), ("subln", 1), ("one_minus_init", 1),
                  ("lam_init", 1), ("lam", 4 * DAD), ("qa_a", 1), ("qa_b", 1), ("kvn", 1),
                  ("mqn", 1), ("mkn", 1), ("w_uq_a", HEADS * QKW), ("w_uq_b", HEADS * QKW),
                  ("w_ukv", HEADS * (NOPE + VW)), ("pool_w", 2 * P)):
    PCOL[_name] = (_n, _n + _w)
    _n += _w
PW = _n
CCOL = {n: (i * P, (i + 1) * P) for i, n in enumerate(("ident", "ones", "ones32", "ones64", "rot"))}
CCOL["dft"] = (5 * P, 7 * P)
CCOL["cos"] = (7 * P, 9 * P)
CCOL["sin"] = (9 * P, 11 * P)
CW = 11 * P
TP_C, TP_L = 0, 4 * CTX
TF_C = TP_L + 4 * 2 * LAT
TF_L = TF_C + 2 * CTX
TW = TF_L + 2 * 2 * LAT
HC = 2 * PAST + HEADS * HD + PAST + PAST


ACT_OWN, DVE_OWN = 19, 189


class Links:

    def __init__(self, eng, sem, per_layer):
        self.eng, self.sem, self.per, self.n = eng, sem, per_layer, 0
        self.layer, self.loop, self.step = 0, 0, 0

    def __call__(self, ins):
        self.n += 1
        return ins.then_inc(self.sem, 1)

    def wait(self):
        self.eng.wait_ge(self.sem, self.layer * self.per + self.loop * self.step + self.n)

    def begin(self, index, step):
        self.loop, self.step, self.start = index, step, self.n

    def end(self, times):
        assert self.n - self.start == self.step, (self.n - self.start)
        self.n += self.step * (times - 1)
        self.loop = self.step = 0


def program(nc, stream, ada_w, params, caches, consts, time_consts, x_in, cond,
            y_out, k_out, v_out, ckv_out, krope_out):
    ctx = ExitStack()
    with ctx:
        def tile(name, width, offset, dt=F32, parts=P):
            offset = -(-offset // 32) * 32
            return nc.alloc_sbuf_tensor_at(name, [parts, width], dt, offset=offset), offset + 4 * width

        def sem(name):
            return ctx.enter_context(nc.semaphore(name))

        def blocks(t, width=TOK):
            return t[:, :].rearrange("p (k t) -> p k t", t=width)

        o = nc.sbuf_base
        x_t, o = tile("x", KD * TOK, o)
        ahi_t, o = tile("act_hi", KD * TOK, o, F32R)
        alo_t, o = tile("act_lo", KD * TOK, o, F32R)
        raw, whi, wlo = [], [], []
        for s in range(SLOTS):
            wlo.append(tile(f"w_lo{s}", UNIT, o, F32R)[0])
            t, o = tile(f"w_raw{s}", UNIT, o)
            raw.append(t)
            t, o = tile(f"w_hi{s}", UNIT, o, F32R)
            whi.append(t)
        ada = []
        for s in range(2):
            t, o = tile(f"ada{s}", UNIT, o)
            ada.append(t)
        par, o = tile("params", PW, o)
        cn, o = tile("consts", CW, o)
        ca, o = tile("cached", HC, o)
        wide_t, o = tile("wide", KD * TOK, o)
        mod_t, o = tile("mod", (ADA - ADA_G) * 2, o)
        modh_t, o = tile("mod_head", ADA_G * 2, o)
        sc1_t, o = tile("scale1", 2 * KD, o)
        sc2_t, o = tile("scale2", 2 * KD, o)
        cond_t, o = tile("cond", 2 * KD, o)
        conds_t, o = tile("cond_silu", STRIP * KD, o)
        lamp_t, o = tile("lam_prod", 2 * DAD, o)
        sm, o = tile("small", 24, o)
        top = o
        gate_a, o = tile("gates_a", PREP_GATES * TOK, top)
        tail = o
        tc, o = tile("time_consts", TW, tail)
        rs_t, o = tile("rstd", 4 * (TOK + PAST), o)
        z_t, o = tile("pool_z", 3 * 2 * P, o)
        fa_t, o = tile("fourier_a", 3 * 4 * P, o)
        prep_end = o
        gate_b, o = tile("gates_b", (U_GATE - PREP_GATES) * TOK, tail)
        o = max(o, prep_end)
        first_at = o
        br_t, o = tile("branch", 8 * TOK, o)
        val_t, o = tile("val", 3 * HEADS * HD, o)
        vm_t, o = tile("mla_val", 4 * HEADS * VW, o)
        att = o
        pj_t, o = tile("proj", len(PJ) * TOK, att)
        qm_t, o = tile("mla_q", HEADS * TOK, o)
        km_t, o = tile("mla_k", HEADS * TOK, o)
        kmp_t, o = tile("mla_k_past", HEADS * PAST, o)
        pt_t, o = tile("probs_t", 384, o)
        rt_t, o = tile("rope_tmp", 2 * LAT, o)
        assert o <= nc.sbuf_usable_end, (o, nc.sbuf_usable_end)
        mhi_t, o = tile("merged_hi", KD * TOK, att, F32R)
        mlo_t, o = tile("merged_lo", KD * TOK, o, F32R)
        ms_t, o = tile("merge_sum", 2 * TOK, o)
        assert o <= nc.sbuf_usable_end, (o, nc.sbuf_usable_end)
        first_t, o = tile("ada_first", ADA_INIT * UNIT, first_at)
        assert o <= nc.sbuf_usable_end, (o, nc.sbuf_usable_end)
        ghi_t, o = tile("mlp_hi", FB * TOK, top, F32R)
        glo_t, o = tile("mlp_lo", FB * TOK, o, F32R)
        ft_t, o = tile("mlp_tmp", 2 * 4 * TOK, o)
        assert o <= nc.sbuf_usable_end, (o, nc.sbuf_usable_end)

        x, ahi, alo, wide = blocks(x_t), blocks(ahi_t), blocks(alo_t), blocks(wide_t)
        mhi, mlo, br, pj = blocks(mhi_t), blocks(mlo_t), blocks(br_t), blocks(pj_t)
        ghi, glo = blocks(ghi_t), blocks(glo_t)
        qm, km, kmp = blocks(qm_t), blocks(km_t), blocks(kmp_t, PAST)
        val, vm = blocks(val_t, HEADS * HD), blocks(vm_t, HEADS * VW)
        conds = blocks(conds_t, STRIP)
        condx = lamp_t[:, 0:2 * KD].rearrange("p (k c) -> p k c", c=2)
        modh, first = blocks(modh_t, 2), blocks(first_t, UNIT)
        mod, sc1, sc2 = blocks(mod_t, 2), blocks(sc1_t, 2), blocks(sc2_t, 2)
        gated = wide_t[:, :].rearrange("p (a n t) -> p a n t", a=2, n=4)
        msum = blocks(ms_t)
        ftmp = ft_t[:, :].rearrange("p (a n t) -> p a n t", a=2, n=4)
        gates = [blocks(gate_a)[:, g] if g < PREP_GATES else blocks(gate_b)[:, g - PREP_GATES]
                 for g in range(U_GATE)]
        rs = blocks(rs_t, TOK + PAST)
        exps = wide_t[:, 4 * TOK:4 * TOK + 4 * 384].rearrange("p (a m k) -> p a m k", a=2, m=2)
        pt = pt_t[:, :].rearrange("p (k q) -> p k q", q=P)
        rsn = rs_t[:, 0:TOK]
        zz, fa = blocks(z_t, 2 * P), blocks(fa_t, 4 * P)
        wb = [(whi[s][:, :].rearrange("p (k m) -> p k m", m=P), wlo[s][:, :].rearrange("p (k m) -> p k m", m=P))
              for s in range(SLOTS)]
        small = sm[:, :]
        EPSC, NEGLAM, GSUB = small[:, 0:1], small[:, 1:2], small[:, 2:3]

        def pc(name, a=0, b=None, p0=0, p1=P):
            lo, hi = PCOL[name]
            return par[p0:p1, lo + a:(hi if b is None else lo + b)]

        def cc(name, p0=0, p1=P, a=0, b=None):
            lo, hi = CCOL[name]
            return cn[p0:p1, lo + a:(hi if b is None else lo + b)]

        bank = [ctx.enter_context(nc.psum_tensor(f"bank{i}", [P, 512], F32)) for i in range(8)]
        RANGES = ((0, CTX, 0), (L0, TOK, 1))
        TILES = (0, L0, L0 + P)

        raw_loaded = [sem(f"raw_loaded{s}") for s in range(SLOTS)]
        ada_loaded = [sem(f"ada_loaded{s}") for s in range(2)]
        first_loaded = [sem(f"first_loaded{s}") for s in range(ADA_INIT // 4)]
        x_loaded = sem("x_loaded")
        fixed_loaded, par_loaded = sem("fixed_loaded"), sem("par_loaded")
        tc_loaded, stored, y_stored = sem("tc_loaded"), sem("stored"), sem("y_stored")
        hi_ready, lo_ready, unit_done, ada_done = sem("hi_ready"), sem("lo_ready"), sem("unit_done"), sem("ada_done")
        act_own, dve_own, pool_own = sem("act_own"), sem("dve_own"), sem("pool_own")
        cond_exp, cond_ready, eps_ready, br_gap = sem("cond_exp"), sem("cond_ready"), sem("eps_ready"), sem("branch_gap")
        sq_ready, ss_done, rstd_ready, norm_full, norm_hi, norm_lo = (
            sem(n) for n in ("sq_ready", "ss_done", "rstd_ready", "norm_full", "norm_hi", "norm_lo"))
        mod_read = sem("mod_read")
        mix_out, gate_ready = sem("mix_out"), sem("gate_ready")
        lam_prod, lam_exp = sem("lam_prod_ready"), sem("lam_exp")
        psq, pss, prs = sem("prep_sq"), sem("prep_ss"), sem("prep_rstd")
        da_normed, ckv_normed, rot_done, da_roped = sem("da_normed"), sem("ckv_normed"), sem("rot_done"), sem("da_roped")
        uq_done, uq_out, uqsq, uqss, uqrs, uq_normed = (
            sem(n) for n in ("uq_done", "uq_out", "uq_sq", "uq_ss", "uq_rstd", "uq_normed"))
        uk_done, uk_out, kr_copied, uksq, ukss, ukrs, uk_normed = (
            sem(n) for n in ("uk_done", "uk_out", "kr_copied", "uk_sq", "uk_ss", "uk_rstd", "uk_normed"))
        vm_done, vm_out, mrot_done, mla_roped = sem("vm_done"), sem("vm_out"), sem("mrot_done"), sem("mla_roped")
        tm1_done, tm1_out, tm2_done, tm2_out = sem("tm1_done"), sem("tm1_out"), sem("tm2_done"), sem("tm2_out")
        scores_done, nm_ready, exp_done, probs_ready, turned, turned_out, av_done, av_out = (
            sem(n) for n in ("scores_done", "negmax_ready", "exp_done", "probs_ready", "turned", "turned_out",
                             "av_done", "av_out"))
        subsq, subss, subrs, sub_out = sem("sub_sq"), sem("sub_ss"), sem("sub_rstd"), sem("sub_out")
        br_hi, br_lo = sem("branch_hi"), sem("branch_lo")
        br_done, gated_ready, merged_ready, mrg_hi, mrg_lo = (
            sem(n) for n in ("branch_done", "gated_ready", "merged_ready", "merged_hi", "merged_lo"))
        x1_ready, x2_ready = sem("x1_ready"), sem("x2_ready")
        tap1, conv_g, conv_v, mlp_tanh, mlp_full, mlp_hi, mlp_lo = (
            sem(n) for n in ("tap1", "conv_gate", "conv_val", "mlp_tanh", "mlp_full", "mlp_hi", "mlp_lo"))
        FROM = 1
        block = ctx.enter_context(nc.Block())

        @block.sync
        def _(sp):
            sp.dma_start(cond_t[:, :], cond).then_inc(fixed_loaded, 16)
            sp.dma_start(first[:, 0:4, :], ada_w[0:4, :, :].rearrange("a p n -> p a n")).then_inc(first_loaded[0], 16)
            sp.dma_start(x_t[:, :], x_in).then_inc(x_loaded, 16)
            sp.dma_start(cn[:, :], consts).then_inc(fixed_loaded, 16)
            for n in range(1, ADA_INIT // 4):
                sp.dma_start(first[:, 4 * n:4 * n + 4, :], ada_w[4 * n:4 * n + 4, :, :].rearrange("a p n -> p a n")
                             ).then_inc(first_loaded[n], 16)
            for a in range(ADA_INIT, ADA_G):
                if a >= ADA_INIT + 2:
                    sp.wait_ge(ada_done, a - 1)
                sp.dma_start(ada[a % 2][:, :], ada_w[a, :, :]).then_inc(ada_loaded[a % 2], 16)
            with sp.Fori(0, DEPTH) as l:
                def load_ada(a):
                    sp.wait_ge(ada_done, ADA_G + l * ADA + a - 1)
                    own_units = ADA - ADA_G
                    at = (l * own_units + DEPTH * ADA_G + a) if a < own_units else (l * ADA_G + ADA_G + a - own_units)
                    sp.dma_start(ada[a % 2][:, :], ada_w[bass.ds(at, 1), :, :].rearrange("a p n -> (a p) n")
                                 ).then_inc(ada_loaded[a % 2], 16)

                def load_unit(u, i=0):
                    sp.wait_ge(unit_done, FROM + l * UNITS + i * SLOTS + max(u - SLOTS + 1, 0))
                    sp.dma_start(raw[u % SLOTS][:, :],
                                 stream[bass.ds(l * UNITS + i * SLOTS + u, 1), :, :].rearrange("a p n -> (a p) n")
                                 ).then_inc(raw_loaded[u % SLOTS], 16)

                for u in range(SLOTS):
                    load_unit(u)
                sp.wait_ge(x2_ready, FROM + l * KD)
                sp.dma_start(par[:, :], params[bass.ds(l, 1), :, :].rearrange("a p n -> (a p) n")).then_inc(par_loaded, 16)
                sp.dma_start(ca[:, :], caches[bass.ds(l, 1), :, :].rearrange("a p n -> (a p) n")).then_inc(par_loaded, 16)
                sp.wait_ge(unit_done, l * UNITS)
                sp.dma_start(tc[:, :], time_consts).then_inc(tc_loaded, 16)
                load_ada(0)
                load_ada(1)
                first_step = G0 + PREP_GATES
                for u in range(SLOTS, first_step + SLOTS):
                    load_unit(u)
                used = 0
                for i in range(STEPS):
                    for a in range(used + 2, used + ADA_STEP[i] + 2):
                        load_ada(a)
                    used += ADA_STEP[i]
                    load_unit(first_step + SLOTS + i)
                for a in range(used + 2, ADA_OWN):
                    load_ada(a)
                for u in range(first_step + SLOTS + STEPS, P0 + SLOTS):
                    load_unit(u)
                with sp.If(l < DEPTH - 1):
                    for a in range(ADA_OWN, ADA_OWN + 8):
                        load_ada(a)
                with sp.Fori(0, U_UP // SLOTS) as i:
                    for j in range(SLOTS):
                        load_unit(P0 + SLOTS + j, i)
                with sp.If(l < DEPTH - 1):
                    for a in range(ADA_OWN + 8, ADA):
                        load_ada(a)
                for u in range(D0 + SLOTS, UNITS):
                    load_unit(u)
            sp.wait_ge(x2_ready, FROM + DEPTH * KD)
            sp.dma_start(y_out, x_t[:, :]).then_inc(y_stored, 16)
            sp.wait_ge(y_stored, 16)
            sp.wait_ge(stored, 16 * 4 * DEPTH)

        @block.gpsimd
        def _(pool):
            nc.gpsimd.memset(small[:, 0:1], EPS).then_inc(eps_ready, 1)
            own = Links(pool, pool_own, KD * 2)
            with pool.Fori(0, DEPTH) as l:
                own.layer = l
                own.n = 0
                pool.wait_ge(da_normed, l * 4 + 4)
                pool.dma_start(k_out[bass.ds(l, 1), :, :].rearrange("a p n -> (a p) n").rearrange("p (b t) -> p b t", t=CTX),
                               pj[:, PJ["k0"]:PJ["k1"] + 1, 0:CTX]).then_inc(stored, 16)
                pool.dma_start(v_out[bass.ds(l, 1), :, :].rearrange("a p n -> (a p) n"), val[:, 0, :]).then_inc(stored, 16)
                pool.dma_start(krope_out[bass.ds(l, 1), :, :].rearrange("a p n -> (a p) n"),
                               pj[NOPE:QKW, PJ["cqr"], 0:CTX]).then_inc(stored, 16)
                pool.wait_ge(ckv_normed, l + 1)
                pool.dma_start(ckv_out[bass.ds(l, 1), :, :].rearrange("a p n -> (a p) n"),
                               pj[:, PJ["ckv"], 0:CTX]).then_inc(stored, 16)
                pool.wait_ge(stored, l * 64 + 64)
                for d in range(KD):
                    s = d % 2
                    pool.wait_ge(gated_ready, FROM + (l * KD + d + 1) * 4)
                    if d >= 2:
                        pool.wait_ge(mrg_lo, l * KD + d - 1)
                    own(nc.gpsimd.tensor_tensor(gated[:, s, 0, :], gated[:, s, 0, :], gated[:, s, 1, :], ALU.add))
                    own(nc.gpsimd.tensor_tensor(gated[:, s, 2, :], gated[:, s, 2, :], gated[:, s, 3, :], ALU.add))
                    own.wait()
                    nc.gpsimd.tensor_tensor(msum[:, s, :], gated[:, s, 0, :], gated[:, s, 2, :], ALU.add).then_inc(merged_ready, 1)

        @block.scalar
        def _(act):
            def A(out, in_, func, **kw):
                return nc.scalar.activation(out, in_, func, **kw)

            def logs():
                nc.scalar.preload_act_table_set("natural_log_exp_and_others")

            def tanhs():
                nc.scalar.preload_act_table_set("exp_and_others")

            tanhs()
            act.wait_ge(fixed_loaded, 32)
            act.wait_ge(eps_ready, 1)
            A(condx, cond_t[:, :].rearrange("p (k c) -> p k c", c=2), ACT.Exp, scale=-1.0).then_inc(cond_exp, 1)
            own = Links(act, act_own, ACT_OWN)
            with act.Fori(0, DEPTH) as l:
                own.layer = l
                own.n = 0

                def split(u, i=0):
                    s = u % SLOTS
                    act.wait_ge(raw_loaded[s], 16 * (l * SLOT_USES[s] + i + u // SLOTS + 1))
                    act.wait_ge(unit_done, FROM + l * UNITS + i * SLOTS + max(u - SLOTS + 1, 0))
                    A(whi[s][:, :], raw[s][:, :], ACT.Copy).then_inc(hi_ready, 1)

                def rstd(out, ss, width, exs, p1=P):
                    own(A(out, ss, ACT.Ln, scale=1.0 / width, bias=EPSC[0:p1]))
                    own.wait()
                    A(out, out, ACT.Exp, scale=-0.5).then_inc(exs, 1)

                def norm(n):
                    logs()
                    if n == 0:
                        act.wait_ge(x_loaded, 16)
                        act.wait_ge(x2_ready, FROM + l * KD)
                    else:
                        act.wait_ge(x1_ready, FROM + l * KD + KD)
                    for k in range(0, KD, 2):
                        A(wide[:, k:k + 2, :], x[:, k:k + 2, :], ACT.Square).then_inc(sq_ready, 1)
                    if n == 1:
                        for u in range(P0, P0 + 3):
                            split(u)
                    act.wait_ge(ss_done, l * 2 + n + 1)
                    own(A(rsn, bank[2][:, 0:TOK], ACT.Ln, scale=1.0 / D, bias=EPSC))
                    own.wait()
                    A(rsn, rsn, ACT.Exp, scale=-0.5).then_inc(rstd_ready, 1)
                    tanhs()
                    if n == 0:
                        split(0)
                        split(1)
                    for k in range(KD):
                        act.wait_ge(norm_full, (l * 2 + n) * KD + k + 1)
                        A(ahi[:, k, :], wide[:, k, :], ACT.Copy).then_inc(norm_hi, 1)

                norm(0)
                act.wait_ge(lam_prod, l + 1)
                A(small[:, 6:8], small[:, 4:6], ACT.Exp).then_inc(lam_exp, 1)
                for u in range(U_MIX):
                    split(u + 2)
                    act.wait_ge(unit_done, FROM + l * UNITS + u + 1)
                    name = MIX[u]
                    if name in PJ:
                        rows = QKW if name == "cqr" else P
                        A(pj[0:rows, PJ[name], :], bank[u % 2][0:rows, 0:TOK], ACT.Copy).then_inc(mix_out, 1)
                    else:
                        c = P * (u - MIX.index("v0"))
                        A(val[:, :, c:c + P], bank[u % 2][:, 0:3 * P].rearrange("p (t c) -> p t c", c=P),
                          ACT.Copy).then_inc(mix_out, 1)
                act.wait_ge(mix_out, (l + 1) * U_MIX)
                for i, (name, rows) in enumerate((("q0", P), ("q1", P), ("k0", P), ("k1", P), ("cq", P), ("cqr", NOPE), ("ckv", P))):
                    A(wide[0:rows, i, :], pj[0:rows, PJ[name], :], ACT.Square).then_inc(psq, 1)

                def gate(g):
                    u = G0 + g
                    act.wait_ge(unit_done, FROM + l * UNITS + u + 1)
                    A(gates[g], bank[u % 2][:, 0:TOK], ACT.Tanh, scale=0.5).then_inc(gate_ready, 1)

                logs()
                for i in range(6):
                    act.wait_ge(pss, l * 6 + i + 1)
                    out = rs_t[:, i * TOK:(i + 1) * TOK] if i < 5 else z_t[:, 0:TOK]
                    rstd(out, bank[2 + i][:, 0:TOK], (DAD, DAD, DAD, DAD, QL, KVL)[i], prs)
                    if i == 2:
                        split(G0 + 2)
                tanhs()
                gate(0)
                split(G0 + 3)
                for h in range(HEADS):
                    act.wait_ge(uq_done, l * HEADS + h + 1)
                    A(qm[0:QKW, h, :], bank[4 + h][0:QKW, 0:TOK], ACT.Copy).then_inc(uq_out, 1)
                act.wait_ge(uq_out, (l + 1) * HEADS)
                A(wide[0:QKW, 0:4, :], qm[0:QKW, :, :], ACT.Square).then_inc(uqsq, 1)
                gate(1)
                split(G0 + 4)
                logs()
                for h in range(HEADS):
                    act.wait_ge(uqss, l * HEADS + h + 1)
                    rstd(rs[0:QKW, h, 0:TOK], bank[4 + h][0:QKW, 0:TOK], QKW, uqrs, QKW)
                tanhs()
                gate(2)
                split(G0 + 5)
                act.wait_ge(vm_done, l * 2 + 1)
                A(vm[:, 0:2, :], bank[3][:, :].rearrange("p (t c) -> p t c", t=2), ACT.Copy).then_inc(vm_out, 1)
                act.wait_ge(uk_out, (l + 1) * 5)
                act.wait_ge(kr_copied, (l + 1) * 2)
                A(wide[0:QKW, 0:4, :], km[0:QKW, :, :], ACT.Square).then_inc(uksq, 1)
                A(wide_t[0:QKW, 4 * TOK:4 * TOK + 512], kmp_t[0:QKW, :], ACT.Square).then_inc(uksq, 1)
                gate(3)
                split(G0 + 6)
                logs()
                act.wait_ge(uq_normed, (l + 1) * HEADS)
                for h in range(HEADS):
                    act.wait_ge(ukss, l * 5 + h + 1)
                    rstd(rs_t[0:QKW, h * TOK:(h + 1) * TOK], bank[4 + h][0:QKW, 0:TOK], QKW, ukrs, QKW)
                act.wait_ge(ukss, l * 5 + 5)
                rstd(rs_t[0:QKW, 4 * TOK:4 * TOK + 512], bank[2][0:QKW, :], QKW, ukrs, QKW)
                tanhs()
                act.wait_ge(vm_done, l * 2 + 2)
                A(vm[:, 2:4, :], bank[3][:, :].rearrange("p (t c) -> p t c", t=2), ACT.Copy).then_inc(vm_out, 1)
                gate(4)
                split(G0 + 7)
                gate(5)
                split(G0 + 8)
                act.wait_ge(prs, (l + 1) * 6)
                act.wait_ge(ckv_normed, l + 1)
                act.wait_ge(tm1_done, l * 5 + 1)
                A(zz[:, 0:2, :], bank[2][:, :].rearrange("p (t c) -> p t c", t=2), ACT.Copy).then_inc(tm1_out, 1)
                act.wait_ge(tm1_done, l * 5 + 2)
                A(zz[:, 2, :], bank[3][:, 0:2 * P], ACT.Copy).then_inc(tm1_out, 1)
                for t in range(3):
                    act.wait_ge(tm1_done, l * 5 + 3 + t)
                    A(fa[:, t, :], bank[4 + t][:, :], ACT.Copy).then_inc(tm1_out, 1)
                gate(6)
                split(G0 + 9)
                for b in range(2):
                    act.wait_ge(tm2_done, l * 4 + b + 1)
                    for a, e, _ in RANGES:
                        ins = A(br[:, b, a:e], bank[2 + b][:, a:e], ACT.Copy, scale=pc("pool_scale", b, b + 1))
                    ins.then_inc(tm2_out, 1)
                for b in range(2):
                    act.wait_ge(tm2_done, l * 4 + b + 3)
                    for a, e, _ in RANGES:
                        ins = A(br[:, 4 + b, a:e], bank[4 + b][:, a:e], ACT.Copy)
                    ins.then_inc(tm2_out, 1)
                gate(7)

                def turn_out(i):
                    act.wait_ge(turned, l * STEPS + i + 1)
                    act.wait_ge(av_done, FROM + l * STEPS + i)
                    n = P if (i // 4) % 3 == 0 else 3 * P
                    A(pt_t[:, 0:n], bank[4][:, 0:n], ACT.Copy).then_inc(turned_out, 1)

                for i in range(STEPS):
                    split(G0 + PREP_GATES + i + 2)
                    if i >= 1:
                        turn_out(i - 1)
                    maps = 2 if i < 12 else 1
                    n = P if (i // 4) % 3 == 0 else 3 * P
                    act.wait_ge(nm_ready, l * STEPS + i + 1)
                    c = 8 + 8 * (i % 2)
                    for m in range(maps):
                        ins = A(exps[:, i % 2, m, 0:n], bank[2 + m][:, 0:n], ACT.Exp,
                                scale=DAD ** -0.5 if i < 12 else QKW ** -0.5,
                                bias=small[:, c + 2 + m:c + 3 + m], accum_out=small[:, c + 4 + m:c + 5 + m])
                    ins.then_inc(exp_done, 1)
                    if i == 13:
                        logs()
                        for b in range(2):
                            act.wait_ge(subss, l * 2 + b + 1)
                            rstd(wide[:, 2 + b, :], bank[(6, 3)[b]][:, 0:TOK], HD, subrs)
                        tanhs()
                    gate(PREP_GATES + i)
                    if i == 12:
                        act.wait_ge(av_out, FROM + l * 6 + 3)
                        act.wait_ge(br_gap, l + 1)
                        A(wide[:, 0:2, :], br[:, 2:4, :], ACT.Square).then_inc(subsq, 1)
                turn_out(STEPS - 1)
                act.wait_ge(unit_done, FROM + l * UNITS + B0)
                act.wait_ge(tm2_out, (l + 1) * 4)
                act.wait_ge(sub_out, (l + 1) * 2)
                for b in (0, 1, 2, 3, 4, 5, 6, 7):
                    if b == 6:
                        act.wait_ge(av_out, FROM + (l + 1) * 6)
                    A(ahi[:, b, :], br[:, b, :], ACT.Copy).then_inc(br_hi, 1)
                for d in range(KD + 1):
                    if d < KD:
                        split(B0 + d + 2)
                    if d >= 1:
                        act.wait_ge(merged_ready, l * KD + d)
                        A(mhi[:, d - 1, :], msum[:, (d - 1) % 2, :], ACT.Copy, scale=0.5).then_inc(mrg_hi, 1)
                for d in range(KD - 2):
                    split(O0 + d + 2)
                norm(1)
                with act.Fori(0, FB // 2) as i:
                    own.begin(i, 0)
                    for j in range(2):
                        u = P0 + 2 * j
                        p = l * FB + i * 2 + j
                        f = ftmp[:, j]
                        split(u + 3, i)
                        act.wait_ge(unit_done, FROM + l * UNITS + i * SLOTS + u + 2)
                        act.wait_ge(mlp_lo, FROM + l * FB + i * 2 + j)
                        for m in range(2):
                            col = i * 4 + 2 * j + m
                            A(f[:, m, :], bank[2 * j + m][:, 0:TOK], ACT.Identity,
                              scale=par[:, bass.ds(PCOL["conv_w"][0] + 2 * FB + col, 1)],
                              bias=par[:, bass.ds(PCOL["conv_b"][0] + col, 1)]).then_inc(tap1, 1)
                        act.wait_ge(conv_g, FROM + p + 2)
                        A(f[:, 2, :], f[:, 0, :], ACT.Tanh, scale=0.5).then_inc(mlp_tanh, 1)
                        split(u + 4, i)
                        act.wait_ge(mlp_full, p + 1)
                        A(ghi[:, bass.ds(i * 2 + j, 1), :].rearrange("p a t -> p (a t)"), f[:, 3, :],
                          ACT.Copy).then_inc(mlp_hi, 1)
                    own.end(FB // 2)
                for u in range(3, U_DN):
                    split(D0 + u)
                assert own.n == ACT_OWN, own.n

        @block.vector
        def _(dve):
            V = nc.vector
            setup = sem("setup")
            V.memset(conds_t[:, :], 0.0).then_inc(setup, 1)
            dve.wait_ge(cond_exp, 1)
            V.tensor_scalar(condx, condx, 1.0, None, ALU.add).then_inc(setup, 1)
            dve.wait_ge(setup, 2)
            V.reciprocal(condx, condx).then_inc(setup, 1)
            dve.wait_ge(setup, 3)
            V.tensor_tensor(conds[:, :, 0:2], condx, cond_t[:, :].rearrange("p (k c) -> p k c", c=2), ALU.mult).then_inc(cond_ready, 1)
            for s in (unit_done, x1_ready, x2_ready, av_done, av_out, turned_out, mla_roped, da_roped, gated_ready):
                V.sem_inc(s, FROM)
            for s in (conv_g, conv_v, mlp_lo):
                V.sem_inc(s, FROM + 1)
            turned_mod = blocks(rt_t, STRIP)

            dve.wait_ge(ada_done, ADA_G)
            V.transpose(rt_t[:, :], bank[7][:, :]).then_inc(mod_read, 1)
            dve.wait_ge(mod_read, 1)
            V.tensor_copy(modh, turned_mod[:, :, 0:2]).then_inc(setup, 1)
            own = Links(dve, dve_own, DVE_OWN)
            with dve.Fori(0, DEPTH) as l:
                own.layer = l
                own.n = 0

                def split(u, i=0):
                    s = u % SLOTS
                    dve.wait_ge(hi_ready, l * UNITS + i * SLOTS + u + 1)
                    V.tensor_tensor(wlo[s][:, :], raw[s][:, :], whi[s][:, :].bitcast(F32), ALU.subtract).then_inc(lo_ready, 1)

                def low(out, full, high):
                    return V.tensor_tensor(out, full, high.bitcast(F32), ALU.subtract)

                def modulation(g):
                    dve.wait_ge(ada_done, ADA_G * (2 + g) + l * ADA)
                    own.wait()
                    V.transpose(rt_t[:, :], bank[7][:, :]).then_inc(mod_read, 1)
                    dve.wait_ge(mod_read, 1 + 3 * l + g + 1)
                    own(V.tensor_tensor(mod[:, g * ADA_G:(g + 1) * ADA_G, :], turned_mod[:, :, 0:2],
                                        pc("b_ada", (g + 1) * ADA_G, (g + 2) * ADA_G).unsqueeze(2).to_broadcast([P, ADA_G, 2]), ALU.add))

                def norm(n):
                    scale, shift = (sc1, modh[:, 0:8, :]) if n == 0 else (sc2, mod[:, 8:16, :])
                    dve.wait_ge(rstd_ready, l * 2 + n + 1)
                    for k in range(KD):
                        own(V.tensor_tensor(wide[:, k, :], x[:, k, :], rsn, ALU.mult))
                    if n == 0:
                        split(0)
                        split(1)
                        dve.wait_ge(par_loaded, 32 * l + 32)
                        dve.wait_ge(setup, 4 + l)
                        own(V.tensor_tensor(modh, modh, pc("b_ada", 0, ADA_G).unsqueeze(2).to_broadcast([P, ADA_G, 2]), ALU.add))
                        own.wait()
                        own(V.scalar_tensor_tensor(sc1, modh[:, 8:16, :], 1.0,
                                                   pc("g1").unsqueeze(2).to_broadcast([P, KD, 2]), ALU.add, ALU.mult))
                        own.wait()
                    else:
                        own.wait()
                    for k in range(KD + 1):
                        if k < KD:
                            for a, b, c in RANGES:
                                ins = V.tensor_scalar(wide[:, k, a:b], wide[:, k, a:b], scale[:, k, c:c + 1],
                                                      shift[:, k, c:c + 1], ALU.mult, ALU.add)
                            ins.then_inc(norm_full, 1)
                        if k >= 1:
                            dve.wait_ge(norm_hi, (l * 2 + n) * KD + k)
                            low(alo[:, k - 1, :], wide[:, k - 1, :], ahi[:, k - 1, :]).then_inc(norm_lo, 1)

                norm(0)
                V.memset(br[:, :, CTX:L0], 0.0).then_inc(br_gap, 1)
                lam = pc("lam").rearrange("p (a b d) -> p a b d", a=2, b=2)
                lp = lamp_t[:, :].rearrange("p (a d) -> p a d", a=2)
                own(V.tensor_tensor(lp, lam[:, :, 0, :], lam[:, :, 1, :], ALU.mult))
                own.wait()
                V.reduce_sum(small[:, 4:6], lp, AX).then_inc(lam_prod, 1)
                dve.wait_ge(lam_exp, l + 1)
                own(V.tensor_tensor(small[:, 1:2], small[:, 7:8], small[:, 6:7], ALU.subtract))
                own.wait()
                own(V.tensor_tensor(NEGLAM, NEGLAM, pc("lam_init"), ALU.subtract))
                own(V.tensor_tensor(GSUB, pc("subln"), pc("one_minus_init"), ALU.mult))
                for u in range(U_MIX):
                    split(u + 2)

                for i, (name, gain) in enumerate((("q0", "qn"), ("q1", "qn"), ("k0", "kn"), ("k1", "kn"))):
                    dve.wait_ge(prs, l * 6 + i + 1)
                    r = pj[:, PJ[name], :]
                    V.scalar_tensor_tensor(r, r, pc(gain), rs_t[:, i * TOK:(i + 1) * TOK], ALU.mult, ALU.mult).then_inc(da_normed, 1)
                dve.wait_ge(prs, l * 6 + 5)
                r = pj[:, PJ["cq"], :]
                own(V.scalar_tensor_tensor(r, r, pc("qa_a"), rs_t[:, 4 * TOK:5 * TOK], ALU.mult, ALU.mult))
                r = pj[0:NOPE, PJ["cqr"], :]
                own(V.scalar_tensor_tensor(r, r, pc("qa_b", p1=NOPE), rs_t[0:NOPE, 4 * TOK:5 * TOK], ALU.mult, ALU.mult))
                dve.wait_ge(prs, l * 6 + 6)
                own.wait()
                r = pj[:, PJ["ckv"], :]
                V.scalar_tensor_tensor(r, r, pc("kvn"), z_t[:, 0:TOK], ALU.mult, ALU.mult).then_inc(ckv_normed, 1)
                split(G0 + 2)
                split(G0 + 3)
                for i, (n0, n1) in enumerate((("q0", "q1"), ("k0", "k1"))):
                    dve.wait_ge(rot_done, l * 2 + i + 1)
                    dve.wait_ge(da_normed, l * 4 + 2 * i + 2)
                    dve.wait_ge(da_roped, FROM + l * 2 + i)
                    xs = pj[:, PJ[n0]:PJ[n1] + 1, L0:TOK]
                    tmp = rt_t[:, :].rearrange("p (b t) -> p b t", b=2)
                    own(V.tensor_tensor(tmp, bank[2 + i][:, :].rearrange("p (b t) -> p b t", b=2),
                                        cc("sin").unsqueeze(1).to_broadcast([P, 2, LAT]), ALU.mult))
                    own(V.tensor_tensor(xs, xs, cc("cos").unsqueeze(1).to_broadcast([P, 2, LAT]), ALU.mult))
                    own.wait()
                    V.tensor_tensor(xs, xs, tmp, ALU.add).then_inc(da_roped, 1)
                split(G0 + 4)
                dve.wait_ge(mix_out, (l + 1) * U_MIX)
                src = pj[NOPE:QKW, PJ["cqr"], :].unsqueeze(1).to_broadcast([ROPE, HEADS, TOK])
                V.tensor_copy(km[NOPE:QKW, :, :], src).then_inc(kr_copied, 1)
                src = ca[NOPE:QKW, HC - PAST:HC].unsqueeze(1).to_broadcast([ROPE, HEADS, PAST])
                V.tensor_copy(kmp[NOPE:QKW, :, :], src).then_inc(kr_copied, 1)
                for h in range(HEADS):
                    dve.wait_ge(uqrs, l * HEADS + h + 1)
                    V.scalar_tensor_tensor(qm[0:QKW, h, :], qm[0:QKW, h, :], pc("mqn", p1=QKW), rs[0:QKW, h, 0:TOK],
                                           ALU.mult, ALU.mult).then_inc(uq_normed, 1)
                split(G0 + 5)
                dve.wait_ge(uk_done, l * 5 + 1)
                V.tensor_copy(kmp[0:NOPE, :, :], bank[2][0:NOPE, :].rearrange("p (h t) -> p h t", h=HEADS)).then_inc(uk_out, 1)
                for h in range(HEADS):
                    dve.wait_ge(uk_done, l * 5 + h + 2)
                    V.tensor_copy(km[0:NOPE, h, :], bank[4 + h][0:NOPE, 0:TOK]).then_inc(uk_out, 1)
                split(G0 + 6)
                for h in range(HEADS):
                    dve.wait_ge(ukrs, l * 5 + h + 1)
                    V.scalar_tensor_tensor(km[0:QKW, h, :], km[0:QKW, h, :], pc("mkn", p1=QKW),
                                           rs_t[0:QKW, h * TOK:(h + 1) * TOK], ALU.mult, ALU.mult).then_inc(uk_normed, 1)
                dve.wait_ge(ukrs, l * 5 + 5)
                V.scalar_tensor_tensor(kmp_t[0:QKW, :], kmp_t[0:QKW, :], pc("mkn", p1=QKW),
                                       rs_t[0:QKW, 4 * TOK:4 * TOK + 512], ALU.mult, ALU.mult).then_inc(uk_normed, 1)
                split(G0 + 7)
                for i in range(4):
                    t = qm if i < 2 else km
                    h = 2 * (i % 2)
                    dve.wait_ge(mrot_done, l * 4 + i + 1)
                    if i == 0:
                        dve.wait_ge(uq_normed, (l + 1) * HEADS)
                        dve.wait_ge(uk_normed, (l + 1) * 5)
                    xs = t[NOPE:QKW, h:h + 2, L0:TOK]
                    dve.wait_ge(mla_roped, FROM + l * 4 + i)
                    tmp = rt_t[NOPE:QKW, :].rearrange("p (b t) -> p b t", b=2)
                    own(V.tensor_tensor(tmp, bank[4 + i][NOPE:QKW, :].rearrange("p (b t) -> p b t", b=2),
                                        cc("sin", NOPE, QKW).unsqueeze(1).to_broadcast([ROPE, 2, LAT]), ALU.mult))
                    own(V.tensor_tensor(xs, xs, cc("cos", NOPE, QKW).unsqueeze(1).to_broadcast([ROPE, 2, LAT]), ALU.mult))
                    own.wait()
                    V.tensor_tensor(xs, xs, tmp, ALU.add).then_inc(mla_roped, 1)
                split(G0 + 8)
                split(G0 + 9)

                def attention_out(i):
                    n, c0 = (2 if i < 12 else 6), TILES[(i // 4) % 3]
                    dve.wait_ge(av_done, FROM + l * STEPS + i + 1)
                    V.tensor_copy(br[:, n:n + 2, c0:c0 + P],
                                  bank[5][:, 0:2 * P].rearrange("p (b t) -> p b t", b=2)).then_inc(av_out, 1)

                for i in range(STEPS):
                    split(G0 + PREP_GATES + i + 2)
                    maps = 2 if i < 12 else 1
                    n = P if (i // 4) % 3 == 0 else 3 * P
                    scale = DAD ** -0.5 if i < 12 else QKW ** -0.5
                    c = 8 + 8 * (i % 2)
                    mx, nm, su, ri = (small[:, c + 2 * q:c + 2 * q + maps] for q in range(4))
                    dve.wait_ge(scores_done, l * STEPS + i + 1)
                    for m in range(maps):
                        own(V.reduce_max(small[:, c + m:c + m + 1], bank[2 + m][:, 0:n], AX))
                    own.wait()
                    V.tensor_scalar(nm, mx, -scale, None, ALU.mult).then_inc(nm_ready, 1)
                    dve.wait_ge(exp_done, l * STEPS + i + 1)
                    own(V.reciprocal(ri, su))
                    own.wait()
                    a0 = exps[:, i % 2, 0, 0:n]
                    if maps == 2:
                        own(V.tensor_tensor(ri[:, 1:2], ri[:, 1:2], NEGLAM, ALU.mult))
                        own(V.tensor_scalar(a0, a0, ri[:, 0:1], None, ALU.mult))
                        own.wait()
                        V.scalar_tensor_tensor(a0, exps[:, i % 2, 1, 0:n], ri[:, 1:2], a0, ALU.mult, ALU.add).then_inc(probs_ready, 1)
                    else:
                        V.tensor_scalar(a0, a0, ri[:, 0:1], None, ALU.mult).then_inc(probs_ready, 1)
                    if i == 15:
                        dve.wait_ge(av_out, FROM + l * 6 + 3)
                        for b in range(2):
                            dve.wait_ge(subrs, l * 2 + b + 1)
                            r = br[:, 2 + b, :]
                            V.scalar_tensor_tensor(r, r, GSUB, wide[:, 2 + b, :], ALU.mult, ALU.mult).then_inc(sub_out, 1)
                    if i >= 1 and (i - 1) % 4 == 3:
                        attention_out(i - 1)
                    if i == 12:
                        modulation(0)
                attention_out(STEPS - 1)
                modulation(1)
                own.wait()
                own(V.scalar_tensor_tensor(sc2, mod[:, 16:24, :], 1.0,
                                           pc("g2").unsqueeze(2).to_broadcast([P, KD, 2]), ALU.add, ALU.mult))
                own.wait()
                for b in range(8):
                    dve.wait_ge(br_hi, l * 8 + b + 1)
                    low(alo[:, b, :], br[:, b, :], ahi[:, b, :]).then_inc(br_lo, 1)

                def merged_low(d):
                    dve.wait_ge(mrg_hi, l * KD + d + 1)
                    V.scalar_tensor_tensor(mlo[:, d, :], msum[:, d % 2, :], 0.5, mhi[:, d, :].bitcast(F32),
                                           ALU.mult, ALU.subtract).then_inc(mrg_lo, 1)

                for d in range(KD):
                    for n in range(4):
                        if n < 3:
                            dve.wait_ge(br_done, (l * KD + d) * 3 + n + 1)
                        else:
                            dve.wait_ge(unit_done, FROM + l * UNITS + B0 + d + 1)
                        if d >= 2:
                            dve.wait_ge(merged_ready, l * KD + d - 1)
                        V.scalar_tensor_tensor(gated[:, d % 2, n, :], gates[n * KD + d], 1.0, bank[n][:, 0:TOK],
                                               ALU.add, ALU.mult).then_inc(gated_ready, 1)
                    split(B0 + d + 2)
                    if d >= 1:
                        merged_low(d - 1)
                merged_low(KD - 1)

                def residual(d, b, gate0, done):
                    for a, e, c in RANGES:
                        ins = V.scalar_tensor_tensor(x[:, d, a:e], bank[b][:, a:e], mod[:, gate0 + d, c:c + 1], x[:, d, a:e],
                                                     ALU.mult, ALU.add)
                    ins.then_inc(done, 1)

                for d in range(KD):
                    if d < KD - 2:
                        split(O0 + d + 2)
                    dve.wait_ge(unit_done, FROM + l * UNITS + O0 + d + 1)
                    residual(d, 4 + d % 4, 0, x1_ready)
                for u in range(P0, P0 + 3):
                    split(u)
                norm(1)
                PAIR = 3
                with dve.Fori(0, FB // 2) as i:
                    own.begin(i, 2 * PAIR)
                    for j in range(2):
                        u = P0 + 2 * j
                        p = l * FB + i * 2 + j
                        f = ftmp[:, j]
                        split(u + 3, i)
                        for m in range(2):
                            dve.wait_ge(tap1, 2 * p + m + 1)
                            b = bank[2 * j + m]
                            col = i * 4 + 2 * j + m + PCOL["conv_w"][0]
                            own(V.scalar_tensor_tensor(f[:, m, 1:TOK], b[:, 0:TOK - 1], par[:, bass.ds(col, 1)],
                                                       f[:, m, 1:TOK], ALU.mult, ALU.add))
                            own.wait()
                            V.scalar_tensor_tensor(f[:, m, 0:TOK - 1], b[:, 1:TOK], par[:, bass.ds(col + 4 * FB, 1)],
                                                   f[:, m, 0:TOK - 1], ALU.mult, ALU.add).then_inc((conv_g, conv_v)[m], 1)
                        dve.wait_ge(mlp_tanh, p + 1)
                        own(V.scalar_tensor_tensor(f[:, 2, :], f[:, 2, :], 1.0, f[:, 0, :], ALU.add, ALU.mult))
                        own.wait()
                        dve.wait_ge(conv_v, FROM + p + 2)
                        V.scalar_tensor_tensor(f[:, 3, :], f[:, 2, :], 0.5, f[:, 1, :], ALU.mult, ALU.mult).then_inc(mlp_full, 1)
                        split(u + 4, i)
                        dve.wait_ge(mlp_hi, p + 1)
                        low(glo[:, bass.ds(i * 2 + j, 1), :].rearrange("p a t -> p (a t)"), f[:, 3, :],
                            ghi[:, bass.ds(i * 2 + j, 1), :].rearrange("p a t -> p (a t)")).then_inc(mlp_lo, 1)
                    own.end(FB // 2)
                for d in range(KD):
                    for u in range(3 * d, 3 * d + 3):
                        if u + 3 < U_DN:
                            split(D0 + u + 3)
                    dve.wait_ge(unit_done, FROM + l * UNITS + D0 + 3 * d + 3)
                    residual(d, d % 4, 24, x2_ready)
                    if d == 1:
                        with dve.If(l < DEPTH - 1):
                            dve.wait_ge(ada_done, ADA_G + (l + 1) * ADA)
                            V.transpose(rt_t[:, :], bank[7][:, :]).then_inc(mod_read, 1)
                            dve.wait_ge(mod_read, 1 + 3 * (l + 1))
                            V.tensor_copy(modh, turned_mod[:, :, 0:2]).then_inc(setup, 1)
                assert own.n == DVE_OWN, own.n

        @block.tensor
        def _(pe):
            T = nc.tensor

            def modulate(w, a):
                k, half = a // 2, a % 2
                for q in range(2):
                    p0 = STRIP * (2 * half + q)
                    ins = T.matmul(bank[7][p0:p0 + STRIP, :], conds[:, k, :], w[:, q * 512:(q + 1) * 512],
                                   start=k == 0, stop=k == KD - 1)
                ins.then_inc(ada_done, 1)

            pe.wait_ge(fixed_loaded, 32)
            pe.wait_ge(cond_ready, 1)
            for a in range(ADA_G):
                if a < ADA_INIT:
                    if a % 4 == 0:
                        pe.wait_ge(first_loaded[a // 4], 16)
                    modulate(first[:, a, :], a)
                else:
                    pe.wait_ge(ada_loaded[a % 2], 16 * ((a - ADA_INIT) // 2 + 1))
                    modulate(ada[a % 2], a)
            with pe.Fori(0, DEPTH) as l:
                def unit_ready(u, i=0):
                    pe.wait_ge(hi_ready, l * UNITS + i * SLOTS + u + 1)
                    pe.wait_ge(lo_ready, l * UNITS + i * SLOTS + u + 1)

                def dense(out, u, ws, hi, lo, first=True, last=True):
                    s = u % SLOTS
                    n = len(ws)
                    for k, w in enumerate(ws):
                        T.matmul(out, wb[s][0][:, w, :], hi[k], start=first and k == 0, stop=False)
                        T.matmul(out, wb[s][0][:, w, :], lo[k], start=False, stop=False)
                        ins = T.matmul(out, wb[s][1][:, w, :], hi[k], start=False, stop=last and k == n - 1)
                    return ins

                HI = [ahi[:, k, :] for k in range(KD)]
                LO = [alo[:, k, :] for k in range(KD)]

                def ada_units(a0, a1):
                    used = (ADA_G - ADA_INIT) // 2
                    for a in range(a0, a1):
                        pe.wait_ge(ada_loaded[a % 2], 16 * (used + l * (ADA // 2) + a // 2 + 1))
                        modulate(ada[a % 2], a % ADA_G)

                def square_sums(n):
                    for k in range(KD):
                        if k % 2 == 0:
                            pe.wait_ge(sq_ready, (l * 2 + n) * 4 + k // 2 + 1)
                        ins = T.matmul(bank[2][:, 0:TOK], cc("ones"), wide[:, k, :], start=k == 0, stop=k == KD - 1)
                    ins.then_inc(ss_done, 1)

                square_sums(0)
                for u in range(U_MIX):
                    unit_ready(u)
                    if u == 0:
                        pe.wait_ge(norm_lo, l * 2 * KD + KD)
                    if u >= 2:
                        pe.wait_ge(mix_out, l * U_MIX + u - 1)
                    name = MIX[u]
                    if name in PJ:
                        ins = dense(bank[u % 2][:, 0:TOK], u, range(KD), HI, LO)
                    else:
                        s = u % SLOTS
                        for t, c0 in enumerate(TILES):
                            out = bank[u % 2][:, t * P:(t + 1) * P]
                            for k in range(KD):
                                h, lw = ahi[:, k, c0:c0 + P], alo[:, k, c0:c0 + P]
                                T.matmul(out, h, wb[s][0][:, k, :], start=k == 0, stop=False)
                                T.matmul(out, h, wb[s][1][:, k, :], start=False, stop=False)
                                ins = T.matmul(out, lw, wb[s][0][:, k, :], start=False, stop=k == KD - 1)
                    ins.then_inc(unit_done, 1)

                def gate(g):
                    u = G0 + g
                    unit_ready(u)
                    if g < 2:
                        pe.wait_ge(mix_out, (l + 1) * U_MIX)
                    else:
                        pe.wait_ge(gate_ready, l * U_GATE + g - 1)
                    dense(bank[u % 2][:, 0:TOK], u, range(KD), HI, LO).then_inc(unit_done, 1)

                for i in range(4):
                    pe.wait_ge(psq, l * 7 + i + 1)
                    T.matmul(bank[2 + i][:, 0:TOK], cc("ones32"), wide[:, i, :], start=True, stop=True).then_inc(pss, 1)
                pe.wait_ge(psq, l * 7 + 6)
                T.matmul(bank[6][:, 0:TOK], cc("ones"), wide[:, 4, :], start=True, stop=False)
                T.matmul(bank[6][:, 0:TOK], cc("ones", 0, NOPE), wide[0:NOPE, 5, :], start=False, stop=True).then_inc(pss, 1)
                pe.wait_ge(psq, l * 7 + 7)
                pe.wait_ge(mod_read, 1 + 3 * l)
                T.matmul(bank[7][:, 0:TOK], cc("ones"), wide[:, 6, :], start=True, stop=True).then_inc(pss, 1)
                gate(0)
                pe.wait_ge(prs, (l + 1) * 6)
                for i, (n0, n1) in enumerate((("q0", "q1"), ("k0", "k1"))):
                    pe.wait_ge(da_normed, l * 4 + 2 * i + 2)
                    T.matmul(bank[2 + i][:, :].rearrange("p (b t) -> p b t", b=2), cc("rot"),
                             pj[:, PJ[n0]:PJ[n1] + 1, L0:TOK], start=True, stop=True).then_inc(rot_done, 1)
                pe.wait_ge(ckv_normed, l + 1)
                for h in range(HEADS):
                    out = bank[4 + h][0:QKW, 0:TOK]
                    T.matmul(out, pc("w_uq_a", h * QKW, (h + 1) * QKW), pj[:, PJ["cq"], :], start=True, stop=False)
                    T.matmul(out, pc("w_uq_b", h * QKW, (h + 1) * QKW, 0, NOPE), pj[0:NOPE, PJ["cqr"], :],
                             start=False, stop=True).then_inc(uq_done, 1)
                gate(1)
                pe.wait_ge(uqsq, l + 1)
                for h in range(HEADS):
                    T.matmul(bank[4 + h][0:QKW, 0:TOK], cc("ones", 0, QKW, 0, QKW), wide[0:QKW, h, :],
                             start=True, stop=True).then_inc(uqss, 1)
                gate(2)
                wk = pc("w_ukv").rearrange("p (h c) -> p h c", h=HEADS)
                pe.wait_ge(da_roped, FROM + (l + 1) * 2)
                for h in range(HEADS):
                    ins = T.matmul(bank[2][0:NOPE, h * PAST:(h + 1) * PAST], wk[:, h, 0:NOPE], ca[:, 512:512 + PAST],
                                   start=True, stop=True)
                ins.then_inc(uk_done, 1)
                pe.wait_ge(uqrs, (l + 1) * HEADS)
                for h in range(HEADS):
                    T.matmul(bank[4 + h][0:NOPE, 0:TOK], wk[:, h, 0:NOPE], pj[:, PJ["ckv"], :],
                             start=True, stop=True).then_inc(uk_done, 1)

                def latent_values(t):
                    src = ca[:, 512:512 + PAST] if t == 3 else pj[:, PJ["ckv"], TILES[t]:TILES[t] + P]
                    return T.matmul(bank[3][:, (t % 2) * 256:(t % 2) * 256 + 256].rearrange("p (h c) -> p h c", h=HEADS),
                                    src, wk[:, :, NOPE:], start=True, stop=True)

                latent_values(0)
                latent_values(1).then_inc(vm_done, 1)
                gate(3)
                pe.wait_ge(uksq, (l + 1) * 2)
                pe.wait_ge(uk_out, (l + 1) * 5)
                for h in range(HEADS):
                    T.matmul(bank[4 + h][0:QKW, 0:TOK], cc("ones", 0, QKW, 0, QKW), wide[0:QKW, h, :],
                             start=True, stop=True).then_inc(ukss, 1)
                T.matmul(bank[2][0:QKW, :], cc("ones", 0, QKW, 0, QKW), wide_t[0:QKW, 4 * TOK:4 * TOK + 512],
                         start=True, stop=True).then_inc(ukss, 1)
                pe.wait_ge(vm_out, l * 2 + 1)
                latent_values(2)
                latent_values(3).then_inc(vm_done, 1)
                gate(4)
                pe.wait_ge(uk_normed, (l + 1) * 5)
                for i in range(4):
                    t, h = (qm, km)[i // 2], 2 * (i % 2)
                    T.matmul(bank[4 + i][NOPE:QKW, :].rearrange("p (b t) -> p b t", b=2), cc("rot", 0, QKW, NOPE, QKW),
                             t[0:QKW, h:h + 2, L0:TOK], start=True, stop=True).then_inc(mrot_done, 1)
                gate(5)
                pe.wait_ge(vm_out, (l + 1) * 2)
                pe.wait_ge(mla_roped, FROM + (l + 1) * 4)
                for t, c0 in enumerate(TILES):
                    for b in range(2):
                        c = (t % 2) * 2 * P + b * P
                        ins = T.matmul(bank[2 + t // 2][:, c:c + P], pj[:, PJ["xa0"] + b, c0:c0 + P],
                                       pc("pool_w", b * P, (b + 1) * P), start=True, stop=True)
                    if t >= 1:
                        ins.then_inc(tm1_done, 1)
                for t, c0 in enumerate(TILES):
                    for b in range(2):
                        ins = T.matmul(bank[4 + t][:, b * 2 * P:(b + 1) * 2 * P], pj[:, PJ["xc0"] + b, c0:c0 + P], cc("dft"),
                                       start=True, stop=True)
                    ins.then_inc(tm1_done, 1)
                gate(6)
                pe.wait_ge(tm1_out, (l + 1) * 5)
                pe.wait_ge(tc_loaded, (l + 1) * 16)
                for b in range(2):
                    for g in (2 * b, 2 * b + 1):
                        r = HD * (g % 2)
                        T.matmul(bank[2 + b][r:r + HD, 0:CTX], zz[:, 0, g * HD:(g + 1) * HD],
                                 tc[:, TP_C + g * CTX:TP_C + (g + 1) * CTX], start=True, stop=True)
                        for t in range(2):
                            c = TP_L + (g * 2 + t) * LAT
                            ins = T.matmul(bank[2 + b][r:r + HD, L0:TOK], zz[:, 1 + t, g * HD:(g + 1) * HD],
                                           tc[:, c:c + LAT], start=t == 0, stop=t == 1)
                    ins.then_inc(tm2_done, 1)
                for b in range(2):
                    for q in range(2):
                        T.matmul(bank[4 + b][:, 0:CTX], fa[:, 0, (2 * b + q) * P:(2 * b + q + 1) * P],
                                 tc[:, TF_C + q * CTX:TF_C + (q + 1) * CTX], start=q == 0, stop=q == 1)
                    for t in range(2):
                        for q in range(2):
                            c = TF_L + (q * 2 + t) * LAT
                            ins = T.matmul(bank[4 + b][:, L0:TOK], fa[:, 1 + t, (2 * b + q) * P:(2 * b + q + 1) * P],
                                           tc[:, c:c + LAT], start=t == 0 and q == 0, stop=t == 1 and q == 1)
                    ins.then_inc(tm2_done, 1)
                gate(7)

                pe.wait_ge(tm2_out, (l + 1) * 4)

                def scores(i):
                    qt, h = (i // 4) % 3, i % 4
                    q0 = TILES[qt]
                    if i >= 1:
                        pe.wait_ge(exp_done, l * STEPS + i)
                    maps = 2 if i < 12 else 1
                    for m in range(maps):
                        if i < 12:
                            p0, b = (h % 2) * HD + m * DAD, h // 2
                            q = pj[p0:p0 + DAD, PJ["q0"] + b, q0:q0 + P]
                            k_self, k_past = pj[p0:p0 + DAD, PJ["k0"] + b, :], ca[p0:p0 + DAD, b * PAST:(b + 1) * PAST]
                        else:
                            q = qm[0:QKW, h, q0:q0 + P]
                            k_self, k_past = km[0:QKW, h, :], kmp[0:QKW, h, :]
                        out = bank[2 + m]
                        if qt == 0:
                            ins = T.matmul(out[:, 0:P], q, k_self[:, 0:CTX], start=True, stop=True)
                        else:
                            T.matmul(out[:, 0:LAT], q, k_self[:, L0:TOK], start=True, stop=True)
                            ins = T.matmul(out[:, LAT:LAT + PAST], q, k_past, start=True, stop=True)
                    ins.then_inc(scores_done, 1)

                def turn(i):
                    pe.wait_ge(probs_ready, l * STEPS + i + 1)
                    pe.wait_ge(turned_out, FROM + l * STEPS + i)
                    n = 1 if (i // 4) % 3 == 0 else 3
                    for k in range(n):
                        ins = T.transpose(bank[4][:, k * P:(k + 1) * P], exps[:, i % 2, 0, k * P:(k + 1) * P], cc("ident"))
                    ins.then_inc(turned, 1)

                def weigh(i):
                    qt, h = (i // 4) % 3, i % 4
                    pe.wait_ge(turned_out, FROM + l * STEPS + i + 1)
                    if h == 0:
                        pe.wait_ge(av_out, FROM + l * 6 + i // 4)
                    out = bank[5][(h % 2) * HD:(h % 2) * HD + HD, (h // 2) * P:(h // 2) * P + P]
                    hs = slice(h * HD, (h + 1) * HD)
                    if i < 12:
                        vs = [val[:, 0, hs]] if qt == 0 else [val[:, 1, hs], val[:, 2, hs], ca[:, 256 + h * HD:256 + (h + 1) * HD]]
                    else:
                        vs = [vm[:, 0, hs]] if qt == 0 else [vm[:, 1, hs], vm[:, 2, hs], vm[:, 3, hs]]
                    for k, v in enumerate(vs):
                        ins = T.matmul(out, v, pt[:, k, :], start=k == 0, stop=k == len(vs) - 1)
                    ins.then_inc(av_done, 1)

                for i in range(STEPS):
                    if i >= 1:
                        turn(i - 1)
                    scores(i)
                    if i == 13:
                        pe.wait_ge(subsq, l + 1)
                        for b in range(2):
                            T.matmul(bank[(6, 3)[b]][:, 0:TOK], cc("ones64"), wide[:, b, :], start=True, stop=True).then_inc(subss, 1)
                    gate(PREP_GATES + i)
                    if i >= 1:
                        weigh(i - 1)
                    if i == 13:
                        pe.wait_ge(mod_read, 1 + 3 * l + 1)
                    ada_units(sum(ADA_STEP[:i]), sum(ADA_STEP[:i + 1]))
                turn(STEPS - 1)
                ada_units(sum(ADA_STEP), ADA_OWN)
                weigh(STEPS - 1)

                with pe.Fori(0, U_BR // SLOTS) as i:
                    pe.wait_ge(gate_ready, (l + 1) * U_GATE)
                    pe.wait_ge(exp_done, (l + 1) * STEPS)
                    for j in range(SLOTS):
                        unit_ready(B0 + j, i)
                        for n in range(4):
                            pe.wait_ge(br_lo, l * 8 + 2 * n + 2)
                            if j == 0:
                                pe.wait_ge(gated_ready, FROM + l * KD * 4 + i * (13 + n))
                            else:
                                pe.wait_ge(gated_ready, FROM + (l * KD + i * SLOTS + j - 1) * 4 + n + 1)
                            ins = dense(bank[n][:, 0:TOK], B0 + j, (2 * n, 2 * n + 1), HI[2 * n:2 * n + 2], LO[2 * n:2 * n + 2])
                            ins.then_inc(br_done if n < 3 else unit_done, 1)
                MH = [mhi[:, k, :] for k in range(KD)]
                ML = [mlo[:, k, :] for k in range(KD)]
                with pe.Fori(0, U_OUT // SLOTS) as i:
                    pe.wait_ge(mrg_lo, (l + 1) * KD)
                    pe.wait_ge(av_out, FROM + (l + 1) * 6)
                    pe.wait_ge(turned_out, FROM + (l + 1) * STEPS)
                    pe.wait_ge(mod_read, 1 + 3 * l + 2)
                    for j in range(SLOTS):
                        unit_ready(O0 + j, i)
                        pe.wait_ge(x1_ready, FROM + l * KD + i * (j + 1))
                        dense(bank[4 + j][:, 0:TOK], O0 + j, range(KD), MH, ML).then_inc(unit_done, 1)
                square_sums(1)
                with pe.If(l < DEPTH - 1):
                    ada_units(ADA_OWN, ADA_OWN + 8)
                with pe.Fori(0, U_UP // SLOTS) as i:
                    pe.wait_ge(norm_lo, (l * 2 + 1) * KD + KD)
                    for j in range(SLOTS):
                        unit_ready(P0 + j, i)
                        pe.wait_ge((conv_g, conv_v)[j % 2], FROM + l * FB + i * 2 + j // 2)
                        dense(bank[j][:, 0:TOK], P0 + j, range(KD), HI, LO).then_inc(unit_done, 1)
                with pe.If(l < DEPTH - 1):
                    ada_units(ADA_OWN + 8, ADA)
                with pe.Fori(0, 2) as i:
                    pe.wait_ge(mlp_lo, FROM + (l + 1) * FB + 1)
                    for d in range(4):
                        pe.wait_ge(x2_ready, FROM + l * KD + i * (d + 1))
                        for q in range(3):
                            u = D0 + 3 * d + q
                            unit_ready(u, i * 3)
                            k0 = q * KD
                            n = min(KD, FB - k0)
                            dense(bank[d][:, 0:TOK], u, range(n), [ghi[:, k0 + k, :] for k in range(n)],
                                  [glo[:, k0 + k, :] for k in range(n)], first=q == 0, last=q == 2).then_inc(unit_done, 1)


def _constants():
    import numpy as np
    f = np.float32
    cn = np.zeros((P, CW), f)

    def put(name, a):
        cn[:a.shape[0], CCOL[name][0]:CCOL[name][0] + a.shape[1]] = a

    put("ident", np.eye(P))
    put("ones", np.ones((P, P)))
    put("ones32", np.kron(np.eye(4), np.ones((32, 32))))
    put("ones64", np.kron(np.eye(2), np.ones((64, 64))))
    r = np.zeros((16, 16))
    for i in range(8):
        r[i, i + 8], r[i + 8, i] = -1, 1
    put("rot", np.kron(np.eye(8), r).T)
    j = np.arange(HD)
    ang = 2 * np.pi * np.outer(j, j) / HD
    put("dft", np.concatenate([np.kron(np.eye(2), np.cos(ang)), np.kron(np.eye(2), np.sin(ang))], 1))
    half = 8
    inv = (np.float32(10000.0) ** (-np.arange(half, dtype=f) / f(half))).astype(f)
    t = np.arange(LAT)
    for name, fn in (("cos", np.cos), ("sin", np.sin)):
        rows = fn((t // GRID_W).astype(f)[None, :] * inv[:, None])
        cols = fn((t % GRID_W).astype(f)[None, :] * inv[:, None])
        put(name, np.tile(np.concatenate([rows, rows, cols, cols]), (4, 1)))

    tc = np.zeros((P, TW), f)
    for n_tok, p0, f0 in ((CTX, TP_C, TF_C), (LAT, TP_L, TF_L)):
        tt = np.arange(n_tok)
        tiles = n_tok // P
        for g, w in enumerate(WINDOWS):
            lo, hi = np.clip(tt - w // 2, 0, n_tok), np.clip(tt + w // 2, 0, n_tok)
            m = ((tt[:, None] >= lo[None, :]) & (tt[:, None] < hi[None, :])) / (hi - lo)[None, :] - np.eye(n_tok)
            for k in range(tiles):
                c = p0 + (g * tiles + k) * n_tok
                tc[:, c:c + n_tok] = m[k * P:(k + 1) * P]
        ang = 2 * np.pi * (np.outer(tt, tt) % n_tok) / n_tok
        s = 1.0 / math.sqrt(n_tok * HD)
        for q, m in enumerate((np.cos(ang) * s, -np.sin(ang) * s)):
            for k in range(tiles):
                c = f0 + (q * tiles + k) * n_tok
                tc[:, c:c + n_tok] = m[k * P:(k + 1) * P]
    return cn, tc


def kernel(**inputs):
    import numpy as np
    import concourse.bacc as bacc
    from concourse.bass_utils import run_bass_kernel_spmd

    w = {k: np.asarray(v) for k, v in inputs.items()}
    f = np.float32

    def units(a, n):
        k = a.shape[0] // P
        return a.reshape(k, P, n, P).transpose(2, 1, 0, 3).reshape(n, P, k * P)

    stream = np.zeros((DEPTH * UNITS, P, UNIT), f)
    ada = np.zeros((DEPTH * ADA, P, UNIT), f)
    par = np.zeros((DEPTH, P, PW), f)
    cache = np.zeros((DEPTH, P, HC), f)
    for l in range(DEPTH):
        wi = w["w_in"][l]
        g, base = wi[:, :4 * D], 4 * D
        xa, qkv, xc, ml = np.split(wi[:, base:], [256, 256 + 768, 256 + 768 + 256], axis=1)
        last = np.zeros((D, P), f)
        last[:, 0:NOPE] = ml[:, P:QL]
        last[:, NOPE:QKW] = ml[:, QL + KVL:]
        mix = np.concatenate([xa, qkv, xc, ml[:, 0:P], ml[:, QL:QL + KVL], last], axis=1)
        s = stream[l * UNITS:(l + 1) * UNITS]
        s[0:G0] = units(mix, U_MIX)
        s[G0:B0] = units(g, U_GATE)
        s[B0:O0] = units(w["w_branch"][l].reshape(D, D), KD)
        s[O0:P0] = units(w["w_out"][l], KD)
        up = units(w["w_up"][l], 2 * FB)
        s[P0:D0:2], s[P0 + 1:D0:2] = up[:FB], up[FB:]
        dn = w["w_down"][l].reshape(FB, P, KD, P).transpose(2, 1, 0, 3)
        for q in range(3):
            part = dn[:, :, q * KD:(q + 1) * KD]
            s[D0 + q::3, :, 0:part.shape[2] * P] = part.reshape(KD, P, -1)
        m = w["w_ada"][l].reshape(KD, P, 3, ADA_G, 2, 2, STRIP).transpose(2, 0, 4, 1, 5, 3, 6).reshape(ADA, P, UNIT)
        ada[l * ADA_G:(l + 1) * ADA_G] = m[:ADA_G]
        ada[DEPTH * ADA_G + l * (ADA - ADA_G):][:ADA - ADA_G] = m[ADA_G:]

        def put(name, a):
            a = np.asarray(a)
            par[l, :a.shape[0], PCOL[name][0]:PCOL[name][0] + a.shape[1]] = a

        put("g1", w["g_norm1"][l].reshape(KD, P).T)
        put("g2", w["g_norm2"][l].reshape(KD, P).T)
        put("b_ada", w["b_ada"][l].reshape(ADA, P).T)
        put("conv_w", w["conv_w"][l].reshape(3, 2, FB, P).transpose(3, 0, 2, 1).reshape(P, -1))
        put("conv_b", w["conv_b"][l].reshape(2, FB, P).transpose(2, 1, 0).reshape(P, -1))
        put("pool_scale", w["pool_scale"][l].reshape(2, P).T)
        put("qn", np.tile(w["diff_qnorm"][l], 4)[:, None])
        put("kn", np.tile(w["diff_knorm"][l], 4)[:, None])
        put("subln", np.tile(w["diff_subln"][l], 2)[:, None])
        init = 0.8 - 0.6 * math.exp(-0.3 * l)
        put("lam_init", np.full((P, 1), init, f))
        put("one_minus_init", np.full((P, 1), 1.0 - init, f))
        put("lam", np.broadcast_to(w["diff_lambda"][l].reshape(1, -1), (P, 4 * DAD)))
        put("qa_a", w["mla_qa_norm"][l][0:P, None])
        put("qa_b", w["mla_qa_norm"][l][P:, None])
        put("kvn", w["mla_kv_norm"][l][:, None])
        put("mqn", w["mla_qnorm"][l][:, None])
        put("mkn", w["mla_knorm"][l][:, None])
        put("w_uq_a", w["w_uq"][l][0:P])
        put("w_uq_b", w["w_uq"][l][P:])
        put("w_ukv", w["w_ukv"][l])
        for b in range(2):
            for q in range(2):
                c = PCOL["pool_w"][0] + b * P + q * HD
                par[l, q * HD:(q + 1) * HD, c:c + HD] = w["pool_w"][l][2 * b + q]
        cache[l, :, 0:256] = w["cache_diff_k"][0, l].reshape(PAST, 2, P).transpose(2, 1, 0).reshape(P, 256)
        cache[l, :, 256:512] = w["cache_diff_v"][0, l].reshape(PAST, 256)
        cache[l, :, 512:640] = w["cache_mla_ckv"][0, l].T
        cache[l, NOPE:QKW, 640:768] = w["cache_mla_krope"][0, l].T

    x_in = np.zeros((P, KD, TOK), f)
    x_in[:, :, 0:CTX] = w["x_prompt"][0].reshape(CTX, KD, P).transpose(2, 1, 0)
    x_in[:, :, L0:] = w["x_sample"][0].reshape(LAT, KD, P).transpose(2, 1, 0)
    cond = np.stack([w["c_ctx"].reshape(KD, P).T, w["c"][0].reshape(KD, P).T], axis=2).reshape(P, 2 * KD)
    cn, tc = _constants()
    arrays = {"stream": stream, "ada_w": ada, "params": par, "caches": cache, "consts": cn, "time_consts": tc,
              "x_in": x_in.reshape(P, KD * TOK), "cond": np.ascontiguousarray(cond)}
    outs = {"y_out": (P, KD * TOK), "k_out": (DEPTH, P, 2 * CTX), "v_out": (DEPTH, CTX, 256),
            "ckv_out": (DEPTH, KVL, CTX), "krope_out": (DEPTH, ROPE, CTX)}
    nc = bacc.Bacc("TRN2", target_bir_lowering=False, num_devices=1)
    args = {k: nc.dram_tensor(k, v.shape, F32, kind="ExternalInput").ap() for k, v in arrays.items()}
    args |= {k: nc.dram_tensor(k, v, F32, kind="ExternalOutput").ap() for k, v in outs.items()}
    program(nc, **args)
    got = run_bass_kernel_spmd(nc, [arrays], core_ids=[0]).results[0]
    y = np.asarray(got["y_out"]).reshape(P, KD, TOK)
    y_prompt = y[:, :, 0:CTX].transpose(2, 1, 0).reshape(1, CTX, D)
    y_sample = y[:, :, L0:].transpose(2, 1, 0).reshape(1, LAT, D)
    k = np.asarray(got["k_out"]).reshape(DEPTH, P, 2, CTX).transpose(0, 3, 2, 1).reshape(1, DEPTH, CTX, HEADS, HD)
    v = np.asarray(got["v_out"]).reshape(1, DEPTH, CTX, HEADS, HD)
    ckv = np.asarray(got["ckv_out"]).transpose(0, 2, 1).reshape(1, DEPTH, CTX, KVL)
    kr = np.asarray(got["krope_out"]).transpose(0, 2, 1).reshape(1, DEPTH, CTX, ROPE)
    return tuple(np.ascontiguousarray(a) for a in (y_prompt, y_sample, k, v, ckv, kr))
```

```python
import math
from contextlib import ExitStack

import concourse.bass as bass
from concourse import mybir

F32 = mybir.dt.float32
F32R = mybir.dt.float32r
ACT = mybir.ActivationFunctionType
ALU = mybir.AluOpType
AX = mybir.AxisListType.X

P = 128
D = 1024
KD = D // P
DEPTH = 2
CTX, LAT, PAST = 128, 256, 128
GAP = 2
L0 = CTX + GAP
TOK = CTX + GAP + LAT
GRID_W = 64
HEADS = 4
HD = 64
DAD = 32
QKW = 96
NOPE, ROPE, VW = 64, 32, 64
QL, KVL = 192, 128
FFN = 2816
FB = FFN // P
EPS = 1e-6
WINDOWS = (2, 4, 8, 16)

UNIT = KD * P
SLOTS = 4
U_MIX, U_GATE, U_BR, U_OUT, U_UP, U_DN = 13, 32, 8, 8, 2 * FB, 3 * KD
G0 = U_MIX
B0 = G0 + U_GATE
O0 = B0 + U_BR
P0 = O0 + U_OUT
D0 = P0 + U_UP
UNITS = D0 + U_DN
SLOT_USES = [len(range(s, UNITS, SLOTS)) for s in range(SLOTS)]
ADA = 48
HEAD, ADA_M, ADA_S, ADA_E = 16, 32, 40, 48
HEAD_PARTS = ((0, 4), (4, 8), (8, 12), (12, 14), (14, 16))
ADA_STEP = [1, 1, 2] * 4 + [0] + [1] * 11
ADA_TAIL = 1
STRIP = 32
PREP_GATES = 8
ROPE_STEPS = (2, 4, 6, 8)
STEPS = 24

MIX = ["xa0", "xa1", "q0", "q1", "k0", "k1", "v0", "v1", "xc0", "xc1", "cq", "ckv", "cqr"]
PJ = {n: i for i, n in enumerate(("xa0", "xa1", "xc0", "xc1", "q0", "q1", "k0", "k1", "cq", "ckv", "cqr"))}
SPLIT_ORDER = (0, 1, 4, 5, 2, 3, 6, 7)

HEAD_PARAMS = 8 + 8 + ADA
PCOL, _n = {}, 0
for _name, _w in (("g1", 8), ("g2", 8), ("b_ada", ADA), ("conv_w", 3 * 2 * FB), ("conv_b", 2 * FB),
                  ("pool_scale", 2), ("qn", 1), ("kn", 1), ("subln", 1), ("one_minus_init", 1),
                  ("lam_init", 1), ("lam", 4 * DAD), ("qa_a", 1), ("qa_b", 1), ("kvn", 1),
                  ("mqn", 1), ("mkn", 1), ("w_uq_a", HEADS * QKW), ("w_uq_b", HEADS * QKW),
                  ("w_ukv", HEADS * (NOPE + VW)), ("pool_w", 2 * P)):
    PCOL[_name] = (_n, _n + _w)
    _n += _w
PW = _n
CCOL = {n: (i * P, (i + 1) * P) for i, n in enumerate(("ones", "ident", "ones32", "ones64", "rot"))}
CCOL["dft"] = (5 * P, 7 * P)
CCOL["cos"] = (7 * P, 9 * P)
CCOL["sin"] = (9 * P, 11 * P)
CW = 11 * P
TP_C, TP_L = 0, 4 * CTX
TF_C = TP_L + 4 * 2 * LAT
TF_L = TF_C + 2 * CTX
TW = TF_L + 2 * 2 * LAT
HC = 2 * PAST + HEADS * HD + PAST + PAST


ACT_OWN, DVE_OWN = 19, 178


class Links:

    def __init__(self, eng, sem, per_layer):
        self.eng, self.sem, self.per, self.n = eng, sem, per_layer, 0
        self.layer, self.loop, self.step = 0, 0, 0

    def __call__(self, ins):
        self.n += 1
        return ins.then_inc(self.sem, 1)

    def wait(self, but=0):
        self.eng.wait_ge(self.sem, self.layer * self.per + self.loop * self.step + self.n - but)

    def begin(self, index, step):
        self.loop, self.step, self.start = index, step, self.n

    def end(self, times):
        assert self.n - self.start == self.step, (self.n - self.start)
        self.n += self.step * (times - 1)
        self.loop = self.step = 0


def program(nc, stream, ada_w, params, caches, consts, time_consts, x_in, cond,
            y_out, k_out, v_out, ckv_out, krope_out):
    ctx = ExitStack()
    with ctx:
        def tile(name, width, offset, dt=F32, parts=P):
            offset = -(-offset // 32) * 32
            return nc.alloc_sbuf_tensor_at(name, [parts, width], dt, offset=offset), offset + 4 * width

        def sem(name):
            return ctx.enter_context(nc.semaphore(name))

        def blocks(t, width=TOK):
            return t[:, :].rearrange("p (k t) -> p k t", t=width)

        o = nc.sbuf_base
        x_t, o = tile("x", KD * TOK, o)
        act_at = o
        ahi_t, o = tile("act_hi", KD * TOK, o, F32R)
        alo_t, o = tile("act_lo", KD * TOK, o, F32R)
        raw, whi, wlo = [], [], []
        for s in range(SLOTS):
            wlo.append(tile(f"w_lo{s}", UNIT, o, F32R)[0])
            t, o = tile(f"w_raw{s}", UNIT, o)
            raw.append(t)
            t, o = tile(f"w_hi{s}", UNIT, o, F32R)
            whi.append(t)
        ada = []
        for s in range(2):
            t, o = tile(f"ada{s}", UNIT, o)
            ada.append(t)
        par, o = tile("params", PW, o)
        cn, o = tile("consts", CW, o)
        ca, o = tile("cached", HC, o)
        wide_t, o = tile("wide", KD * TOK, o)
        mod_t, o = tile("mod", ADA * 2, o)
        sc1_t, o = tile("scale1", 2 * KD, o)
        sc2_t, o = tile("scale2", 2 * KD, o)
        cond_t, o = tile("cond", 2 * KD, o)
        conds_t, o = tile("cond_silu", STRIP * KD, o)
        lamp_t, o = tile("lam_prod", 2 * DAD, o)
        sm, o = tile("small", 24, o)
        top = o
        gate_a, o = tile("gates_a", PREP_GATES * TOK, top)
        tail = o
        tc, o = tile("time_consts", TW, tail)
        rs_t, o = tile("rstd", 4 * (TOK + PAST), o)
        z_t, o = tile("pool_z", 3 * 2 * P, o)
        fa_t, o = tile("fourier_a", 3 * 4 * P, o)
        prep_end = o
        gate_b, o = tile("gates_b", (U_GATE - PREP_GATES) * TOK, tail)
        o = max(o, prep_end)
        first_at = o
        br_t, o = tile("branch", 8 * TOK, o)
        val_at = o
        val_t, o = tile("val", 3 * HEADS * HD, o)
        vm_t, o = tile("mla_val", 4 * HEADS * VW, o)
        att = o
        pj_t, o = tile("proj", len(PJ) * TOK, att)
        qm_t, o = tile("mla_q", HEADS * TOK, o)
        km_t, o = tile("mla_k", HEADS * TOK, o)
        kmp_t, o = tile("mla_k_past", HEADS * PAST, o)
        pt_t, o = tile("probs_t", 384, o)
        rt_t, rt_end = tile("rope_tmp", 2 * LAT, nc.sbuf_usable_end - 4 * 2 * LAT - 32)
        assert o <= rt_end - 4 * 2 * LAT and rt_end <= nc.sbuf_usable_end, (o, nc.sbuf_usable_end)
        brh_t, o = tile("branch_hi", 6 * TOK, att, F32R)
        brl_t, _ = tile("branch_lo", 8 * TOK, first_at, F32R)
        mhi_t, o = tile("merged_hi", KD * TOK, o, F32R)
        mlo_t, o = tile("merged_lo", KD * TOK, o, F32R)
        ms_t, ms_end = tile("merge_sum", 2 * TOK, val_at)
        assert ms_end <= att
        assert o <= nc.sbuf_usable_end, (o, nc.sbuf_usable_end)
        ghi_t, o = tile("mlp_hi", FB * TOK, top, F32R)
        glo_t, o = tile("mlp_lo", FB * TOK, o, F32R)
        heada_t, heada_end = tile("ada_head_a", 8 * UNIT, o)
        assert heada_end <= rt_end - 4 * 2 * LAT
        headb_t, _ = tile("ada_head_b", 6 * UNIT, act_at)
        ft_t, o = tile("mlp_tmp", 2 * 4 * TOK, o)
        assert o <= nc.sbuf_usable_end, (o, nc.sbuf_usable_end)

        x, ahi, alo, wide = blocks(x_t), blocks(ahi_t), blocks(alo_t), blocks(wide_t)
        mhi, mlo, br, pj = blocks(mhi_t), blocks(mlo_t), blocks(br_t), blocks(pj_t)
        brl, brh = blocks(brl_t), blocks(brh_t)
        ghi, glo = blocks(ghi_t), blocks(glo_t)
        qm, km, kmp = blocks(qm_t), blocks(km_t), blocks(kmp_t, PAST)
        val, vm = blocks(val_t, HEADS * HD), blocks(vm_t, HEADS * VW)
        conds = blocks(conds_t, STRIP)
        condx = lamp_t[:, 0:2 * KD].rearrange("p (k c) -> p k c", c=2)
        heada, headb = blocks(heada_t, UNIT), blocks(headb_t, UNIT)
        head = [heada[:, a] for a in range(8)] + [headb[:, a] for a in range(6)] + [ada[0][:, :], ada[1][:, :]]
        mod, sc1, sc2 = blocks(mod_t, 2), blocks(sc1_t, 2), blocks(sc2_t, 2)
        gated = wide_t[:, :].rearrange("p (a n t) -> p a n t", a=2, n=4)
        msum = blocks(ms_t)
        branch_hi = [brh[:, SPLIT_ORDER.index(b)] if b < 6 else ahi[:, b] for b in range(8)]
        branch_bank = [[use % 7 for use in range(4 * d, 4 * d + 4)] for d in range(KD)]
        ftmp = ft_t[:, :].rearrange("p (a n t) -> p a n t", a=2, n=4)
        gates = [blocks(gate_a)[:, g] if g < PREP_GATES else blocks(gate_b)[:, g - PREP_GATES]
                 for g in range(U_GATE)]
        rs = blocks(rs_t, TOK + PAST)
        exps = wide_t[:, 4 * TOK:4 * TOK + 4 * 384].rearrange("p (a m k) -> p a m k", a=2, m=2)
        pt = pt_t[:, :].rearrange("p (k q) -> p k q", q=P)
        rsn = rs_t[:, 0:TOK]
        zz, fa = blocks(z_t, 2 * P), blocks(fa_t, 4 * P)
        wb = [(whi[s][:, :].rearrange("p (k m) -> p k m", m=P), wlo[s][:, :].rearrange("p (k m) -> p k m", m=P))
              for s in range(SLOTS)]
        small = sm[:, :]
        EPSC, NEGLAM, GSUB = small[:, 0:1], small[:, 1:2], small[:, 2:3]

        def pc(name, a=0, b=None, p0=0, p1=P):
            lo, hi = PCOL[name]
            return par[p0:p1, lo + a:(hi if b is None else lo + b)]

        def cc(name, p0=0, p1=P, a=0, b=None):
            lo, hi = CCOL[name]
            return cn[p0:p1, lo + a:(hi if b is None else lo + b)]

        bank = [ctx.enter_context(nc.psum_tensor(f"bank{i}", [P, 512], F32)) for i in range(8)]
        RANGES = ((0, CTX, 0), (L0, TOK, 1))
        TILES = (0, L0, L0 + P)

        raw_loaded = [sem(f"raw_loaded{s}") for s in range(SLOTS)]
        ada_loaded = [sem(f"ada_loaded{s}") for s in range(2)]
        head_loaded = [sem(f"head_loaded{n}") for n in range(len(HEAD_PARTS))]
        x_loaded = sem("x_loaded")
        cond_loaded, ones_loaded, consts_loaded, head_par_loaded, par_loaded = (
            sem(n) for n in ("cond_loaded", "ones_loaded", "consts_loaded", "head_par_loaded",
                           "par_loaded"))
        tc_loaded, stored, y_stored = sem("tc_loaded"), sem("stored"), sem("y_stored")
        hi_ready, lo_ready, unit_done, ada_done = sem("hi_ready"), sem("lo_ready"), sem("unit_done"), sem("ada_done")
        act_own, dve_own, pool_own = sem("act_own"), sem("dve_own"), sem("pool_own")
        cond_exp, cond_ready, eps_ready, br_gap = sem("cond_exp"), sem("cond_ready"), sem("eps_ready"), sem("branch_gap")
        sq_ready, ss_done, rstd_ready, norm_full, norm_hi, norm_lo = (
            sem(n) for n in ("sq_ready", "ss_done", "rstd_ready", "norm_full", "norm_hi", "norm_lo"))
        mod_read = sem("mod_read")
        mix_out, gate_ready = sem("mix_out"), sem("gate_ready")
        lam_prod, lam_exp = sem("lam_prod_ready"), sem("lam_exp")
        psq, pss, prs = sem("prep_sq"), sem("prep_ss"), sem("prep_rstd")
        da_normed, ckv_normed, rot_done, da_roped = sem("da_normed"), sem("ckv_normed"), sem("rot_done"), sem("da_roped")
        uq_done, uq_out, uqsq, uqss, uqrs, uq_normed = (
            sem(n) for n in ("uq_done", "uq_out", "uq_sq", "uq_ss", "uq_rstd", "uq_normed"))
        uk_done, uk_out, kr_copied, uksq, ukss, ukrs, uk_normed = (
            sem(n) for n in ("uk_done", "uk_out", "kr_copied", "uk_sq", "uk_ss", "uk_rstd", "uk_normed"))
        vm_done, vm_out, mrot_done, mla_roped = sem("vm_done"), sem("vm_out"), sem("mrot_done"), sem("mla_roped")
        tm1_done, tm1_out, tm2_done, tm2_out = sem("tm1_done"), sem("tm1_out"), sem("tm2_done"), sem("tm2_out")
        scores_done, nm_ready, exp_done, probs_ready, turned, turned_out, av_done, av_out = (
            sem(n) for n in ("scores_done", "negmax_ready", "exp_done", "probs_ready", "turned", "turned_out",
                             "av_done", "av_out"))
        subsq, subss, subrs, sub_out = sem("sub_sq"), sem("sub_ss"), sem("sub_rstd"), sem("sub_out")
        br_hi, br_lo = sem("branch_hi"), sem("branch_lo")
        br_done, gated_ready, merged_ready, mrg_hi, mrg_lo = (
            sem(n) for n in ("branch_done", "gated_ready", "merged_ready", "merged_hi", "merged_lo"))
        x1_ready, x2_ready = sem("x1_ready"), sem("x2_ready")
        tap1, conv_g, conv_v, mlp_tanh, mlp_full, mlp_hi, mlp_lo = (
            sem(n) for n in ("tap1", "conv_gate", "conv_val", "mlp_tanh", "mlp_full", "mlp_hi", "mlp_lo"))
        FROM = 1
        block = ctx.enter_context(nc.Block())

        @block.sync
        def _(sp):
            def load_head(a, at):
                part = next(n for n, (a0, a1) in enumerate(HEAD_PARTS) if a0 <= a < a1)
                sp.dma_start(head[a], ada_w[at, :, :].rearrange("a p n -> (a p) n")).then_inc(head_loaded[part], 16)

            sp.dma_start(cond_t[:, :], cond).then_inc(cond_loaded, 16)
            sp.dma_start(cn[:, 0:P], consts[:, 0:P]).then_inc(ones_loaded, 16)
            for a in range(HEAD):
                if a == 4:
                    sp.dma_start(x_t[:, :], x_in).then_inc(x_loaded, 16)
                load_head(a, slice(a, a + 1))
            with sp.Fori(0, DEPTH) as l:
                def load_ada(a):
                    sp.wait_ge(ada_done, l * ADA + a - 1)
                    sp.dma_start(ada[a % 2][:, :], ada_w[bass.ds(l * (ADA - HEAD) + DEPTH * HEAD + a - HEAD, 1), :, :].rearrange("a p n -> (a p) n")
                                 ).then_inc(ada_loaded[a % 2], 16)

                def load_unit(u, i=0):
                    sp.wait_ge(unit_done, FROM + l * UNITS + i * SLOTS + max(u - SLOTS + 1, 0))
                    sp.dma_start(raw[u % SLOTS][:, :],
                                 stream[bass.ds(l * UNITS + i * SLOTS + u, 1), :, :].rearrange("a p n -> (a p) n")
                                 ).then_inc(raw_loaded[u % SLOTS], 16)

                def load_params(c0, c1, done):
                    sp.dma_start(par[:, c0:c1], params[bass.ds(l, 1), :, c0:c1].rearrange("a p n -> (a p) n")).then_inc(done, 16)

                sp.wait_ge(x2_ready, FROM + l * KD)
                load_params(0, HEAD_PARAMS, head_par_loaded)
                load_unit(0)
                load_unit(1)
                load_params(HEAD_PARAMS, PW, par_loaded)
                load_unit(2)
                load_unit(3)
                sp.dma_start(ca[:, :], caches[bass.ds(l, 1), :, :].rearrange("a p n -> (a p) n")).then_inc(par_loaded, 16)
                with sp.If(l < 1):
                    sp.dma_start(cn[:, P:CW], consts[:, P:CW]).then_inc(consts_loaded, 16)
                sp.dma_start(tc[:, :], time_consts).then_inc(tc_loaded, 16)
                load_ada(HEAD)
                load_ada(HEAD + 1)
                first_step = G0 + PREP_GATES
                for u in range(SLOTS, first_step + SLOTS):
                    load_unit(u)
                used = HEAD
                for i in range(STEPS):
                    for a in range(used + 2, used + ADA_STEP[i] + 2):
                        load_ada(a)
                    used += ADA_STEP[i]
                    load_unit(first_step + SLOTS + i)
                for a in range(used + 2, used + 2 + ADA_TAIL):
                    load_ada(a)
                for u in range(first_step + SLOTS + STEPS, P0 + SLOTS):
                    load_unit(u)
                for a in range(used + 2 + ADA_TAIL, ADA_E):
                    load_ada(a)
                with sp.Fori(0, U_UP // SLOTS) as i:
                    for j in range(SLOTS):
                        load_unit(P0 + SLOTS + j, i)
                with sp.If(l < DEPTH - 1):
                    for n, u in enumerate(range(D0 + SLOTS, UNITS)):
                        load_unit(u)
                        if n == 1:
                            sp.wait_ge(mlp_lo, FROM + 1 + (l + 1) * FB)
                        if n == HEAD - 1:
                            sp.wait_ge(ada_done, (l + 1) * ADA)
                        if 1 <= n <= HEAD:
                            load_head(n - 1, bass.ds(l * HEAD + n - 1 + HEAD, 1))
                with sp.If(l == DEPTH - 1):
                    for u in range(D0 + SLOTS, UNITS):
                        load_unit(u)
            for k0, k1 in ((0, 6), (6, 7), (7, 8)):
                sp.wait_ge(x2_ready, FROM + (DEPTH - 1) * KD + k1)
                sp.dma_start(y_out[:, k0 * TOK:k1 * TOK], x_t[:, k0 * TOK:k1 * TOK]).then_inc(y_stored, 16)
            sp.wait_ge(y_stored, 48)
            sp.wait_ge(stored, 16 * 4 * DEPTH)

        @block.gpsimd
        def _(pool):
            nc.gpsimd.memset(small[:, 0:1], EPS).then_inc(eps_ready, 1)
            own = Links(pool, pool_own, KD * 2)
            with pool.Fori(0, DEPTH) as l:
                own.layer = l
                own.n = 0
                pool.wait_ge(da_normed, l * 4 + 4)
                pool.dma_start(k_out[bass.ds(l, 1), :, :].rearrange("a p n -> (a p) n").rearrange("p (b t) -> p b t", t=CTX),
                               pj[:, PJ["k0"]:PJ["k1"] + 1, 0:CTX]).then_inc(stored, 16)
                pool.dma_start(v_out[bass.ds(l, 1), :, :].rearrange("a p n -> (a p) n"), val[:, 0, :]).then_inc(stored, 16)
                pool.dma_start(krope_out[bass.ds(l, 1), :, :].rearrange("a p n -> (a p) n"),
                               pj[NOPE:QKW, PJ["cqr"], 0:CTX]).then_inc(stored, 16)
                pool.wait_ge(ckv_normed, l + 1)
                pool.dma_start(ckv_out[bass.ds(l, 1), :, :].rearrange("a p n -> (a p) n"),
                               pj[:, PJ["ckv"], 0:CTX]).then_inc(stored, 16)
                pool.wait_ge(stored, l * 64 + 64)
                for d in range(KD):
                    s = d % 2
                    pool.wait_ge(gated_ready, FROM + (l * KD + d + 1) * 4)
                    if d >= 2:
                        pool.wait_ge(mrg_lo, l * KD + d - 1)
                    own(nc.gpsimd.tensor_tensor(gated[:, s, 0, :], gated[:, s, 0, :], gated[:, s, 1, :], ALU.add))
                    own(nc.gpsimd.tensor_tensor(gated[:, s, 2, :], gated[:, s, 2, :], gated[:, s, 3, :], ALU.add))
                    own.wait()
                    nc.gpsimd.tensor_tensor(msum[:, s, :], gated[:, s, 0, :], gated[:, s, 2, :], ALU.add).then_inc(merged_ready, 1)

        @block.scalar
        def _(act):
            def A(out, in_, func, **kw):
                return nc.scalar.activation(out, in_, func, **kw)

            def logs():
                nc.scalar.preload_act_table_set("natural_log_exp_and_others")

            def tanhs():
                nc.scalar.preload_act_table_set("exp_and_others")

            tanhs()
            act.wait_ge(eps_ready, 1)
            act.wait_ge(cond_loaded, 16)
            A(condx, cond_t[:, :].rearrange("p (k c) -> p k c", c=2), ACT.Exp, scale=-1.0).then_inc(cond_exp, 1)

            def square(k):
                A(wide[:, k:k + 2, :], x[:, k:k + 2, :], ACT.Square).then_inc(sq_ready, 1)

            act.wait_ge(x_loaded, 16)
            for k in range(0, KD, 2):
                square(k)
            own = Links(act, act_own, ACT_OWN)
            with act.Fori(0, DEPTH) as l:
                own.layer = l
                own.n = 0

                def split(u, i=0):
                    s = u % SLOTS
                    act.wait_ge(raw_loaded[s], 16 * (l * SLOT_USES[s] + i + u // SLOTS + 1))
                    act.wait_ge(unit_done, FROM + l * UNITS + i * SLOTS + max(u - SLOTS + 1, 0))
                    A(whi[s][:, :], raw[s][:, :], ACT.Copy).then_inc(hi_ready, 1)

                def rstds(items, after=None):
                    for i in range(len(items) + 1):
                        if i < len(items):
                            out, ss, width, ready, (semaphore, count) = items[i]
                            act.wait_ge(semaphore, count)
                            own(A(out, ss, ACT.Ln, scale=1.0 / width, bias=EPSC[0:out.shape[0]]))
                        if i >= 1:
                            out, ready = items[i - 1][0], items[i - 1][3]
                            own.wait(1 if i < len(items) else 0)
                            A(out, out, ACT.Exp, scale=-0.5).then_inc(ready, 1)
                        if after and i in after:
                            after[i]()

                def norm(n):
                    shift = mod[:, 0:8, :] if n == 0 else mod[:, 24:32, :]
                    act.wait_ge(ss_done, l * 2 + n + 1)
                    own(A(rsn, bank[4][:, 0:TOK], ACT.Ln, scale=1.0 / D, bias=EPSC))
                    own.wait()
                    A(rsn, rsn, ACT.Exp, scale=-0.5).then_inc(rstd_ready, 1)
                    if n == 0:
                        split(0)
                        split(1)
                    else:
                        tanhs()
                        split(P0 + 2)
                    for k in range(KD):
                        act.wait_ge(norm_full, (l * 2 + n) * KD + k + 1)
                        for a, e, c in RANGES:
                            ins = A(ahi[:, k, a:e], wide[:, k, a:e], ACT.Identity, bias=shift[:, k, c:c + 1])
                        ins.then_inc(norm_hi, 1)

                logs()
                norm(0)
                act.wait_ge(lam_prod, l + 1)
                A(small[:, 6:8], small[:, 4:6], ACT.Exp).then_inc(lam_exp, 1)
                for u in range(U_MIX):
                    split(u + 2)
                    act.wait_ge(unit_done, FROM + l * UNITS + u + 1)
                    name = MIX[u]
                    if name in PJ:
                        rows = QKW if name == "cqr" else P
                        A(pj[0:rows, PJ[name], :], bank[u % 2][0:rows, 0:TOK], ACT.Copy).then_inc(mix_out, 1)
                    else:
                        c = P * (u - MIX.index("v0"))
                        A(val[:, :, c:c + P], bank[u % 2][:, 0:3 * P].rearrange("p (t c) -> p t c", c=P),
                          ACT.Copy).then_inc(mix_out, 1)
                act.wait_ge(mix_out, (l + 1) * U_MIX)
                for i, (name, rows) in enumerate((("q0", P), ("q1", P), ("k0", P), ("k1", P), ("cq", P), ("cqr", NOPE), ("ckv", P))):
                    A(wide[0:rows, i, :], pj[0:rows, PJ[name], :], ACT.Square).then_inc(psq, 1)

                def gate(g):
                    u = G0 + g
                    act.wait_ge(unit_done, FROM + l * UNITS + u + 1)
                    if g < PREP_GATES:
                        A(gates[g], bank[u % 2][:, 0:TOK], ACT.Copy).then_inc(gate_ready, 1)
                    else:
                        A(gates[g], bank[u % 2][:, 0:TOK], ACT.Tanh, scale=0.5).then_inc(gate_ready, 1)

                outs = [rs_t[:, i * TOK:(i + 1) * TOK] for i in range(5)] + [z_t[:, 0:TOK]]
                rstds([(outs[i], bank[2 + i][:, 0:TOK], (DAD, DAD, DAD, DAD, QL, KVL)[i], prs, (pss, l * 6 + i + 1))
                       for i in range(6)], {2: lambda: split(G0 + 2)})
                gate(0)
                split(G0 + 3)
                for h in range(HEADS):
                    act.wait_ge(uq_done, l * HEADS + h + 1)
                    A(qm[0:QKW, h, :], bank[4 + h][0:QKW, 0:TOK], ACT.Copy).then_inc(uq_out, 1)
                act.wait_ge(uq_out, (l + 1) * HEADS)
                A(wide[0:QKW, 0:4, :], qm[0:QKW, :, :], ACT.Square).then_inc(uqsq, 1)
                gate(1)
                split(G0 + 4)
                rstds([(rs[0:QKW, h, 0:TOK], bank[4 + h][0:QKW, 0:TOK], QKW, uqrs, (uqss, l * HEADS + h + 1))
                       for h in range(HEADS)])
                gate(2)
                split(G0 + 5)
                act.wait_ge(vm_done, l * 2 + 1)
                A(vm[:, 0:2, :], bank[3][:, :].rearrange("p (t c) -> p t c", t=2), ACT.Copy).then_inc(vm_out, 1)
                act.wait_ge(uk_out, (l + 1) * 5)
                act.wait_ge(kr_copied, (l + 1) * 2)
                A(wide[0:QKW, 0:4, :], km[0:QKW, :, :], ACT.Square).then_inc(uksq, 1)
                A(wide_t[0:QKW, 4 * TOK:4 * TOK + 512], kmp_t[0:QKW, :], ACT.Square).then_inc(uksq, 1)
                gate(3)
                split(G0 + 6)
                act.wait_ge(uq_normed, (l + 1) * HEADS)
                rstds([(rs_t[0:QKW, h * TOK:(h + 1) * TOK], bank[4 + h][0:QKW, 0:TOK], QKW, ukrs, (ukss, l * 5 + h + 1))
                       for h in range(HEADS)]
                      + [(rs_t[0:QKW, 4 * TOK:4 * TOK + 512], bank[2][0:QKW, :], QKW, ukrs, (ukss, l * 5 + 5))])
                act.wait_ge(vm_done, l * 2 + 2)
                A(vm[:, 2:4, :], bank[3][:, :].rearrange("p (t c) -> p t c", t=2), ACT.Copy).then_inc(vm_out, 1)
                gate(4)
                split(G0 + 7)
                gate(5)
                split(G0 + 8)
                act.wait_ge(prs, (l + 1) * 6)
                act.wait_ge(ckv_normed, l + 1)
                act.wait_ge(tm1_done, l * 5 + 1)
                A(zz[:, 0:2, :], bank[2][:, :].rearrange("p (t c) -> p t c", t=2), ACT.Copy).then_inc(tm1_out, 1)
                act.wait_ge(tm1_done, l * 5 + 2)
                A(zz[:, 2, :], bank[3][:, 0:2 * P], ACT.Copy).then_inc(tm1_out, 1)
                for t in range(3):
                    act.wait_ge(tm1_done, l * 5 + 3 + t)
                    A(fa[:, t, :], bank[4 + t][:, :], ACT.Copy).then_inc(tm1_out, 1)
                gate(6)
                split(G0 + 9)
                for b in range(2):
                    act.wait_ge(tm2_done, l * 4 + b + 1)
                    for a, e, _ in RANGES:
                        ins = A(br[:, b, a:e], bank[2 + b][:, a:e], ACT.Copy, scale=pc("pool_scale", b, b + 1))
                    ins.then_inc(tm2_out, 1)
                for b in range(2):
                    act.wait_ge(tm2_done, l * 4 + b + 3)
                    for a, e, _ in RANGES:
                        ins = A(br[:, 4 + b, a:e], bank[4 + b][:, a:e], ACT.Copy)
                    ins.then_inc(tm2_out, 1)
                gate(7)
                tanhs()

                def turn_out(i):
                    act.wait_ge(turned, l * STEPS + i + 1)
                    act.wait_ge(av_done, FROM + l * STEPS + i)
                    n = P if (i // 4) % 3 == 0 else 3 * P
                    A(pt_t[:, 0:n], bank[4][:, 0:n], ACT.Copy).then_inc(turned_out, 1)

                def split_branch(n):
                    b = SPLIT_ORDER[n]
                    A(branch_hi[b], br[:, b, :], ACT.Copy).then_inc(br_hi, 1)

                for i in range(STEPS):
                    split(G0 + PREP_GATES + i + 2)
                    if i >= 1:
                        turn_out(i - 1)
                    if 2 <= i < 6:
                        if i == 2:
                            act.wait_ge(tm2_out, (l + 1) * 4)
                            act.wait_ge(br_gap, l + 1)
                        split_branch(i - 2)
                    if i in (17, 18):
                        act.wait_ge(sub_out, (l + 1) * 2)
                        split_branch(i - 13)
                    maps = 2 if i < 12 else 1
                    n = P if (i // 4) % 3 == 0 else 3 * P
                    act.wait_ge(nm_ready, l * STEPS + i + 1)
                    c = 8 + 8 * (i % 2)
                    for m in range(maps):
                        ins = A(exps[:, i % 2, m, 0:n], bank[2 + m][:, 0:n], ACT.Exp,
                                scale=DAD ** -0.5 if i < 12 else QKW ** -0.5,
                                bias=small[:, c + 2 + m:c + 3 + m], accum_out=small[:, c + 4 + m:c + 5 + m])
                    ins.then_inc(exp_done, 1)
                    if i < PREP_GATES:
                        act.wait_ge(gate_ready, l * U_GATE + i + 1)
                        A(gates[i], gates[i], ACT.Tanh, scale=0.5)
                    if i == 13:
                        logs()
                        rstds([(wide[:, 2 + b, :], bank[(6, 3)[b]][:, 0:TOK], HD, subrs, (subss, l * 2 + b + 1))
                               for b in range(2)])
                        tanhs()
                    gate(PREP_GATES + i)
                    if i == 12:
                        act.wait_ge(av_out, FROM + l * 6 + 3)
                        act.wait_ge(br_gap, l + 1)
                        A(wide[:, 0:2, :], br[:, 2:4, :], ACT.Square).then_inc(subsq, 1)
                turn_out(STEPS - 1)
                act.wait_ge(unit_done, FROM + l * UNITS + B0)
                act.wait_ge(av_out, FROM + (l + 1) * 6)
                split_branch(6)
                split_branch(7)
                for d in range(KD + 1):
                    if d < KD:
                        split(B0 + d + 2)
                    if d >= 1:
                        act.wait_ge(merged_ready, l * KD + d)
                        A(mhi[:, d - 1, :], msum[:, (d - 1) % 2, :], ACT.Copy, scale=0.5).then_inc(mrg_hi, 1)
                for d in range(KD):
                    split(O0 + d + 2)
                    if d in (3, 5, 7):
                        act.wait_ge(x1_ready, FROM + l * KD + d - 1)
                        square(d - 3)
                logs()
                act.wait_ge(x1_ready, FROM + l * KD + KD)
                square(KD - 2)
                norm(1)
                with act.Fori(0, FB // 2) as i:
                    own.begin(i, 0)
                    for j in range(2):
                        u = P0 + 2 * j
                        p = l * FB + i * 2 + j
                        f = ftmp[:, j]
                        split(u + 3, i)
                        act.wait_ge(unit_done, FROM + l * UNITS + i * SLOTS + u + 2)
                        act.wait_ge(mlp_lo, FROM + l * FB + i * 2 + j)
                        for m in range(2):
                            col = i * 4 + 2 * j + m
                            A(f[:, m, :], bank[2 * j + m][:, 0:TOK], ACT.Identity,
                              scale=par[:, bass.ds(PCOL["conv_w"][0] + 2 * FB + col, 1)],
                              bias=par[:, bass.ds(PCOL["conv_b"][0] + col, 1)]).then_inc(tap1, 1)
                        act.wait_ge(conv_g, FROM + p + 2)
                        A(f[:, 2, :], f[:, 0, :], ACT.Tanh, scale=0.5).then_inc(mlp_tanh, 1)
                        split(u + 4, i)
                        act.wait_ge(mlp_full, p + 1)
                        A(ghi[:, bass.ds(i * 2 + j, 1), :].rearrange("p a t -> p (a t)"), f[:, 3, :],
                          ACT.Copy).then_inc(mlp_hi, 1)
                    own.end(FB // 2)
                for u in range(3, U_DN + 1):
                    if u < U_DN:
                        split(D0 + u)
                    if u in (10, 16, 22, 24):
                        k = 2 * ((u - 9) // 5) if u < U_DN else KD - 2
                        act.wait_ge(x2_ready, FROM + l * KD + k + 2)
                        square(k)
                assert own.n == ACT_OWN, own.n

        @block.vector
        def _(dve):
            V = nc.vector
            setup = sem("setup")
            V.memset(conds_t[:, :], 0.0).then_inc(setup, 1)
            dve.wait_ge(cond_exp, 1)
            V.tensor_scalar(condx, condx, 1.0, None, ALU.add).then_inc(setup, 1)
            dve.wait_ge(setup, 2)
            V.reciprocal(condx, condx).then_inc(setup, 1)
            dve.wait_ge(setup, 3)
            V.tensor_tensor(conds[:, :, 0:2], condx, cond_t[:, :].rearrange("p (k c) -> p k c", c=2), ALU.mult).then_inc(cond_ready, 1)
            for s in (unit_done, x1_ready, x2_ready, av_done, av_out, turned_out, mla_roped, da_roped, gated_ready,
                      mod_read):
                V.sem_inc(s, FROM)
            for s in (conv_g, conv_v, mlp_lo):
                V.sem_inc(s, FROM + 1)
            turned_mod = blocks(rt_t, STRIP)

            own = Links(dve, dve_own, DVE_OWN)
            with dve.Fori(0, DEPTH) as l:
                own.layer = l
                own.n = 0

                def split(u, i=0):
                    s = u % SLOTS
                    dve.wait_ge(hi_ready, l * UNITS + i * SLOTS + u + 1)
                    V.tensor_tensor(wlo[s][:, :], raw[s][:, :], whi[s][:, :].bitcast(F32), ALU.subtract).then_inc(lo_ready, 1)

                def low(out, full, high):
                    return V.tensor_tensor(out, full, high.bitcast(F32), ALU.subtract)

                def modulation(g, k0, k1, c0=0):
                    w = (k1 - k0) * STRIP
                    dve.wait_ge(ada_done, l * ADA + (HEAD, ADA_M, ADA_S, ADA_E)[g])
                    own.wait()
                    V.transpose(rt_t[:, 0:w], bank[7][:, c0:c0 + w]).then_inc(mod_read, 1)
                    dve.wait_ge(mod_read, FROM + 4 * l + g + 1)
                    own(V.tensor_tensor(mod[:, k0:k1, :], turned_mod[:, 0:k1 - k0, 0:2],
                                        pc("b_ada", k0, k1).unsqueeze(2).to_broadcast([P, k1 - k0, 2]), ALU.add))

                def scales(out, k0, gain):
                    own.wait()
                    own(V.scalar_tensor_tensor(out, mod[:, k0:k0 + KD, :], 1.0,
                                               pc(gain).unsqueeze(2).to_broadcast([P, KD, 2]), ALU.add, ALU.mult))

                def norm(n):
                    scale, shift = (sc1, mod[:, 0:8, :]) if n == 0 else (sc2, mod[:, 24:32, :])
                    if n == 0:
                        split(0)
                        split(1)
                        dve.wait_ge(head_par_loaded, 16 * l + 16)
                        modulation(0, 0, 16)
                        scales(sc1, 8, "g1")
                    for t in (ahi, alo):
                        own(V.memset(t[:, :, CTX:L0].bitcast(F32), 0.0))
                    own.wait()
                    dve.wait_ge(rstd_ready, l * 2 + n + 1)
                    for k in range(KD + 1):
                        if k < KD:
                            for a, b, c in RANGES:
                                ins = V.scalar_tensor_tensor(wide[:, k, a:b], x[:, k, a:b], scale[:, k, c:c + 1],
                                                             rsn[:, a:b], ALU.mult, ALU.mult)
                            ins.then_inc(norm_full, 1)
                        if k >= 1:
                            dve.wait_ge(norm_hi, (l * 2 + n) * KD + k)
                            for a, b, c in RANGES:
                                ins = V.scalar_tensor_tensor(alo[:, k - 1, a:b], wide[:, k - 1, a:b], shift[:, k - 1, c:c + 1],
                                                             ahi[:, k - 1, a:b].bitcast(F32), ALU.add, ALU.subtract)
                            ins.then_inc(norm_lo, 1)

                norm(0)
                V.memset(br[:, :, CTX:L0], 0.0).then_inc(br_gap, 1)
                lam = pc("lam").rearrange("p (a b d) -> p a b d", a=2, b=2)
                lp = lamp_t[:, :].rearrange("p (a d) -> p a d", a=2)
                dve.wait_ge(par_loaded, 32 * l + 32)
                own(V.tensor_tensor(lp, lam[:, :, 0, :], lam[:, :, 1, :], ALU.mult))
                own.wait()
                V.reduce_sum(small[:, 4:6], lp, AX).then_inc(lam_prod, 1)
                dve.wait_ge(lam_exp, l + 1)
                own(V.tensor_tensor(small[:, 1:2], small[:, 7:8], small[:, 6:7], ALU.subtract))
                own.wait()
                own(V.tensor_tensor(NEGLAM, NEGLAM, pc("lam_init"), ALU.subtract))
                own(V.tensor_tensor(GSUB, pc("subln"), pc("one_minus_init"), ALU.mult))
                for u in range(U_MIX):
                    split(u + 2)

                for i, (name, gain) in enumerate((("q0", "qn"), ("q1", "qn"), ("k0", "kn"), ("k1", "kn"))):
                    dve.wait_ge(prs, l * 6 + i + 1)
                    r = pj[:, PJ[name], :]
                    V.scalar_tensor_tensor(r, r, pc(gain), rs_t[:, i * TOK:(i + 1) * TOK], ALU.mult, ALU.mult).then_inc(da_normed, 1)
                dve.wait_ge(prs, l * 6 + 5)
                r = pj[:, PJ["cq"], :]
                own(V.scalar_tensor_tensor(r, r, pc("qa_a"), rs_t[:, 4 * TOK:5 * TOK], ALU.mult, ALU.mult))
                r = pj[0:NOPE, PJ["cqr"], :]
                own(V.scalar_tensor_tensor(r, r, pc("qa_b", p1=NOPE), rs_t[0:NOPE, 4 * TOK:5 * TOK], ALU.mult, ALU.mult))
                dve.wait_ge(prs, l * 6 + 6)
                own.wait()
                r = pj[:, PJ["ckv"], :]
                V.scalar_tensor_tensor(r, r, pc("kvn"), z_t[:, 0:TOK], ALU.mult, ALU.mult).then_inc(ckv_normed, 1)
                split(G0 + 2)
                split(G0 + 3)
                for i, (n0, n1) in enumerate((("q0", "q1"), ("k0", "k1"))):
                    dve.wait_ge(rot_done, l * 2 + i + 1)
                    dve.wait_ge(da_normed, l * 4 + 2 * i + 2)
                    dve.wait_ge(da_roped, FROM + l * 2 + i)
                    xs = pj[:, PJ[n0]:PJ[n1] + 1, L0:TOK]
                    tmp = rt_t[:, :].rearrange("p (b t) -> p b t", b=2)
                    own(V.tensor_tensor(tmp, bank[2 + i][:, :].rearrange("p (b t) -> p b t", b=2),
                                        cc("sin").unsqueeze(1).to_broadcast([P, 2, LAT]), ALU.mult))
                    own(V.tensor_tensor(xs, xs, cc("cos").unsqueeze(1).to_broadcast([P, 2, LAT]), ALU.mult))
                    own.wait()
                    V.tensor_tensor(xs, xs, tmp, ALU.add).then_inc(da_roped, 1)
                split(G0 + 4)
                dve.wait_ge(mix_out, (l + 1) * U_MIX)
                src = pj[NOPE:QKW, PJ["cqr"], :].unsqueeze(1).to_broadcast([ROPE, HEADS, TOK])
                V.tensor_copy(km[NOPE:QKW, :, :], src).then_inc(kr_copied, 1)
                src = ca[NOPE:QKW, HC - PAST:HC].unsqueeze(1).to_broadcast([ROPE, HEADS, PAST])
                V.tensor_copy(kmp[NOPE:QKW, :, :], src).then_inc(kr_copied, 1)
                for h in range(HEADS):
                    dve.wait_ge(uqrs, l * HEADS + h + 1)
                    V.scalar_tensor_tensor(qm[0:QKW, h, :], qm[0:QKW, h, :], pc("mqn", p1=QKW), rs[0:QKW, h, 0:TOK],
                                           ALU.mult, ALU.mult).then_inc(uq_normed, 1)
                split(G0 + 5)
                dve.wait_ge(uk_done, l * 5 + 1)
                V.tensor_copy(kmp[0:NOPE, :, :], bank[2][0:NOPE, :].rearrange("p (h t) -> p h t", h=HEADS)).then_inc(uk_out, 1)
                for h in range(HEADS):
                    dve.wait_ge(uk_done, l * 5 + h + 2)
                    V.tensor_copy(km[0:NOPE, h, :], bank[4 + h][0:NOPE, 0:TOK]).then_inc(uk_out, 1)
                split(G0 + 6)
                for h in range(HEADS):
                    dve.wait_ge(ukrs, l * 5 + h + 1)
                    V.scalar_tensor_tensor(km[0:QKW, h, :], km[0:QKW, h, :], pc("mkn", p1=QKW),
                                           rs_t[0:QKW, h * TOK:(h + 1) * TOK], ALU.mult, ALU.mult).then_inc(uk_normed, 1)
                dve.wait_ge(ukrs, l * 5 + 5)
                V.scalar_tensor_tensor(kmp_t[0:QKW, :], kmp_t[0:QKW, :], pc("mkn", p1=QKW),
                                       rs_t[0:QKW, 4 * TOK:4 * TOK + 512], ALU.mult, ALU.mult).then_inc(uk_normed, 1)
                split(G0 + 7)
                split(G0 + 8)
                split(G0 + 9)

                def attention_out(i):
                    n, c0 = (2 if i < 12 else 6), TILES[(i // 4) % 3]
                    dve.wait_ge(av_done, FROM + l * STEPS + i + 1)
                    V.tensor_copy(br[:, n:n + 2, c0:c0 + P],
                                  bank[5][:, 0:2 * P].rearrange("p (b t) -> p b t", b=2)).then_inc(av_out, 1)

                def rope(i):
                    t, h = (qm, km)[i // 2], 2 * (i % 2)
                    dve.wait_ge(mrot_done, l * 4 + i + 1)
                    if i == 0:
                        dve.wait_ge(uq_normed, (l + 1) * HEADS)
                        dve.wait_ge(uk_normed, (l + 1) * 5)
                    xs = t[NOPE:QKW, h:h + 2, L0:TOK]
                    dve.wait_ge(mla_roped, FROM + l * 4 + i)
                    tmp = rt_t[NOPE:QKW, :].rearrange("p (b t) -> p b t", b=2)
                    own(V.tensor_tensor(tmp, bank[6][NOPE:QKW, :].rearrange("p (b t) -> p b t", b=2),
                                        cc("sin", NOPE, QKW).unsqueeze(1).to_broadcast([ROPE, 2, LAT]), ALU.mult))
                    own(V.tensor_tensor(xs, xs, cc("cos", NOPE, QKW).unsqueeze(1).to_broadcast([ROPE, 2, LAT]), ALU.mult))
                    own.wait()
                    V.tensor_tensor(xs, xs, tmp, ALU.add).then_inc(mla_roped, 1)

                def low_branch(n):
                    b = SPLIT_ORDER[n]
                    dve.wait_ge(br_hi, l * 8 + n + 1)
                    low(brl[:, b, :], br[:, b, :], branch_hi[b]).then_inc(br_lo, 1)

                for i in range(STEPS):
                    split(G0 + PREP_GATES + i + 2)
                    maps = 2 if i < 12 else 1
                    n = P if (i // 4) % 3 == 0 else 3 * P
                    scale = DAD ** -0.5 if i < 12 else QKW ** -0.5
                    c = 8 + 8 * (i % 2)
                    mx, nm, su, ri = (small[:, c + 2 * q:c + 2 * q + maps] for q in range(4))
                    dve.wait_ge(scores_done, l * STEPS + i + 1)
                    for m in range(maps):
                        own(V.reduce_max(small[:, c + m:c + m + 1], bank[2 + m][:, 0:n], AX))
                    own.wait()
                    V.tensor_scalar(nm, mx, -scale, None, ALU.mult).then_inc(nm_ready, 1)
                    dve.wait_ge(exp_done, l * STEPS + i + 1)
                    own(V.reciprocal(ri, su))
                    own.wait()
                    a0 = exps[:, i % 2, 0, 0:n]
                    if maps == 2:
                        own(V.tensor_tensor(ri[:, 1:2], ri[:, 1:2], NEGLAM, ALU.mult))
                        own(V.tensor_scalar(a0, a0, ri[:, 0:1], None, ALU.mult))
                        own.wait()
                        V.scalar_tensor_tensor(a0, exps[:, i % 2, 1, 0:n], ri[:, 1:2], a0, ALU.mult, ALU.add).then_inc(probs_ready, 1)
                    else:
                        V.tensor_scalar(a0, a0, ri[:, 0:1], None, ALU.mult).then_inc(probs_ready, 1)
                    if i == 15:
                        dve.wait_ge(av_out, FROM + l * 6 + 3)
                        for b in range(2):
                            dve.wait_ge(subrs, l * 2 + b + 1)
                            r = br[:, 2 + b, :]
                            V.scalar_tensor_tensor(r, r, GSUB, wide[:, 2 + b, :], ALU.mult, ALU.mult).then_inc(sub_out, 1)
                    if i >= 1 and (i - 1) % 4 == 3:
                        attention_out(i - 1)
                    if i == 12:
                        modulation(1, 16, 32)
                    if 3 <= i < 7:
                        low_branch(i - 3)
                    if i in ROPE_STEPS:
                        rope(ROPE_STEPS.index(i))
                    if i in (18, 19):
                        low_branch(i - 14)
                attention_out(STEPS - 1)
                modulation(2, 32, 40)
                scales(sc2, 32, "g2")
                low_branch(6)
                low_branch(7)

                def merged_low(d):
                    dve.wait_ge(mrg_hi, l * KD + d + 1)
                    V.scalar_tensor_tensor(mlo[:, d, :], msum[:, d % 2, :], 0.5, mhi[:, d, :].bitcast(F32),
                                           ALU.mult, ALU.subtract).then_inc(mrg_lo, 1)

                for d in range(KD):
                    for n in range(4):
                        if n < 3:
                            dve.wait_ge(br_done, (l * KD + d) * 3 + n + 1)
                        else:
                            dve.wait_ge(unit_done, FROM + l * UNITS + B0 + d + 1)
                        if d >= 2:
                            dve.wait_ge(merged_ready, l * KD + d - 1)
                        V.scalar_tensor_tensor(gated[:, d % 2, n, :], gates[n * KD + d], 1.0,
                                               bank[branch_bank[d][n]][:, 0:TOK],
                                               ALU.add, ALU.mult).then_inc(gated_ready, 1)
                    split(B0 + d + 2)
                    if d >= 1:
                        merged_low(d - 1)
                merged_low(KD - 1)

                def residual(d, b, gate0, done):
                    for a, e, c in RANGES:
                        ins = V.scalar_tensor_tensor(x[:, d, a:e], bank[b][:, a:e], mod[:, gate0 + d, c:c + 1], x[:, d, a:e],
                                                     ALU.mult, ALU.add)
                    ins.then_inc(done, 1)

                for d in range(KD):
                    split(O0 + d + 2)
                    dve.wait_ge(unit_done, FROM + l * UNITS + O0 + d + 1)
                    residual(d, d % 4, 16, x1_ready)
                split(P0 + 2)
                norm(1)
                modulation(3, 40, 48, 256)
                PAIR = 3
                with dve.Fori(0, FB // 2) as i:
                    own.begin(i, 2 * PAIR)
                    for j in range(2):
                        u = P0 + 2 * j
                        p = l * FB + i * 2 + j
                        f = ftmp[:, j]
                        split(u + 3, i)
                        for m in range(2):
                            dve.wait_ge(tap1, 2 * p + m + 1)
                            b = bank[2 * j + m]
                            col = i * 4 + 2 * j + m + PCOL["conv_w"][0]
                            own(V.scalar_tensor_tensor(f[:, m, 1:TOK], b[:, 0:TOK - 1], par[:, bass.ds(col, 1)],
                                                       f[:, m, 1:TOK], ALU.mult, ALU.add))
                            own.wait()
                            V.scalar_tensor_tensor(f[:, m, 0:TOK - 1], b[:, 1:TOK], par[:, bass.ds(col + 4 * FB, 1)],
                                                   f[:, m, 0:TOK - 1], ALU.mult, ALU.add).then_inc((conv_g, conv_v)[m], 1)
                        dve.wait_ge(mlp_tanh, p + 1)
                        own(V.scalar_tensor_tensor(f[:, 2, :], f[:, 2, :], 1.0, f[:, 0, :], ALU.add, ALU.mult))
                        own.wait()
                        dve.wait_ge(conv_v, FROM + p + 2)
                        V.scalar_tensor_tensor(f[:, 3, :], f[:, 2, :], 0.5, f[:, 1, :], ALU.mult, ALU.mult).then_inc(mlp_full, 1)
                        split(u + 4, i)
                        dve.wait_ge(mlp_hi, p + 1)
                        low(glo[:, bass.ds(i * 2 + j, 1), :].rearrange("p a t -> p (a t)"), f[:, 3, :],
                            ghi[:, bass.ds(i * 2 + j, 1), :].rearrange("p a t -> p (a t)")).then_inc(mlp_lo, 1)
                    own.end(FB // 2)
                for d in range(KD):
                    for u in range(3 * d, 3 * d + 3):
                        if u + 3 < U_DN:
                            split(D0 + u + 3)
                    dve.wait_ge(unit_done, FROM + l * UNITS + D0 + 3 * d + 3)
                    residual(d, d % 4, 40, x2_ready)
                assert own.n == DVE_OWN, own.n

        @block.tensor
        def _(pe):
            T = nc.tensor

            def modulate(w, a):
                if a < ADA_M:
                    n, c0, k, strips = 512, 0, a % 16 // 2, (2 * (a % 2), 2 * (a % 2) + 1)
                else:
                    n, c0, k, strips = 256, 256 * (a >= ADA_S), a % 8, range(4)
                for q, strip in enumerate(strips):
                    p0 = STRIP * strip
                    ins = T.matmul(bank[7][p0:p0 + STRIP, c0:c0 + n], conds[:, k, :], w[:, q * n:(q + 1) * n],
                                   start=k == 0, stop=k == KD - 1)
                ins.then_inc(ada_done, 1)

            pe.wait_ge(cond_ready, 1)
            pe.wait_ge(ones_loaded, 16)
            with pe.Fori(0, DEPTH) as l:
                def unit_ready(u, i=0):
                    pe.wait_ge(hi_ready, l * UNITS + i * SLOTS + u + 1)
                    pe.wait_ge(lo_ready, l * UNITS + i * SLOTS + u + 1)

                def dense(out, u, ws, hi, lo, first=True, last=True):
                    s = u % SLOTS
                    n = len(ws)
                    for k, w in enumerate(ws):
                        T.matmul(out, wb[s][0][:, w, :], hi[k], start=first and k == 0, stop=False)
                        T.matmul(out, wb[s][0][:, w, :], lo[k], start=False, stop=False)
                        ins = T.matmul(out, wb[s][1][:, w, :], hi[k], start=False, stop=last and k == n - 1)
                    return ins

                HI = [ahi[:, k, :] for k in range(KD)]
                LO = [alo[:, k, :] for k in range(KD)]

                def pair(u, b, hi, lo, wait):
                    unit_ready(u)
                    unit_ready(u + 1)
                    for k in range(KD):
                        wait(k)
                        for q in range(2):
                            ins = dense(bank[b + q][:, 0:TOK], u + q, [k], hi[k:k + 1], lo[k:k + 1], k == 0, k == KD - 1)
                            if k == KD - 1:
                                ins.then_inc(unit_done, 1)

                def ada_units(a0, a1):
                    for a in range(a0, a1):
                        pe.wait_ge(ada_loaded[a % 2], 16 * (l * ((ADA - HEAD) // 2) + (a - HEAD) // 2 + 1))
                        modulate(ada[a % 2], a)

                def square_sums(n):
                    for k in range(KD):
                        if k % 2 == 0:
                            pe.wait_ge(sq_ready, (l * 2 + n) * 4 + k // 2 + 1)
                        ins = T.matmul(bank[4][:, 0:TOK], cc("ones"), wide[:, k, :], start=k == 0, stop=k == KD - 1)
                    ins.then_inc(ss_done, 1)

                pe.wait_ge(mod_read, FROM + 4 * l)
                for n, (a0, a1) in enumerate(HEAD_PARTS):
                    pe.wait_ge(head_loaded[n], (l + 1) * 16 * (a1 - a0))
                    for a in range(a0, a1):
                        modulate(head[a], a)
                    if n == 0:
                        square_sums(0)
                pair(0, 0, HI, LO, lambda k: pe.wait_ge(norm_lo, l * 2 * KD + k + 1))
                for u in range(2, U_MIX):
                    unit_ready(u)
                    pe.wait_ge(mix_out, l * U_MIX + u - 1)
                    name = MIX[u]
                    if name in PJ:
                        ins = dense(bank[u % 2][:, 0:TOK], u, range(KD), HI, LO)
                    else:
                        s = u % SLOTS
                        for t, c0 in enumerate(TILES):
                            out = bank[u % 2][:, t * P:(t + 1) * P]
                            for k in range(KD):
                                h, lw = ahi[:, k, c0:c0 + P], alo[:, k, c0:c0 + P]
                                T.matmul(out, h, wb[s][0][:, k, :], start=k == 0, stop=False)
                                T.matmul(out, h, wb[s][1][:, k, :], start=False, stop=False)
                                ins = T.matmul(out, lw, wb[s][0][:, k, :], start=False, stop=k == KD - 1)
                    ins.then_inc(unit_done, 1)

                def gate(g):
                    u = G0 + g
                    unit_ready(u)
                    if g < 2:
                        pe.wait_ge(mix_out, (l + 1) * U_MIX)
                    else:
                        pe.wait_ge(gate_ready, l * U_GATE + g - 1)
                    dense(bank[u % 2][:, 0:TOK], u, range(KD), HI, LO).then_inc(unit_done, 1)

                pe.wait_ge(consts_loaded, 16)
                for i in range(4):
                    pe.wait_ge(psq, l * 7 + i + 1)
                    T.matmul(bank[2 + i][:, 0:TOK], cc("ones32"), wide[:, i, :], start=True, stop=True).then_inc(pss, 1)
                pe.wait_ge(psq, l * 7 + 6)
                T.matmul(bank[6][:, 0:TOK], cc("ones"), wide[:, 4, :], start=True, stop=False)
                T.matmul(bank[6][:, 0:TOK], cc("ones", 0, NOPE), wide[0:NOPE, 5, :], start=False, stop=True).then_inc(pss, 1)
                pe.wait_ge(psq, l * 7 + 7)
                pe.wait_ge(mod_read, FROM + 4 * l + 1)
                T.matmul(bank[7][:, 0:TOK], cc("ones"), wide[:, 6, :], start=True, stop=True).then_inc(pss, 1)
                gate(0)
                pe.wait_ge(prs, (l + 1) * 6)
                for i, (n0, n1) in enumerate((("q0", "q1"), ("k0", "k1"))):
                    pe.wait_ge(da_normed, l * 4 + 2 * i + 2)
                    T.matmul(bank[2 + i][:, :].rearrange("p (b t) -> p b t", b=2), cc("rot"),
                             pj[:, PJ[n0]:PJ[n1] + 1, L0:TOK], start=True, stop=True).then_inc(rot_done, 1)
                pe.wait_ge(ckv_normed, l + 1)
                for h in range(HEADS):
                    out = bank[4 + h][0:QKW, 0:TOK]
                    T.matmul(out, pc("w_uq_a", h * QKW, (h + 1) * QKW), pj[:, PJ["cq"], :], start=True, stop=False)
                    T.matmul(out, pc("w_uq_b", h * QKW, (h + 1) * QKW, 0, NOPE), pj[0:NOPE, PJ["cqr"], :],
                             start=False, stop=True).then_inc(uq_done, 1)
                gate(1)
                pe.wait_ge(uqsq, l + 1)
                for h in range(HEADS):
                    T.matmul(bank[4 + h][0:QKW, 0:TOK], cc("ones", 0, QKW, 0, QKW), wide[0:QKW, h, :],
                             start=True, stop=True).then_inc(uqss, 1)
                gate(2)
                wk = pc("w_ukv").rearrange("p (h c) -> p h c", h=HEADS)
                pe.wait_ge(da_roped, FROM + (l + 1) * 2)
                for h in range(HEADS):
                    ins = T.matmul(bank[2][0:NOPE, h * PAST:(h + 1) * PAST], wk[:, h, 0:NOPE], ca[:, 512:512 + PAST],
                                   start=True, stop=True)
                ins.then_inc(uk_done, 1)
                pe.wait_ge(uqrs, (l + 1) * HEADS)
                for h in range(HEADS):
                    T.matmul(bank[4 + h][0:NOPE, 0:TOK], wk[:, h, 0:NOPE], pj[:, PJ["ckv"], :],
                             start=True, stop=True).then_inc(uk_done, 1)

                def latent_values(t):
                    src = ca[:, 512:512 + PAST] if t == 3 else pj[:, PJ["ckv"], TILES[t]:TILES[t] + P]
                    return T.matmul(bank[3][:, (t % 2) * 256:(t % 2) * 256 + 256].rearrange("p (h c) -> p h c", h=HEADS),
                                    src, wk[:, :, NOPE:], start=True, stop=True)

                latent_values(0)
                latent_values(1).then_inc(vm_done, 1)
                gate(3)
                pe.wait_ge(uksq, (l + 1) * 2)
                pe.wait_ge(uk_out, (l + 1) * 5)
                for h in range(HEADS):
                    T.matmul(bank[4 + h][0:QKW, 0:TOK], cc("ones", 0, QKW, 0, QKW), wide[0:QKW, h, :],
                             start=True, stop=True).then_inc(ukss, 1)
                T.matmul(bank[2][0:QKW, :], cc("ones", 0, QKW, 0, QKW), wide_t[0:QKW, 4 * TOK:4 * TOK + 512],
                         start=True, stop=True).then_inc(ukss, 1)
                pe.wait_ge(vm_out, l * 2 + 1)
                latent_values(2)
                latent_values(3).then_inc(vm_done, 1)
                gate(4)
                gate(5)
                pe.wait_ge(vm_out, (l + 1) * 2)
                pe.wait_ge(ukrs, (l + 1) * 5)
                for t, c0 in enumerate(TILES):
                    for b in range(2):
                        c = (t % 2) * 2 * P + b * P
                        ins = T.matmul(bank[2 + t // 2][:, c:c + P], pj[:, PJ["xa0"] + b, c0:c0 + P],
                                       pc("pool_w", b * P, (b + 1) * P), start=True, stop=True)
                    if t >= 1:
                        ins.then_inc(tm1_done, 1)
                for t, c0 in enumerate(TILES):
                    for b in range(2):
                        ins = T.matmul(bank[4 + t][:, b * 2 * P:(b + 1) * 2 * P], pj[:, PJ["xc0"] + b, c0:c0 + P], cc("dft"),
                                       start=True, stop=True)
                    ins.then_inc(tm1_done, 1)
                gate(6)
                pe.wait_ge(tm1_out, (l + 1) * 5)
                pe.wait_ge(tc_loaded, (l + 1) * 16)
                for b in range(2):
                    for g in (2 * b, 2 * b + 1):
                        r = HD * (g % 2)
                        T.matmul(bank[2 + b][r:r + HD, 0:CTX], zz[:, 0, g * HD:(g + 1) * HD],
                                 tc[:, TP_C + g * CTX:TP_C + (g + 1) * CTX], start=True, stop=True)
                        for t in range(2):
                            c = TP_L + (g * 2 + t) * LAT
                            ins = T.matmul(bank[2 + b][r:r + HD, L0:TOK], zz[:, 1 + t, g * HD:(g + 1) * HD],
                                           tc[:, c:c + LAT], start=t == 0, stop=t == 1)
                    ins.then_inc(tm2_done, 1)
                for b in range(2):
                    for q in range(2):
                        T.matmul(bank[4 + b][:, 0:CTX], fa[:, 0, (2 * b + q) * P:(2 * b + q + 1) * P],
                                 tc[:, TF_C + q * CTX:TF_C + (q + 1) * CTX], start=q == 0, stop=q == 1)
                    for t in range(2):
                        for q in range(2):
                            c = TF_L + (q * 2 + t) * LAT
                            ins = T.matmul(bank[4 + b][:, L0:TOK], fa[:, 1 + t, (2 * b + q) * P:(2 * b + q + 1) * P],
                                           tc[:, c:c + LAT], start=t == 0 and q == 0, stop=t == 1 and q == 1)
                    ins.then_inc(tm2_done, 1)
                gate(7)

                pe.wait_ge(tm2_out, (l + 1) * 4)

                def scores(i):
                    qt, h = (i // 4) % 3, i % 4
                    q0 = TILES[qt]
                    if i >= 1:
                        pe.wait_ge(exp_done, l * STEPS + i)
                    maps = 2 if i < 12 else 1
                    for m in range(maps):
                        if i < 12:
                            p0, b = (h % 2) * HD + m * DAD, h // 2
                            q = pj[p0:p0 + DAD, PJ["q0"] + b, q0:q0 + P]
                            k_self, k_past = pj[p0:p0 + DAD, PJ["k0"] + b, :], ca[p0:p0 + DAD, b * PAST:(b + 1) * PAST]
                        else:
                            q = qm[0:QKW, h, q0:q0 + P]
                            k_self, k_past = km[0:QKW, h, :], kmp[0:QKW, h, :]
                        out = bank[2 + m]
                        if qt == 0:
                            ins = T.matmul(out[:, 0:P], q, k_self[:, 0:CTX], start=True, stop=True)
                        else:
                            T.matmul(out[:, 0:LAT], q, k_self[:, L0:TOK], start=True, stop=True)
                            ins = T.matmul(out[:, LAT:LAT + PAST], q, k_past, start=True, stop=True)
                    ins.then_inc(scores_done, 1)

                def turn(i):
                    pe.wait_ge(probs_ready, l * STEPS + i + 1)
                    pe.wait_ge(turned_out, FROM + l * STEPS + i)
                    n = 1 if (i // 4) % 3 == 0 else 3
                    for k in range(n):
                        ins = T.transpose(bank[4][:, k * P:(k + 1) * P], exps[:, i % 2, 0, k * P:(k + 1) * P], cc("ident"))
                    ins.then_inc(turned, 1)

                def weigh(i):
                    qt, h = (i // 4) % 3, i % 4
                    pe.wait_ge(turned_out, FROM + l * STEPS + i + 1)
                    if h == 0:
                        pe.wait_ge(av_out, FROM + l * 6 + i // 4)
                    out = bank[5][(h % 2) * HD:(h % 2) * HD + HD, (h // 2) * P:(h // 2) * P + P]
                    hs = slice(h * HD, (h + 1) * HD)
                    if i < 12:
                        vs = [val[:, 0, hs]] if qt == 0 else [val[:, 1, hs], val[:, 2, hs], ca[:, 256 + h * HD:256 + (h + 1) * HD]]
                    else:
                        vs = [vm[:, 0, hs]] if qt == 0 else [vm[:, 1, hs], vm[:, 2, hs], vm[:, 3, hs]]
                    for k, v in enumerate(vs):
                        ins = T.matmul(out, v, pt[:, k, :], start=k == 0, stop=k == len(vs) - 1)
                    ins.then_inc(av_done, 1)

                def rotate(i):
                    t, h = (qm, km)[i // 2], 2 * (i % 2)
                    pe.wait_ge(uk_normed, (l + 1) * 5)
                    pe.wait_ge(mla_roped, FROM + l * 4 + i)
                    T.matmul(bank[6][NOPE:QKW, :].rearrange("p (b t) -> p b t", b=2), cc("rot", 0, QKW, NOPE, QKW),
                             t[0:QKW, h:h + 2, L0:TOK], start=True, stop=True).then_inc(mrot_done, 1)

                for i in range(STEPS):
                    if i >= 1:
                        turn(i - 1)
                    if i == 12:
                        pe.wait_ge(mla_roped, FROM + (l + 1) * 4)
                    scores(i)
                    if i + 1 in ROPE_STEPS:
                        rotate(ROPE_STEPS.index(i + 1))
                    if i == 13:
                        pe.wait_ge(subsq, l + 1)
                        for b in range(2):
                            T.matmul(bank[(6, 3)[b]][:, 0:TOK], cc("ones64"), wide[:, b, :], start=True, stop=True).then_inc(subss, 1)
                    gate(PREP_GATES + i)
                    if i >= 1:
                        weigh(i - 1)
                    if i == 13:
                        pe.wait_ge(mod_read, FROM + 4 * l + 2)
                    ada_units(HEAD + sum(ADA_STEP[:i]), HEAD + sum(ADA_STEP[:i + 1]))
                ada_units(HEAD + sum(ADA_STEP), HEAD + sum(ADA_STEP) + ADA_TAIL)
                turn(STEPS - 1)

                def branch(d, n):
                    use = 4 * d + n
                    if use >= 7:
                        pe.wait_ge(gated_ready, FROM + l * KD * 4 + use - 6)
                    else:
                        semaphore, count = ((gate_ready, (l + 1) * U_GATE), (gate_ready, (l + 1) * U_GATE),
                                            (exp_done, (l + 1) * STEPS), (exp_done, (l + 1) * STEPS),
                                            (turned_out, FROM + (l + 1) * STEPS), (av_out, FROM + (l + 1) * 6),
                                            (subrs, (l + 1) * 2))[use]
                        pe.wait_ge(semaphore, count)
                    pe.wait_ge(br_lo, l * 8 + (2, 6, 4, 8)[n])
                    ins = dense(bank[branch_bank[d][n]][:, 0:TOK], B0 + d, (2 * n, 2 * n + 1),
                                branch_hi[2 * n:2 * n + 2], [brl[:, 2 * n, :], brl[:, 2 * n + 1, :]])
                    ins.then_inc(br_done if n < 3 else unit_done, 1)

                unit_ready(B0)
                for n in range(3):
                    branch(0, n)
                weigh(STEPS - 1)
                branch(0, 3)
                for d in range(1, KD):
                    unit_ready(B0 + d)
                    for n in range(4):
                        branch(d, n)
                MH = [mhi[:, k, :] for k in range(KD)]
                ML = [mlo[:, k, :] for k in range(KD)]
                pair(O0, 0, MH, ML, lambda k: pe.wait_ge(mrg_lo, l * KD + k + 1))
                for d in range(2, KD):
                    unit_ready(O0 + d)
                    if d >= SLOTS:
                        pe.wait_ge(x1_ready, FROM + l * KD + d - SLOTS + 1)
                    dense(bank[d % 4][:, 0:TOK], O0 + d, range(KD), MH, ML).then_inc(unit_done, 1)
                square_sums(1)
                ada_units(HEAD + sum(ADA_STEP) + ADA_TAIL, ADA_E)
                pair(P0, 0, HI, LO, lambda k: pe.wait_ge(norm_lo, (l * 2 + 1) * KD + k + 1))
                for j in range(2, SLOTS):
                    unit_ready(P0 + j)
                    dense(bank[j][:, 0:TOK], P0 + j, range(KD), HI, LO).then_inc(unit_done, 1)
                with pe.Fori(0, U_UP // SLOTS - 1) as i:
                    for j in range(SLOTS):
                        unit_ready(P0 + SLOTS + j, i)
                        pe.wait_ge((conv_g, conv_v)[j % 2], FROM + l * FB + i * 2 + 2 + j // 2)
                        dense(bank[j][:, 0:TOK], P0 + j, range(KD), HI, LO).then_inc(unit_done, 1)
                with pe.Fori(0, 2) as i:
                    for d in range(4):
                        pe.wait_ge(x2_ready, FROM + l * KD + i * (d + 1))
                        for q in range(3):
                            u = D0 + 3 * d + q
                            unit_ready(u, i * 3)
                            k0 = q * KD
                            n = min(KD, FB - k0)
                            pe.wait_ge(mlp_lo, FROM + 1 + l * FB + k0 + n)
                            dense(bank[d][:, 0:TOK], u, range(n), [ghi[:, k0 + k, :] for k in range(n)],
                                  [glo[:, k0 + k, :] for k in range(n)], first=q == 0, last=q == 2).then_inc(unit_done, 1)


def _constants():
    import numpy as np
    f = np.float32
    cn = np.zeros((P, CW), f)

    def put(name, a):
        cn[:a.shape[0], CCOL[name][0]:CCOL[name][0] + a.shape[1]] = a

    put("ident", np.eye(P))
    put("ones", np.ones((P, P)))
    put("ones32", np.kron(np.eye(4), np.ones((32, 32))))
    put("ones64", np.kron(np.eye(2), np.ones((64, 64))))
    r = np.zeros((16, 16))
    for i in range(8):
        r[i, i + 8], r[i + 8, i] = -1, 1
    put("rot", np.kron(np.eye(8), r).T)
    j = np.arange(HD)
    ang = 2 * np.pi * np.outer(j, j) / HD
    put("dft", np.concatenate([np.kron(np.eye(2), np.cos(ang)), np.kron(np.eye(2), np.sin(ang))], 1))
    half = 8
    inv = (np.float32(10000.0) ** (-np.arange(half, dtype=f) / f(half))).astype(f)
    t = np.arange(LAT)
    for name, fn in (("cos", np.cos), ("sin", np.sin)):
        rows = fn((t // GRID_W).astype(f)[None, :] * inv[:, None])
        cols = fn((t % GRID_W).astype(f)[None, :] * inv[:, None])
        put(name, np.tile(np.concatenate([rows, rows, cols, cols]), (4, 1)))

    tc = np.zeros((P, TW), f)
    for n_tok, p0, f0 in ((CTX, TP_C, TF_C), (LAT, TP_L, TF_L)):
        tt = np.arange(n_tok)
        tiles = n_tok // P
        for g, w in enumerate(WINDOWS):
            lo, hi = np.clip(tt - w // 2, 0, n_tok), np.clip(tt + w // 2, 0, n_tok)
            m = ((tt[:, None] >= lo[None, :]) & (tt[:, None] < hi[None, :])) / (hi - lo)[None, :] - np.eye(n_tok)
            for k in range(tiles):
                c = p0 + (g * tiles + k) * n_tok
                tc[:, c:c + n_tok] = m[k * P:(k + 1) * P]
        ang = 2 * np.pi * (np.outer(tt, tt) % n_tok) / n_tok
        s = 1.0 / math.sqrt(n_tok * HD)
        for q, m in enumerate((np.cos(ang) * s, -np.sin(ang) * s)):
            for k in range(tiles):
                c = f0 + (q * tiles + k) * n_tok
                tc[:, c:c + n_tok] = m[k * P:(k + 1) * P]
    return cn, tc


def kernel(**inputs):
    import numpy as np
    import concourse.bacc as bacc
    from concourse.bass_utils import run_bass_kernel_spmd

    w = {k: np.asarray(v) for k, v in inputs.items()}
    f = np.float32

    def units(a, n):
        k = a.shape[0] // P
        return a.reshape(k, P, n, P).transpose(2, 1, 0, 3).reshape(n, P, k * P)

    stream = np.zeros((DEPTH * UNITS, P, UNIT), f)
    ada = np.zeros((DEPTH * ADA, P, UNIT), f)
    par = np.zeros((DEPTH, P, PW), f)
    cache = np.zeros((DEPTH, P, HC), f)
    for l in range(DEPTH):
        wi = w["w_in"][l]
        g, base = wi[:, :4 * D], 4 * D
        xa, qkv, xc, ml = np.split(wi[:, base:], [256, 256 + 768, 256 + 768 + 256], axis=1)
        last = np.zeros((D, P), f)
        last[:, 0:NOPE] = ml[:, P:QL]
        last[:, NOPE:QKW] = ml[:, QL + KVL:]
        mix = np.concatenate([xa, qkv, xc, ml[:, 0:P], ml[:, QL:QL + KVL], last], axis=1)
        s = stream[l * UNITS:(l + 1) * UNITS]
        s[0:G0] = units(mix, U_MIX)
        s[G0:B0] = units(g, U_GATE)
        s[B0:O0] = units(w["w_branch"][l].reshape(D, D), KD)
        s[O0:P0] = units(w["w_out"][l], KD)
        up = units(w["w_up"][l], 2 * FB)
        s[P0:D0:2], s[P0 + 1:D0:2] = up[:FB], up[FB:]
        dn = w["w_down"][l].reshape(FB, P, KD, P).transpose(2, 1, 0, 3)
        for q in range(3):
            part = dn[:, :, q * KD:(q + 1) * KD]
            s[D0 + q::3, :, 0:part.shape[2] * P] = part.reshape(KD, P, -1)
        m = w["w_ada"][l].reshape(KD, P, 3, 16, 2, 2, STRIP).transpose(2, 0, 4, 1, 5, 3, 6).reshape(3 * 16, P, UNIT)
        own = DEPTH * HEAD + l * (ADA - HEAD)
        ada[l * HEAD:(l + 1) * HEAD] = m[:HEAD]
        ada[own:own + 16] = m[HEAD:ADA_M]
        m = w["w_ada"][l][:, 4 * D:].reshape(KD, P, 2, 8, 4, STRIP).transpose(2, 0, 1, 4, 3, 5).reshape(16, P, UNIT)
        ada[own + 16:own + 32] = m

        def put(name, a):
            a = np.asarray(a)
            par[l, :a.shape[0], PCOL[name][0]:PCOL[name][0] + a.shape[1]] = a

        put("g1", w["g_norm1"][l].reshape(KD, P).T)
        put("g2", w["g_norm2"][l].reshape(KD, P).T)
        put("b_ada", w["b_ada"][l].reshape(ADA, P).T)
        put("conv_w", w["conv_w"][l].reshape(3, 2, FB, P).transpose(3, 0, 2, 1).reshape(P, -1))
        put("conv_b", w["conv_b"][l].reshape(2, FB, P).transpose(2, 1, 0).reshape(P, -1))
        put("pool_scale", w["pool_scale"][l].reshape(2, P).T)
        put("qn", np.tile(w["diff_qnorm"][l], 4)[:, None])
        put("kn", np.tile(w["diff_knorm"][l], 4)[:, None])
        put("subln", np.tile(w["diff_subln"][l], 2)[:, None])
        init = 0.8 - 0.6 * math.exp(-0.3 * l)
        put("lam_init", np.full((P, 1), init, f))
        put("one_minus_init", np.full((P, 1), 1.0 - init, f))
        put("lam", np.broadcast_to(w["diff_lambda"][l].reshape(1, -1), (P, 4 * DAD)))
        put("qa_a", w["mla_qa_norm"][l][0:P, None])
        put("qa_b", w["mla_qa_norm"][l][P:, None])
        put("kvn", w["mla_kv_norm"][l][:, None])
        put("mqn", w["mla_qnorm"][l][:, None])
        put("mkn", w["mla_knorm"][l][:, None])
        put("w_uq_a", w["w_uq"][l][0:P])
        put("w_uq_b", w["w_uq"][l][P:])
        put("w_ukv", w["w_ukv"][l])
        for b in range(2):
            for q in range(2):
                c = PCOL["pool_w"][0] + b * P + q * HD
                par[l, q * HD:(q + 1) * HD, c:c + HD] = w["pool_w"][l][2 * b + q]
        cache[l, :, 0:256] = w["cache_diff_k"][0, l].reshape(PAST, 2, P).transpose(2, 1, 0).reshape(P, 256)
        cache[l, :, 256:512] = w["cache_diff_v"][0, l].reshape(PAST, 256)
        cache[l, :, 512:640] = w["cache_mla_ckv"][0, l].T
        cache[l, NOPE:QKW, 640:768] = w["cache_mla_krope"][0, l].T

    x_in = np.zeros((P, KD, TOK), f)
    x_in[:, :, 0:CTX] = w["x_prompt"][0].reshape(CTX, KD, P).transpose(2, 1, 0)
    x_in[:, :, L0:] = w["x_sample"][0].reshape(LAT, KD, P).transpose(2, 1, 0)
    cond = np.stack([w["c_ctx"].reshape(KD, P).T, w["c"][0].reshape(KD, P).T], axis=2).reshape(P, 2 * KD)
    cn, tc = _constants()
    arrays = {"stream": stream, "ada_w": ada, "params": par, "caches": cache, "consts": cn, "time_consts": tc,
              "x_in": x_in.reshape(P, KD * TOK), "cond": np.ascontiguousarray(cond)}
    outs = {"y_out": (P, KD * TOK), "k_out": (DEPTH, P, 2 * CTX), "v_out": (DEPTH, CTX, 256),
            "ckv_out": (DEPTH, KVL, CTX), "krope_out": (DEPTH, ROPE, CTX)}
    nc = bacc.Bacc("TRN2", target_bir_lowering=False, num_devices=1)
    args = {k: nc.dram_tensor(k, v.shape, F32, kind="ExternalInput").ap() for k, v in arrays.items()}
    args |= {k: nc.dram_tensor(k, v, F32, kind="ExternalOutput").ap() for k, v in outs.items()}
    program(nc, **args)
    got = run_bass_kernel_spmd(nc, [arrays], core_ids=[0]).results[0]
    y = np.asarray(got["y_out"]).reshape(P, KD, TOK)
    y_prompt = y[:, :, 0:CTX].transpose(2, 1, 0).reshape(1, CTX, D)
    y_sample = y[:, :, L0:].transpose(2, 1, 0).reshape(1, LAT, D)
    k = np.asarray(got["k_out"]).reshape(DEPTH, P, 2, CTX).transpose(0, 3, 2, 1).reshape(1, DEPTH, CTX, HEADS, HD)
    v = np.asarray(got["v_out"]).reshape(1, DEPTH, CTX, HEADS, HD)
    ckv = np.asarray(got["ckv_out"]).transpose(0, 2, 1).reshape(1, DEPTH, CTX, KVL)
    kr = np.asarray(got["krope_out"]).transpose(0, 2, 1).reshape(1, DEPTH, CTX, ROPE)
    return tuple(np.ascontiguousarray(a) for a in (y_prompt, y_sample, k, v, ckv, kr))
```
